# Optimizing a Trainium2 kernel written in Bass

```python
import math
import jax, jax.numpy as jnp
from jax import lax
import numpy as np

D_MODEL = 1024
BATCH = 1
SEQ = 512
DEPTH = 2

GRID_W = 64
CTX_LEN = 256
N_MIXERS = 4
EPS = 1e-6
ROPE_THETA = 10000.0
Q_BLOCK = 128

FNET_GROUPS = 8
FNET_GROUP_DIM = D_MODEL // FNET_GROUPS
DIFF_HEAD_DIM = 64
DIFF_HEADS = D_MODEL // (2 * DIFF_HEAD_DIM)
HGRN_EXPAND = 128
HGRN_HEADS = D_MODEL // HGRN_EXPAND
HGRN_HEAD_V = D_MODEL // HGRN_HEADS
HGRN_FORGET_DIM = HGRN_HEADS * HGRN_EXPAND
HGRN_CHUNK = 64
GQA_HEAD_DIM = 128
GQA_Q_HEADS = D_MODEL // GQA_HEAD_DIM
GQA_KV_HEADS = 2
GQA_GROUP = GQA_Q_HEADS // GQA_KV_HEADS
D_FF = -(-8 * D_MODEL // (3 * 256)) * 256
N_FNET_LAYERS = len(range(0, DEPTH, N_MIXERS))
N_DIFF_LAYERS = len(range(1, DEPTH, N_MIXERS))
N_HGRN_LAYERS = len(range(2, DEPTH, N_MIXERS))
N_GQA_LAYERS = len(range(3, DEPTH, N_MIXERS))


def rms_norm(x, gain):
    xf = x.astype(jnp.float32)
    y = xf * lax.rsqrt(jnp.mean(xf * xf, axis=-1, keepdims=True) + EPS)
    return (y * gain.astype(jnp.float32)).astype(x.dtype)

def modulate(h, shift, scale):
    return h * (1.0 + scale) + shift

def swiglu(h, w_in, w_out):
    gate, up = jnp.split(h @ w_in, 2, axis=-1)
    return (jax.nn.silu(gate) * up) @ w_out

def axial_rope_tables(rows, head_dim):
    row = jnp.repeat(jnp.arange(rows, dtype=jnp.float32), GRID_W)
    col = jnp.tile(jnp.arange(GRID_W, dtype=jnp.float32), rows)
    n_freq = head_dim // 4
    inv_freq = ROPE_THETA ** (-jnp.arange(n_freq, dtype=jnp.float32) / n_freq)
    ang = jnp.concatenate([row[:, None] * inv_freq, col[:, None] * inv_freq], axis=-1)
    return jnp.cos(ang), jnp.sin(ang)

def apply_rope(x, cos, sin):
    shape = (cos.shape[0],) + (1,) * (x.ndim - 3) + (cos.shape[1],)
    cos = cos.reshape(shape)
    sin = sin.reshape(shape)
    x1, x2 = jnp.split(x.astype(jnp.float32), 2, axis=-1)
    return jnp.concatenate([x1 * cos - x2 * sin, x1 * sin + x2 * cos], axis=-1).astype(x.dtype)

def sweep_query_blocks(q, attend):
    b, l = q.shape[:2]
    nb = l // Q_BLOCK
    qb = jnp.moveaxis(q.reshape((b, nb, Q_BLOCK) + q.shape[2:]), 1, 0)
    out = lax.map(attend, qb)
    return jnp.moveaxis(out, 0, 1).reshape((b, l) + out.shape[3:])

def fnet_mixer(h_lat, h_ctx, w_out, b_out, need_ctx):
    def mix(h):
        b, l, _ = h.shape
        hg = h.astype(jnp.float32).reshape(b, l, FNET_GROUPS, FNET_GROUP_DIM)
        y = jnp.fft.fftn(hg, axes=(1, 3), norm='ortho').real
        return y.reshape(b, l, D_MODEL).astype(h.dtype) @ w_out + b_out
    return mix(h_lat), (mix(h_ctx) if need_ctx else None)

def diff_attn_core(q, k, v, lam):
    s = jnp.einsum('bqhcd,bkhcd->bhcqk', q.astype(jnp.float32), k.astype(jnp.float32)) * DIFF_HEAD_DIM ** -0.5
    p = jax.nn.softmax(s, axis=-1)
    w = p[:, :, 0] - lam * p[:, :, 1]
    return jnp.einsum('bhqk,bkhe->bqhe', w, v.astype(jnp.float32)).astype(v.dtype)

def diff_attention_mixer(h_lat, h_ctx, w_in, q_gain, k_gain, lam_par, subln_gain, w_out, layer_idx, rows, need_ctx):
    lam_init = 0.8 - 0.6 * math.exp(-0.3 * layer_idx)
    lp = lam_par.astype(jnp.float32)
    lam = jnp.exp(jnp.sum(lp[0] * lp[1])) - jnp.exp(jnp.sum(lp[2] * lp[3])) + lam_init
    cos, sin = axial_rope_tables(rows, DIFF_HEAD_DIM)

    def project(h, with_q):
        b, l, _ = h.shape
        if with_q:
            q, k, v = jnp.split(h @ w_in, 3, axis=-1)
            q = rms_norm(q.reshape(b, l, DIFF_HEADS, 2, DIFF_HEAD_DIM), q_gain)
        else:
            k, v = jnp.split(h @ w_in[:, D_MODEL:], 2, axis=-1)
            q = None
        k = rms_norm(k.reshape(b, l, DIFF_HEADS, 2, DIFF_HEAD_DIM), k_gain)
        return q, k, v.reshape(b, l, DIFF_HEADS, 2 * DIFF_HEAD_DIM)

    def finish(o):
        b, l = o.shape[:2]
        o = rms_norm(o, subln_gain) * (1.0 - lam_init)
        return o.reshape(b, l, D_MODEL) @ w_out

    q_c, k_c, v_c = project(h_ctx, need_ctx)
    q_l, k_l, v_l = project(h_lat, True)
    q_l = apply_rope(q_l, cos, sin)
    k_l = apply_rope(k_l, cos, sin)
    k_all = jnp.concatenate([k_c, k_l], axis=1)
    v_all = jnp.concatenate([v_c, v_l], axis=1)
    o_lat = finish(sweep_query_blocks(q_l, lambda qb: diff_attn_core(qb, k_all, v_all, lam)))
    o_ctx = finish(diff_attn_core(q_c, k_c, v_c, lam)) if need_ctx else None
    return o_lat, o_ctx

def gla_chunk_scan(q, k, v, log_f, s0):
    b, l, h, dk = q.shape
    dv = v.shape[-1]
    n = l // HGRN_CHUNK

    def chunks(t):
        return jnp.moveaxis(t.reshape((b, n, HGRN_CHUNK) + t.shape[2:]), 1, 0)

    lower = jnp.tril(jnp.ones((HGRN_CHUNK, HGRN_CHUNK), dtype=bool))[None, :, :, None, None]

    def step(s, inp):
        qc, kc, vc, gc = inp
        bc = jnp.cumsum(gc, axis=1)
        decay = jnp.exp(jnp.where(lower, bc[:, :, None] - bc[:, None, :], -jnp.inf))
        scores = jnp.einsum('bthk,bshk,btshk->bhts', qc, kc, decay)
        o = jnp.einsum('bhts,bshv->bthv', scores, vc) + jnp.einsum('bthk,bhkv->bthv', qc * jnp.exp(bc), s)
        b_last = bc[:, -1]
        s = jnp.exp(b_last)[..., None] * s + jnp.einsum('bshk,bshv->bhkv', kc * jnp.exp(b_last[:, None] - bc), vc)
        return s, o

    s_fin, o = lax.scan(step, s0, (chunks(q), chunks(k), chunks(v), chunks(log_f)))
    return jnp.moveaxis(o, 0, 1).reshape(b, l, h, dv), s_fin

def hgrn2_mixer(h_lat, h_ctx, w_in, lower_bound, norm_gain, w_out, layer_idx, need_ctx):
    lbs = jnp.cumsum(jax.nn.softmax(lower_bound.astype(jnp.float32), axis=1), axis=1)
    lb = (lbs[:, layer_idx] - lbs[:, 0]).reshape(2, HGRN_HEADS, HGRN_EXPAND)

    def project(h):
        b, l, _ = h.shape
        q, z_fwd, z_bwd, v, g = jnp.split(h @ w_in, 5, axis=-1)
        q = jax.nn.silu(q).reshape(b, l, HGRN_HEADS, HGRN_EXPAND).astype(jnp.float32)
        v = v.reshape(b, l, HGRN_HEADS, HGRN_HEAD_V).astype(jnp.float32)
        log_f = [jnp.log(lb[d] + (1.0 - lb[d]) * jax.nn.sigmoid(z.reshape(b, l, HGRN_HEADS, HGRN_EXPAND).astype(jnp.float32)))
                 for d, z in enumerate((z_fwd, z_bwd))]
        return q, v, log_f, g

    def run(q, v, lf, s0, reverse):
        if reverse:
            q, v, lf = jnp.flip(q, 1), jnp.flip(v, 1), jnp.flip(lf, 1)
        o, s = gla_chunk_scan(q, -jnp.expm1(lf), v, lf, s0)
        return (jnp.flip(o, 1) if reverse else o), s

    def finish(o, g):
        b, l = o.shape[:2]
        o = rms_norm(o, norm_gain) * jax.nn.silu(g.reshape(b, l, HGRN_HEADS, HGRN_HEAD_V).astype(jnp.float32))
        return o.reshape(b, l, D_MODEL).astype(g.dtype) @ w_out

    q_c, v_c, lf_c, g_c = project(h_ctx)
    q_l, v_l, lf_l, g_l = project(h_lat)
    s0 = jnp.zeros((h_ctx.shape[0], HGRN_HEADS, HGRN_EXPAND, HGRN_HEAD_V), jnp.float32)
    o_ctx_f, s_ctx_f = run(q_c, v_c, lf_c[0], s0, False)
    o_ctx_b, s_ctx_b = run(q_c, v_c, lf_c[1], s0, True)
    o_lat_f, _ = run(q_l, v_l, lf_l[0], s_ctx_f, False)
    o_lat_b, _ = run(q_l, v_l, lf_l[1], s_ctx_b, True)
    o_lat = finish(o_lat_f + o_lat_b, g_l)
    o_ctx = finish(o_ctx_f + o_ctx_b, g_c) if need_ctx else None
    return o_lat, o_ctx

def gqa_core(q, k, v):
    s = jnp.einsum('bqhgd,bkhd->bhgqk', q.astype(jnp.float32), k.astype(jnp.float32)) * GQA_HEAD_DIM ** -0.5
    p = jax.nn.softmax(s, axis=-1)
    return jnp.einsum('bhgqk,bkhd->bqhgd', p, v.astype(jnp.float32)).astype(v.dtype)

def gqa_mixer(h_lat, h_ctx, w_in, q_gain, k_gain, w_out, rows, need_ctx):
    qd = GQA_Q_HEADS * GQA_HEAD_DIM
    cos, sin = axial_rope_tables(rows, GQA_HEAD_DIM)

    def project(h, with_q):
        b, l, _ = h.shape
        if with_q:
            q, kv = jnp.split(h @ w_in, [qd], axis=-1)
            q = rms_norm(q.reshape(b, l, GQA_KV_HEADS, GQA_GROUP, GQA_HEAD_DIM), q_gain)
        else:
            kv = h @ w_in[:, qd:]
            q = None
        k, v = jnp.split(kv, 2, axis=-1)
        k = rms_norm(k.reshape(b, l, GQA_KV_HEADS, GQA_HEAD_DIM), k_gain)
        return q, k, v.reshape(b, l, GQA_KV_HEADS, GQA_HEAD_DIM)

    def finish(o):
        b, l = o.shape[:2]
        return o.reshape(b, l, D_MODEL) @ w_out

    q_c, k_c, v_c = project(h_ctx, need_ctx)
    q_l, k_l, v_l = project(h_lat, True)
    q_l = apply_rope(q_l, cos, sin)
    k_l = apply_rope(k_l, cos, sin)
    k_all = jnp.concatenate([k_c, k_l], axis=1)
    v_all = jnp.concatenate([v_c, v_l], axis=1)
    o_lat = finish(sweep_query_blocks(q_l, lambda qb: gqa_core(qb, k_all, v_all)))
    o_ctx = finish(gqa_core(q_c, k_c, v_c)) if need_ctx else None
    return o_lat, o_ctx

def first_inputs(seed: int = 0) -> dict:
    key = jax.random.key(seed)
    ks = iter(jax.random.split(key, 32))
    D = D_MODEL

    def nrm(shape, scale):
        return jax.random.normal(next(ks), shape, jnp.float32) * scale

    def gain(shape):
        return 1.0 + nrm(shape, 0.05)

    return {
        'x': nrm((BATCH, SEQ, D), 1.0),
        'c': nrm((BATCH, D), 1.0),
        'ctx': nrm((BATCH, CTX_LEN, D), 1.0),
        'c_ctx': nrm((D,), 1.0),
        'w_ada': nrm((DEPTH, D, 6 * D), 0.5 * D ** -0.5),
        'b_ada': nrm((DEPTH, 6 * D), 0.02),
        'norm_gain': gain((DEPTH, 2, D)),
        'ffn_w_in': nrm((DEPTH, D, 2 * D_FF), D ** -0.5),
        'ffn_w_out': nrm((DEPTH, D_FF, D), D_FF ** -0.5),
        'fnet_w_out': nrm((N_FNET_LAYERS, D, D), D ** -0.5),
        'fnet_b_out': nrm((N_FNET_LAYERS, D), 0.02),
        'diff_w_in': nrm((N_DIFF_LAYERS, D, 3 * D), D ** -0.5),
        'diff_q_gain': gain((N_DIFF_LAYERS, 2, DIFF_HEAD_DIM)),
        'diff_k_gain': gain((N_DIFF_LAYERS, 2, DIFF_HEAD_DIM)),
        'diff_lambda': nrm((N_DIFF_LAYERS, 4, DIFF_HEAD_DIM), 0.1),
        'diff_subln_gain': gain((N_DIFF_LAYERS, 2 * DIFF_HEAD_DIM)),
        'diff_w_out': nrm((N_DIFF_LAYERS, D, D), D ** -0.5),
        'hgrn_w_in': nrm((N_HGRN_LAYERS, D, 5 * D), D ** -0.5),
        'hgrn_lower_bound': nrm((2, DEPTH, HGRN_FORGET_DIM), 1.0),
        'hgrn_norm_gain': gain((N_HGRN_LAYERS, HGRN_HEAD_V)),
        'hgrn_w_out': nrm((N_HGRN_LAYERS, D, D), D ** -0.5),
        'gqa_w_in': nrm((N_GQA_LAYERS, D, (GQA_Q_HEADS + 2 * GQA_KV_HEADS) * GQA_HEAD_DIM), D ** -0.5),
        'gqa_q_gain': gain((N_GQA_LAYERS, GQA_HEAD_DIM)),
        'gqa_k_gain': gain((N_GQA_LAYERS, GQA_HEAD_DIM)),
        'gqa_w_out': nrm((N_GQA_LAYERS, D, D), D ** -0.5),
    }

def first_block(x, c, ctx, c_ctx, w_ada, b_ada, norm_gain, ffn_w_in, ffn_w_out, fnet_w_out, fnet_b_out,
              diff_w_in, diff_q_gain, diff_k_gain, diff_lambda, diff_subln_gain, diff_w_out,
              hgrn_w_in, hgrn_lower_bound, hgrn_norm_gain, hgrn_w_out,
              gqa_w_in, gqa_q_gain, gqa_k_gain, gqa_w_out):
    rows = x.shape[1] // GRID_W
    cond_lat = jax.nn.silu(c)[:, None, :]
    cond_ctx = jax.nn.silu(c_ctx)[None, None, :]
    for i in range(DEPTH):
        m, j = i % N_MIXERS, i // N_MIXERS
        need_ctx = i < DEPTH - 1
        sh1, sc1, g1, sh2, sc2, g2 = jnp.split(cond_lat @ w_ada[i] + b_ada[i], 6, axis=-1)
        csh1, csc1, cg1, csh2, csc2, cg2 = jnp.split(cond_ctx @ w_ada[i] + b_ada[i], 6, axis=-1)
        h_lat = modulate(rms_norm(x, norm_gain[i, 0]), sh1, sc1)
        h_ctx = modulate(rms_norm(ctx, norm_gain[i, 0]), csh1, csc1) if (need_ctx or m != 0) else None
        if m == 0:
            o_lat, o_ctx = fnet_mixer(h_lat, h_ctx, fnet_w_out[j], fnet_b_out[j], need_ctx)
        elif m == 1:
            o_lat, o_ctx = diff_attention_mixer(h_lat, h_ctx, diff_w_in[j], diff_q_gain[j], diff_k_gain[j], diff_lambda[j],
                                                diff_subln_gain[j], diff_w_out[j], i, rows, need_ctx)
        elif m == 2:
            o_lat, o_ctx = hgrn2_mixer(h_lat, h_ctx, hgrn_w_in[j], hgrn_lower_bound, hgrn_norm_gain[j], hgrn_w_out[j], i, need_ctx)
        else:
            o_lat, o_ctx = gqa_mixer(h_lat, h_ctx, gqa_w_in[j], gqa_q_gain[j], gqa_k_gain[j], gqa_w_out[j], rows, need_ctx)
        x = x + g1 * o_lat
        x = x + g2 * swiglu(modulate(rms_norm(x, norm_gain[i, 1]), sh2, sc2), ffn_w_in[i], ffn_w_out[i])
        if need_ctx:
            ctx = ctx + cg1 * o_ctx
            ctx = ctx + cg2 * swiglu(modulate(rms_norm(ctx, norm_gain[i, 1]), csh2, csc2), ffn_w_in[i], ffn_w_out[i])
    return x


DEPTH_2 = 1

N_META = 16
CHUNK = 128
PAD = CHUNK - N_META
D_SSD = 2 * D_MODEL
SSD_HEAD_DIM = 64
H_SSD = D_SSD // SSD_HEAD_DIM
SSD_GROUPS = 4
D_STATE = 128
CONV_K = 4
CONV_DIM = D_SSD + 2 * SSD_GROUPS * D_STATE
H_ATT = 16
ATT_HEAD_DIM = 64
D_ATT = H_ATT * ATT_HEAD_DIM
N_COLS = D_SSD + CONV_DIM + H_SSD + D_ATT + 3 * D_ATT + H_ATT + 2 * D_MODEL


def rmsnorm(x, g):
    xf = x.astype(jnp.float32)
    y = xf * lax.rsqrt(jnp.mean(xf * xf, axis=-1, keepdims=True) + EPS)
    return (y * g.astype(jnp.float32)).astype(x.dtype)

def gated_group_rmsnorm(y, z, g):
    u = (y * jax.nn.silu(z)).astype(jnp.float32)
    shp = u.shape
    u = u.reshape(shp[:-1] + (SSD_GROUPS, shp[-1] // SSD_GROUPS))
    u = u * lax.rsqrt(jnp.mean(u * u, axis=-1, keepdims=True) + EPS)
    return (u.reshape(shp) * g.astype(jnp.float32)).astype(y.dtype)

def causal_depthwise_conv(u, w, b):
    C = u.shape[-1]
    out = lax.conv_general_dilated(u, w[:, None, :].astype(u.dtype), window_strides=(1,),
                                   padding=[(CONV_K - 1, 0)],
                                   dimension_numbers=("NWC", "WIO", "NWC"),
                                   feature_group_count=C)
    return out + b

def ssd_chunked(xh, dt, a, bmat, cmat):
    Bsz, Lp, H, P = xh.shape
    G, N = bmat.shape[-2:]
    R = H // G
    nc = Lp // CHUNK
    xdt = (xh.astype(jnp.float32) * dt[..., None]).reshape(Bsz, nc, CHUNK, G, R, P)
    adt = (dt * a).reshape(Bsz, nc, CHUNK, G, R).transpose(0, 1, 3, 4, 2)
    a_cs = jnp.cumsum(adt, axis=-1)
    bm = bmat.astype(jnp.float32).reshape(Bsz, nc, CHUNK, G, N)
    cm = cmat.astype(jnp.float32).reshape(Bsz, nc, CHUNK, G, N)
    causal = jnp.tril(jnp.ones((CHUNK, CHUNK), dtype=bool))
    seg = a_cs[..., :, None] - a_cs[..., None, :]
    decay = jnp.exp(jnp.where(causal, seg, -jnp.inf))
    cb = jnp.einsum("bclgn,bcsgn->bcgls", cm, bm)
    y_diag = jnp.einsum("bcgls,bcgrls,bcsgrp->bclgrp", cb, decay, xdt)
    decay_states = jnp.exp(a_cs[..., -1:] - a_cs)
    states = jnp.einsum("bclgn,bcgrl,bclgrp->bcgrpn", bm, decay_states, xdt)
    chunk_decay = jnp.exp(a_cs[..., -1])

    def step(h, inp):
        s, d = inp
        return h * d[..., None, None] + s, h

    h0 = jnp.zeros((Bsz, G, R, P, N), jnp.float32)
    _, h_in = lax.scan(step, h0, (jnp.swapaxes(states, 0, 1), jnp.swapaxes(chunk_decay, 0, 1)))
    h_in = jnp.swapaxes(h_in, 0, 1)
    y_off = jnp.einsum("bclgn,bcgrpn,bcgrl->bclgrp", cm, h_in, jnp.exp(a_cs))
    return (y_diag + y_off).reshape(Bsz, Lp, H, P)

def forgetting_attention(q, k, v, logf):
    Bsz, Lp, H, Dh = q.shape
    scale = 1.0 / math.sqrt(Dh)
    c = jnp.cumsum(logf, axis=1)
    c_k = jnp.transpose(c, (0, 2, 1))
    nb = Lp // Q_BLOCK
    qb = q.reshape(Bsz, nb, Q_BLOCK, H, Dh).transpose(1, 0, 2, 3, 4)
    cqb = c.reshape(Bsz, nb, Q_BLOCK, H).transpose(1, 0, 3, 2)
    kpos = jnp.arange(Lp)

    def block(args):
        i, qi, cqi = args
        qpos = i * Q_BLOCK + jnp.arange(Q_BLOCK)
        s = jnp.einsum("bthd,bshd->bhts", qi, k).astype(jnp.float32) * scale
        s = s + (cqi[..., :, None] - c_k[..., None, :])
        s = jnp.where(kpos[None, :] <= qpos[:, None], s, -jnp.inf)
        p = jax.nn.softmax(s, axis=-1).astype(v.dtype)
        return jnp.einsum("bhts,bshd->bthd", p, v)

    out = lax.map(block, (jnp.arange(nb), qb, cqb))
    return out.transpose(1, 0, 2, 3, 4).reshape(Bsz, Lp, H, Dh)

def hybrid_layer(h, norm_pre, w_in, conv_w, conv_b, dt_bias, a_log, d_skip, ssd_norm,
                 fgate_bias, gate_bias, w_proj_ssd, w_proj_att, w_out, norm_post):
    Bsz, L, _ = h.shape
    Lp = L + PAD
    u = rmsnorm(h, norm_pre)
    proj = u @ w_in
    cuts = [D_SSD, D_SSD + CONV_DIM, D_SSD + CONV_DIM + H_SSD,
            D_SSD + CONV_DIM + H_SSD + D_ATT,
            D_SSD + CONV_DIM + H_SSD + 2 * D_ATT,
            D_SSD + CONV_DIM + H_SSD + 3 * D_ATT,
            D_SSD + CONV_DIM + H_SSD + 4 * D_ATT,
            D_SSD + CONV_DIM + H_SSD + 4 * D_ATT + H_ATT]
    z_ssd, xbc, dt_raw, z_att, q, k, v, f_raw, g_raw = jnp.split(proj, cuts, axis=-1)

    xbc = jax.nn.silu(causal_depthwise_conv(xbc, conv_w, conv_b))
    xs, bm, cm = jnp.split(xbc, [D_SSD, D_SSD + SSD_GROUPS * D_STATE], axis=-1)
    dt = jax.nn.softplus(dt_raw.astype(jnp.float32) + dt_bias.astype(jnp.float32))
    a = -jnp.exp(a_log.astype(jnp.float32))
    front = ((0, 0), (PAD, 0), (0, 0))
    xs_p = jnp.pad(xs, front).reshape(Bsz, Lp, H_SSD, SSD_HEAD_DIM)
    bm_p = jnp.pad(bm, front).reshape(Bsz, Lp, SSD_GROUPS, D_STATE)
    cm_p = jnp.pad(cm, front).reshape(Bsz, Lp, SSD_GROUPS, D_STATE)
    dt_p = jnp.pad(dt, front)
    y = ssd_chunked(xs_p, dt_p, a, bm_p, cm_p)
    y = y + d_skip.astype(jnp.float32)[:, None] * xs_p.astype(jnp.float32)
    y = y[:, PAD:].reshape(Bsz, L, D_SSD).astype(h.dtype)
    y_ssd = gated_group_rmsnorm(y, z_ssd, ssd_norm)

    logf = jax.nn.log_sigmoid(f_raw.astype(jnp.float32) + fgate_bias.astype(jnp.float32))
    back = ((0, 0), (0, PAD), (0, 0))
    qh = jnp.pad(q, back).reshape(Bsz, Lp, H_ATT, ATT_HEAD_DIM)
    kh = jnp.pad(k, back).reshape(Bsz, Lp, H_ATT, ATT_HEAD_DIM)
    vh = jnp.pad(v, back).reshape(Bsz, Lp, H_ATT, ATT_HEAD_DIM)
    o = forgetting_attention(qh, kh, vh, jnp.pad(logf, back))
    o = o[:, :L].reshape(Bsz, L, D_ATT)
    y_att = o * jax.nn.silu(z_att)

    gates = jax.nn.sigmoid(g_raw + gate_bias)
    g_ssd, g_att = jnp.split(gates, 2, axis=-1)
    merged = g_ssd * (y_ssd @ w_proj_ssd) + g_att * (y_att @ w_proj_att)
    return h + rmsnorm(merged @ w_out, norm_post)

def second_inputs(seed: int = 0) -> dict:
    key = jax.random.key(seed)
    ks = jax.random.split(key, 16)
    D = D_MODEL
    nrm = jax.random.normal
    x = nrm(ks[0], (BATCH, SEQ, D), jnp.float32)
    meta_tokens = nrm(ks[1], (N_META, D), jnp.float32)
    norm_pre = 1.0 + 0.05 * nrm(ks[2], (DEPTH_2, D), jnp.float32)
    w_in = nrm(ks[3], (DEPTH_2, D, N_COLS), jnp.float32) * D ** -0.5
    conv_w = jax.random.uniform(ks[4], (DEPTH_2, CONV_K, CONV_DIM), jnp.float32, -0.5, 0.5)
    conv_b = 0.05 * nrm(ks[5], (DEPTH_2, CONV_DIM), jnp.float32)
    dt0 = jnp.exp(jax.random.uniform(ks[6], (DEPTH_2, H_SSD), jnp.float32,
                                     math.log(1e-3), math.log(1e-1)))
    dt_bias = dt0 + jnp.log(-jnp.expm1(-dt0))
    a_log = jnp.log(jax.random.uniform(ks[7], (DEPTH_2, H_SSD), jnp.float32, 1.0, 16.0))
    d_skip = 1.0 + 0.1 * nrm(ks[8], (DEPTH_2, H_SSD), jnp.float32)
    ssd_norm = 1.0 + 0.05 * nrm(ks[9], (DEPTH_2, D_SSD), jnp.float32)
    fgate_bias = jax.random.uniform(ks[10], (DEPTH_2, H_ATT), jnp.float32, 1.0, 6.0)
    gate_bias = 0.1 * nrm(ks[11], (DEPTH_2, 2 * D), jnp.float32)
    w_proj_ssd = nrm(ks[12], (DEPTH_2, D_SSD, D), jnp.float32) * D_SSD ** -0.5
    w_proj_att = nrm(ks[13], (DEPTH_2, D_ATT, D), jnp.float32) * D_ATT ** -0.5
    w_out = nrm(ks[14], (DEPTH_2, D, D), jnp.float32) * D ** -0.5
    norm_post = 1.0 + 0.05 * nrm(ks[15], (DEPTH_2, D), jnp.float32)
    return {"x": x, "meta_tokens": meta_tokens, "norm_pre": norm_pre, "w_in": w_in,
            "conv_w": conv_w, "conv_b": conv_b, "dt_bias": dt_bias, "a_log": a_log,
            "d_skip": d_skip, "ssd_norm": ssd_norm, "fgate_bias": fgate_bias,
            "gate_bias": gate_bias, "w_proj_ssd": w_proj_ssd, "w_proj_att": w_proj_att,
            "w_out": w_out, "norm_post": norm_post}

def second_block(x, meta_tokens, norm_pre, w_in, conv_w, conv_b, dt_bias, a_log, d_skip,
              ssd_norm, fgate_bias, gate_bias, w_proj_ssd, w_proj_att, w_out, norm_post):
    Bsz = x.shape[0]
    meta = jnp.broadcast_to(meta_tokens[None].astype(x.dtype), (Bsz, N_META, D_MODEL))
    h = jnp.concatenate([meta, x], axis=1)
    for i in range(DEPTH_2):
        h = hybrid_layer(h, norm_pre[i], w_in[i], conv_w[i], conv_b[i], dt_bias[i], a_log[i],
                         d_skip[i], ssd_norm[i], fgate_bias[i], gate_bias[i], w_proj_ssd[i],
                         w_proj_att[i], w_out[i], norm_post[i])
    return h[:, N_META:]


def setup_inputs(seed=0):
    out = dict(first_inputs(seed))
    for name, value in second_inputs(seed + 1).items():
        if name != "x":
            out[name + "_2"] = value
    return out


def reference(
    x, c, ctx, c_ctx, w_ada, b_ada, norm_gain, ffn_w_in, ffn_w_out, fnet_w_out, fnet_b_out,
    diff_w_in, diff_q_gain, diff_k_gain, diff_lambda, diff_subln_gain, diff_w_out, hgrn_w_in,
    hgrn_lower_bound, hgrn_norm_gain, hgrn_w_out, gqa_w_in, gqa_q_gain, gqa_k_gain, gqa_w_out,
    meta_tokens_2, norm_pre_2, w_in_2, conv_w_2, conv_b_2, dt_bias_2, a_log_2, d_skip_2,
    ssd_norm_2, fgate_bias_2, gate_bias_2, w_proj_ssd_2, w_proj_att_2, w_out_2, norm_post_2,
):
    x = first_block(
        x, c, ctx, c_ctx, w_ada, b_ada, norm_gain, ffn_w_in, ffn_w_out, fnet_w_out, fnet_b_out,
        diff_w_in, diff_q_gain, diff_k_gain, diff_lambda, diff_subln_gain, diff_w_out,
        hgrn_w_in, hgrn_lower_bound, hgrn_norm_gain, hgrn_w_out, gqa_w_in, gqa_q_gain,
        gqa_k_gain, gqa_w_out,
    )
    return second_block(
        x, meta_tokens_2, norm_pre_2, w_in_2, conv_w_2, conv_b_2, dt_bias_2, a_log_2, d_skip_2,
        ssd_norm_2, fgate_bias_2, gate_bias_2, w_proj_ssd_2, w_proj_att_2, w_out_2, norm_post_2,
    )


_drawn_inputs = setup_inputs


def setup_inputs(seed=0):
    import zlib

    import numpy as np

    out = dict(_drawn_inputs(seed))
    spreads = {}
    factors = {'fnet_b_out': 6.073, 'diff_q_gain': 8.0, 'diff_k_gain': 8.0, 'diff_subln_gain': 4.311}
    for name, (base, spread) in spreads.items():
        noise = np.random.default_rng([zlib.crc32(name.encode()), seed]).standard_normal(out[name].shape)
        drawn = base * np.exp(spread * noise) if base else spread * noise
        out[name] = __import__('jax').numpy.asarray(drawn.astype(out[name].dtype))
    for name, factor in factors.items():
        out[name] = (out[name] * factor).astype(out[name].dtype)
    return out
```

```python
from contextlib import ExitStack

import numpy as np
import concourse.bass as bass
from concourse import mybir

F32 = mybir.dt.float32
ALU = mybir.AluOpType
ACT = mybir.ActivationFunctionType
AX = mybir.AxisListType

P = 128
D = 1024
KC = D // P
LAT, CTX, META = 512, 256, 16
NT = LAT // P
ROWS = LAT + CTX
F = 2816
PAIRS = F // 256
GROUPS = [(0, 4), (4, 8), (8, 11)]
HEADS = 8
DH = 64
EPS = 1e-6
LAM_INIT = 0.8 - 0.6 * float(np.exp(-0.3))
SG = 4
COL_Z, COL_X, COL_B, COL_C, COL_DT = 0, 2048, 4096, 4608, 5120
COL_ZA, COL_Q, COL_K, COL_V, COL_F, COL_G = 5152, 6176, 7200, 8224, 9248, 9264
NR = 4
NEG = -1e30

ROW_C, ROW_CC, ROW_NG, ROW_FB, ROW_NP, ROW_SN, ROW_GB, ROW_SUB, ROW_QG, ROW_KG, N_A = 0, 8, 16, 48, 56, 64, 80, 96, 97, 98, 99
ROW_ADA, ROW_CB, N_B = 0, 96, 120
N_C = 96
(K_ID, K_ONE, K_BLK, K_UP, K_LOW, K_NEG, K_DFT, K_COS, K_SIN, N_K) = (0, 128, 256, 384, 512, 640, 768, 1024, 1536, 2048)


def constants():
    i = np.arange(P)
    k = np.zeros((P, N_K), np.float32)
    k[:, K_ID:K_ID + P] = np.eye(P)
    k[:, K_ONE:K_ONE + P] = 1.0
    k[:, K_BLK:K_BLK + P] = (i[:, None] // DH == i[None, :] // DH)
    k[:, K_UP:K_UP + P] = i[:, None] <= i[None, :]
    k[:, K_LOW:K_LOW + P] = i[:, None] > i[None, :]
    k[:, K_NEG:K_NEG + P] = np.where(i[None, :] > i[:, None], NEG, 0.0)
    a = 2 * np.pi * (np.outer(i, i) % P) / P
    k[:, K_DFT:K_DFT + P] = np.cos(a)
    k[:, K_DFT + P:K_DFT + 2 * P] = np.sin(a)
    row = np.repeat(np.arange(LAT // 64, dtype=np.float32), 64)
    col = np.tile(np.arange(64, dtype=np.float32), LAT // 64)
    nf = DH // 4
    inv = (np.float32(10000.0) ** (-np.arange(nf, dtype=np.float32) / np.float32(nf))).astype(np.float32)
    ang = np.concatenate([row[:, None] * inv, col[:, None] * inv], axis=-1).astype(np.float32).astype(np.float64).T
    k[:, K_COS:K_COS + LAT] = np.tile(np.cos(ang), (4, 1))
    k[:, K_SIN:K_SIN + LAT] = np.tile(np.concatenate([-np.sin(ang), np.sin(ang)]), (2, 1))

    def dft(n):
        j = np.arange(n)
        a = 2 * np.pi * (np.outer(j, j) % n) / n
        t = np.stack([np.cos(a), -np.sin(a)], axis=1) / np.sqrt(n * P)
        return np.ascontiguousarray(t.reshape(n // P, P, 2 * n).transpose(1, 0, 2).reshape(P, -1), np.float32)

    return k, dft(LAT), dft(CTX)


def stream_plan():
    plan = [("ada", 0, b) for b in range(8)]
    for g in range(KC):
        plan += [("ada", 0, 8 + 2 * g), ("ada", 0, 9 + 2 * g)]
    plan += [("fnet", cb) for cb in range(4)]
    for layer in range(2):
        for lo, hi in GROUPS:
            for p in range(lo, hi):
                plan += [("gate", layer, p), ("up", layer, p)]
                if layer == 0:
                    plan += [("ada", 1, b) for b in ada1_blocks(p)]
            plan += [("down", layer, lo, cb) for cb in range(4)]
        if layer == 0:
            plan += [(w, cb) for w in ("dk", "dq", "dv") for cb in range(4)]
            plan += [("dout", cb) for cb in range(4)]
    plan += [("B", j) for j in range(2)] + [("C", j) for j in range(2)]
    for g in range(SG):
        plan += [("z", g, j) for j in range(2)] + [("xs", g, j) for j in range(2)]
    for f in range(4):
        plan += [("q", f), ("k", f), ("v", f), ("za", f)]
    for cb in range(4):
        plan += [("gs", cb), ("ga", cb), ("ps", cb, 0), ("ps", cb, 1), ("pa", cb)]
    plan += [("wo", cb) for cb in range(4)]
    return plan


def ada1_blocks(p):
    return [2 * p, 2 * p + 1] + ([22, 23] if p == PAIRS - 1 else [])


def step_plan():
    steps = [(("fnet", cb), [("fnet", cb)]) for cb in range(4)]
    for layer in range(2):
        for lo, hi in GROUPS:
            for p in range(lo, hi):
                steps.append((("in", layer, p, 0), []))
                steps.append((("in", layer, p, 1), [("gate", layer, p), ("up", layer, p)]))
            steps += [(("down", layer, lo, cb), [("down", layer, lo, cb)]) for cb in range(4)]
        if layer == 0:
            steps += [((w, cb), [(w, cb)]) for w in ("dk", "dq", "dv") for cb in range(4)]
            steps += [(("dout", cb), [("dout", cb)]) for cb in range(4)]
    steps += [((w, j), [(w, j)]) for w in ("B", "C") for j in range(2)]
    for g in range(SG):
        steps += [((w, g, j), [(w, g, j)]) for w in ("z", "xs") for j in range(2)]
    for f in range(4):
        steps += [((w, f), [(w, f)]) for w in ("q", "k", "v", "za")]
    for cb in range(4):
        steps += [(("gs", cb), [("gs", cb)]), (("ga", cb), [("ga", cb)]),
                  (("ps", cb), [("ps", cb, 0), ("ps", cb, 1)]), (("pa", cb), [("pa", cb)])]
    steps += [(("wo", cb), [("wo", cb)]) for cb in range(4)]
    return steps


def bass_two_blocks_kernel(nc, io, kt_d, dl_d, dc_d, out, dump=None, stage=99):
    PLAN = stream_plan()
    N_OF = {key: n for n, key in enumerate(PLAN)}
    STEPS = step_plan()
    T_OF = {key: t for t, (key, _) in enumerate(STEPS)}
    w_ada, w_in2 = io["w_ada"], io["w_in_2"][0]

    def source(key):
        kind = key[0]
        if kind == "ada":
            return w_ada[key[1]], 0, KC, 256 * key[2]
        if kind == "fnet":
            return io["fnet_w_out"][0], 0, KC, 256 * key[1]
        if kind == "gate":
            return io["ffn_w_in"][key[1]], 0, KC, 256 * key[2]
        if kind == "up":
            return io["ffn_w_in"][key[1]], 0, KC, F + 256 * key[2]
        if kind == "down":
            _, layer, lo, cb = key
            hi = dict(GROUPS)[lo]
            return io["ffn_w_out"][layer], 256 * lo, 2 * (hi - lo), 256 * cb
        if kind in ("dq", "dk", "dv"):
            return io["diff_w_in"][0], 0, KC, {"dq": 0, "dk": D, "dv": 2 * D}[kind] + 256 * key[1]
        if kind == "dout":
            return io["diff_w_out"][0], 0, KC, 256 * key[1]
        if kind in ("B", "C"):
            return w_in2, 0, KC, {"B": COL_B, "C": COL_C}[kind] + 256 * key[1]
        if kind in ("xs", "z"):
            return w_in2, 0, KC, {"xs": COL_X, "z": COL_Z}[kind] + 512 * key[1] + 256 * key[2]
        if kind in ("q", "k", "v", "za"):
            return w_in2, 0, KC, {"q": COL_Q, "k": COL_K, "v": COL_V, "za": COL_ZA}[kind] + 256 * key[1]
        if kind in ("gs", "ga"):
            return w_in2, 0, KC, COL_G + (D if kind == "ga" else 0) + 256 * key[1]
        if kind == "ps":
            return io["w_proj_ssd_2"][0], D * key[2], KC, 256 * key[1]
        if kind == "pa":
            return io["w_proj_att_2"][0], 0, KC, 256 * key[1]
        return io["w_out_2"][0], 0, KC, 256 * key[1]

    with ExitStack() as ctx:
        here = [ctx]

        def sb(name, shape, dt=F32):
            return here[-1].enter_context(nc.sbuf_tensor(name, shape, dt))

        def sem(name):
            return ctx.enter_context(nc.semaphore(name))

        bank = [ctx.enter_context(nc.psum_tensor(f"bank{i}", [P, 512], F32)) for i in range(4, 8)]
        two = [ctx.enter_context(nc.psum_tensor(f"two{i}", [P, 1024], F32)) for i in range(2)]
        bank = [two[0][:, 0:512], two[0][:, 512:1024], two[1][:, 0:512], two[1][:, 512:1024]] + [b[:, :] for b in bank]

        kt = sb("kt", [P, N_K])
        ident, ones, blk = kt[:, K_ID:K_ID + P], kt[:, K_ONE:K_ONE + P], kt[:, K_BLK:K_BLK + P]
        upper, lower, negm = kt[:, K_UP:K_UP + P], kt[:, K_LOW:K_LOW + P], kt[:, K_NEG:K_NEG + P]
        dft128, cosT, sinT = kt[:, K_DFT:K_DFT + 2 * P], kt[:, K_COS:K_COS + LAT], kt[:, K_SIN:K_SIN + LAT]
        colA, colB, colC = sb("colA", [P, N_A]), sb("colB", [P, N_B]), sb("colC", [P, N_C])
        cond = sb("cond", [P, KC, 2])
        ada = [sb(f"ada{i}", [P, 48, 2]) for i in range(2)]
        mult = sb("mult", [P, 4, KC, 2])
        gbias = sb("gbias", [P, KC, 2])
        epsc = sb("epsc", [P, 1])
        xT = sb("xT", [P, KC, ROWS])
        metaT = sb("metaT", [P, KC, META])
        wdtf = sb("wdtf", [P, KC, 48])
        bdtf = sb("bdtf", [P, 48])
        alog = sb("alog", [P, 32])
        dskip = sb("dskip", [P, 32])
        lamv = sb("lamv", [P, 4 * DH])
        lamt = sb("lamt", [P, DH])
        lams = sb("lams", [P, 8])
        gpost = sb("gpost", [P, D])
        ring = sb("ring", [P, NR, KC, 256])

        def phase():
            s = ExitStack()
            here.append(s)
            return s

        def leave():
            here.pop().close()

        phase()
        hT = sb("hT", [P, KC, ROWS])
        sq = sb("sq", [P, 2, ROWS])
        rstd = sb("rstd", [P, ROWS])
        phase()
        xraw = sb("xraw", [P, 6, D])
        mraw = sb("mraw", [META, D])
        rowA, rowB, rowC = sb("rowA", [N_A, P]), sb("rowB", [N_B, P]), sb("rowC", [N_C, P])
        dftL = sb("dftL", [P, NT, 2, LAT])
        dftC = sb("dftC", [P, 2, 2, CTX])
        fa = sb("fa", [P, 2, 6, 256])
        tmpF = sb("tmpF", [P, 2, ROWS])
        leave()
        phase()
        hid = sb("hid", [P, 8, ROWS])
        gateS = sb("gateS", [P, 2, ROWS])
        leave()
        phase()
        kT = sb("kT", [P, HEADS, ROWS])
        qT = sb("qT", [P, HEADS, LAT])
        V = sb("V", [P, 6, D])
        krot = sb("krot", [P, LAT])
        kraw = sb("kraw", [P, LAT])
        prob = sb("prob", [P, 2, 2, ROWS])
        WT = sb("WT", [P, 6, LAT])
        attmx = sb("attmx", [P, 2, 2, 4])
        leave()
        leave()
        here.append(ctx)
        phase()
        ALL = LAT + META
        uT = sb("uT", [P, KC, ALL])
        ysT = sb("ysT", [P, 2 * KC, LAT])
        dtr = sb("dtr", [P, 5, 48])
        dtt = sb("dtt", [P, 4 * 240])
        dta, dtu, dtw, dtl = (dtt[:, 240 * k:240 * k + 240].rearrange("p (a n) -> p a n", a=5) for k in range(4))
        ysq = dtt[:, 0:512]
        dtv = sb("dtv", [P, 5, 32])
        logf = sb("logf", [P, 5, 16])
        expa = sb("expa", [P, 32])
        adt = sb("adt", [P, 5, 32])
        dec = sb("dec", [P, 352])
        ckT, cqT = sb("ckT", [16, ALL]), sb("cqT", [16, LAT])
        stt4 = sb("stt4", [P, 8])
        phase()
        Brow = sb("Brow", [P, 4, 4 * P])
        BT = sb("BT", [P, 4, ALL])
        CTt = sb("CTt", [P, 4, LAT])
        cin = sb("cin", [P, 2, ALL + 3])
        cacc = sb("cacc", [P, 2, ALL])
        xrow = sb("xrow", [P, 5, 512])
        xdt, xds = sb("xdt", [P, 2, 512]), sb("xds", [P, 512])
        xd = sb("xd", [P, 512])
        lseg = sb("lseg", [P, 1056])
        sqb = lseg[:].rearrange("p (a n) -> p a n", a=2)
        Mt = sb("Mt", [P, 8, P])
        rstdb = Mt[:].rearrange("p a n -> p (a n)")[:, 0:ALL]
        CBm = sb("CBm", [P, P])
        Hst = sb("Hst", [P, 2, 512])
        yrow = sb("yrow", [P, 512])
        zrow = sb("zrow", [P, 4, 512])
        leave()
        phase()
        yaT = sb("yaT", [P, KC, LAT])
        phase()
        qA = sb("qA", [P, 4, LAT])
        kA = sb("kA", [P, 4, ALL])
        vA = sb("vA", [P, 5, 256])
        zA = sb("zA", [P, 4, 256])
        probA = sb("probA", [P, 2, ALL])
        PT = sb("PT", [P, 2, 5 * P])
        amx = sb("amx", [P, 2, 4])
        asum = sb("asum", [P, 4, 4])
        yA = sb("yA", [P, 256])
        leave()
        phase()
        mg = sb("mg", [P, KC, LAT])
        gsb, gab = sb("gsb", [P, 2, LAT]), sb("gab", [P, 2, LAT])
        orow = sb("orow", [P, 4, D])
        leave()
        leave()
        leave()

        s_load, s_tab, s_x = sem("s_load"), sem("s_tab"), sem("s_x")
        s_x2, s_dft, s_small = sem("s_x2"), sem("s_dft"), sem("s_small")
        ring_ready = [sem(f"ring_ready{i}") for i in range(NR)]
        s_cols_t, s_cols = sem("s_cols_t"), sem("s_cols")
        s_cond, s_xt, s_xlat, s_xctx, s_meta_t, s_meta = sem("s_cond"), sem("s_xt"), sem("s_xlat"), sem("s_xctx"), sem("s_meta_t"), sem("s_meta")
        ada_done, ada_taken, s_mult = sem("ada_done"), sem("ada_taken"), sem("s_mult")
        n_sq, n_used, n_sum, n_ln, n_rstd, h_ready = sem("n_sq"), sem("n_used"), sem("n_sum"), sem("n_ln"), sem("n_rstd"), sem("h_ready")
        tile_done = sem("tile_done")
        f_a, f_acopy, f_y, f_ycopy = sem("f_a"), sem("f_acopy"), sem("f_y"), sem("f_ycopy")
        r_tmp, r_res = sem("r_tmp"), sem("r_res")
        g_silu, g_hid = sem("g_silu"), sem("g_hid")
        v_chain, a_chain = sem("v_chain"), sem("a_chain")
        s_dump = sem("s_dump")
        k_sq, k_sum, k_rstd, k_norm, k_rot, k_done = sem("k_sq"), sem("k_sum"), sem("k_rstd"), sem("k_norm"), sem("k_rot"), sem("k_done")
        v_copy, v_copyd, s_lam, s_lamx = sem("v_copy"), sem("v_copyd"), sem("s_lam"), sem("s_lamx")
        a_s, a_max, a_exp, a_w, a_wt, a_wtc, a_pv, a_sq, a_ms, a_rs, a_o = (sem(x) for x in (
            "a_s", "a_max", "a_exp", "a_w", "a_wt", "a_wtc", "a_pv", "a_sq", "a_ms", "a_rs", "a_o"))

        (c_in, c_acc, c_out, c_t, c_tev, z_act, x_act, x_dve, m_gate, m_mix, o_act) = (sem(x) for x in (
            "c_in", "c_acc", "c_out", "c_t", "c_tev", "z_act", "x_act", "x_dve", "m_gate", "m_mix", "o_act"))
        (d_zero, d_raw, d_biased, d_u, d_w, d_ln, d_expa, d_adt, d_sums, d_dec, d_ct, d_cta) = (sem(x) for x in (
            "d_zero", "d_raw", "d_biased", "d_u", "d_w", "d_ln", "d_expa", "d_adt", "d_sums", "d_dec", "d_ct", "d_cta"))
        (p_lseg, p_xdt, p_xds, p_xd, e_seg, e_exp, e_cb, e_cbm, e_m, e_y, e_yoff, e_st, e_h, e_gated, e_ss, e_rs, e_un, e_t, e_tev) = (sem(x) for x in (
            "p_lseg", "p_xdt", "p_xds", "p_xd", "e_seg", "e_exp", "e_cb", "e_cbm", "e_m", "e_y", "e_yoff", "e_st", "e_h",
            "e_gated", "e_ss", "e_rs", "e_un", "e_t", "e_tev"))
        (b_one, b_k, b_q, b_s, b_max, b_exp, b_pt, b_pta, b_ptd, b_o, b_y, b_yt, b_ytev) = (sem(x) for x in (
            "b_one", "b_k", "b_q", "b_s", "b_max", "b_exp", "b_pt", "b_pta", "b_ptd", "b_o", "b_y", "b_yt", "b_ytev"))
        (o_ss, o_rs, o_xt, o_fin, s_out) = (sem(x) for x in ("o_ss", "o_rs", "o_xt", "o_fin", "s_out"))

        block = ctx.enter_context(nc.Block())

        class Chain:

            def __init__(self, eng, s):
                self.eng, self.s, self.n = eng, s, 0

            def __call__(self, ins):
                self.n += 1
                ins.then_inc(self.s, 1)

            def wait(self):
                self.eng.wait_ge(self.s, self.n)

        def blocks_used(key):
            if key[0] == "ada":
                return ada_done, 24 * key[1] + key[2] + 1
            for t, (_, ends) in enumerate(STEPS):
                if key in ends:
                    return tile_done, 2 * t + 2
            raise KeyError(key)

        def banks_read(t):
            key = STEPS[t][0]
            kind = key[0]
            if kind == "fnet":
                return [(r_tmp, 2 * key[1] + 2)]
            if kind == "in":
                return [(g_hid, 22 * key[1] + 2 * key[2] + key[3] + 1)]
            if kind == "down":
                _, layer, lo, cb = key
                return [(r_res, (8, 40)[layer] + 8 * [a for a, _ in GROUPS].index(lo) + 2 * cb + 2)]
            if kind == "dout":
                return [(r_res, 32 + 2 * key[1] + 2)]
            if kind in ("dk", "dq"):
                return [(k_norm, (8 if kind == "dq" else 0) + 2 * key[1] + 2)]
            if kind == "dv":
                return [(v_copy, key[1] + 1), (v_copyd, key[1] + 1)]
            if kind in ("B", "C", "xs"):
                return [(c_in, conv_tile(kind, key, 1) + 1)]
            if kind == "z":
                return [(z_act, 2 * key[1] + key[2] + 1)]
            if kind in ("q", "k", "v"):
                i = 3 * key[1] + "qkv".index(kind) + 1
                return [(x_act, i), (x_dve, i)]
            if kind == "za":
                return [(z_act, 2 * SG + key[1] + 1)]
            if kind in ("gs", "ga"):
                return [(m_gate, 2 * key[1] + (kind == "ga") + 1)]
            if kind in ("ps", "pa"):
                return [(m_mix, 2 * key[1] + (kind == "pa") + 1)]
            if kind == "wo":
                return [(o_act, key[1] + 1)]
            raise KeyError(key)

        def conv_tile(kind, key, j):
            return {"B": 2 * key[1], "C": 4 + 2 * key[1], "xs": 8 + 4 * key[1] + (2 * key[2] if len(key) > 2 else 0)}[kind] + j

        def halves(with_ctx):
            return [(0, LAT, 0), (LAT, ROWS, 1)] if with_ctx else [(0, LAT, 0)]

        NORM_SQ = {0: 0, 1: KC, 2: 2 * KC, 3: 3 * KC, 4: 4 * KC}
        last_stage = stage

        def steps_in(layer, lo, hi):
            return [("in", layer, p, j) for p in range(lo, hi) for j in range(2)]

        @block.sync
        def _(sp):
            sp.dma_start(kt[:], kt_d).then_inc(s_load, 16)
            for i in range(4):
                sp.dma_start(xraw[:, i, :], io["x"][0, i * P:(i + 1) * P, :]).then_inc(s_x, 16)

            def stream(n):
                key = PLAN[n]
                if n >= NR:
                    s, v = blocks_used(PLAN[n - NR])
                    sp.wait_ge(s, v)
                w, r0, kc, c0 = source(key)
                sp.dma_start(ring[:, n % NR, 0:kc, :],
                             w[r0:r0 + kc * P, c0:c0 + 256].rearrange("(c p) n -> p c n", p=P)) \
                    .then_inc(ring_ready[n % NR], 16)

            for n in range(NR):
                stream(n)
            for i in range(2):
                sp.dma_start(xraw[:, 4 + i, :], io["ctx"][0, i * P:(i + 1) * P, :]).then_inc(s_x2, 16)
            sp.dma_start(mraw[:, :], io["meta_tokens_2"]).then_inc(s_x2, 16)
            for n in range(NR, 8):
                stream(n)
            sp.dma_start(dftL[:].rearrange("p a b n -> p (a b n)"), dl_d).then_inc(s_dft, 16)
            sp.dma_start(dftC[:].rearrange("p a b n -> p (a b n)"), dc_d).then_inc(s_dft, 16)
            end = {0: N_OF[("gate", 0, 0)], 1: N_OF[("dk", 0)], 2: N_OF[("gate", 1, 0)], 3: N_OF[("B", 0)]}.get(stage, len(PLAN))
            for n in range(8, end):
                stream(n)
            if stage == 0:
                sp.wait_ge(r_res, 8)
            elif stage == 1:
                sp.wait_ge(r_res, 8 + 24)
            elif stage == 2:
                sp.wait_ge(r_res, 8 + 24 + 8)
            elif stage == 3:
                sp.wait_ge(r_res, 8 + 24 + 8 + 24)
            sp.wait_ge(s_small, 128)
            if stage < 4:
                sp.dma_start(dump, xT[:].rearrange("p c r -> p (c r)")).then_inc(s_dump, 16)
                sp.dma_start(out[0, 0:P, :], kt[:, 0:D]).then_inc(s_dump, 16)
                sp.wait_ge(s_dump, 32)
                return
            for i in range(NT):
                sp.wait_ge(o_fin, 2 * i + 2)
                sp.dma_start(out[0, i * P:(i + 1) * P, :], orow[:, i, :]).then_inc(s_out, 16)
            sp.wait_ge(s_out, 16 * NT)

        @block.tensor
        def _(pe):
            used = [0]
            step = [0]

            def weights(key):
                n = used[0]
                assert PLAN[n] == key, (PLAN[n], key)
                used[0] += 1
                pe.wait_ge(ring_ready[n % NR], 16 * (n // NR + 1))
                return ring[:, n % NR]

            def begin(key):
                t = step[0]
                assert STEPS[t][0] == key, (STEPS[t][0], key)
                step[0] += 1
                if t >= 2:
                    for w in banks_read(t - 2):
                        pe.wait_ge(*w)
                return t % 2

            def tile(s, half, parts, extra):
                n = len(parts)
                for i, (w, r, wait) in enumerate(parts):
                    if wait is not None:
                        pe.wait_ge(*wait)
                    m = nc.tensor.matmul(bank[3 * s + half], w, r[:, 0:LAT], start=i == 0, stop=i == n - 1)
                if extra:
                    for i, (w, r, _) in enumerate(parts):
                        m = nc.tensor.matmul(bank[3 * s + 2][:, 256 * half:256 * half + extra], w,
                                             r[:, LAT:LAT + extra], start=i == 0, stop=i == n - 1)
                m.then_inc(tile_done, 1)

            def ada_block(layer, b):
                w = weights(("ada", layer, b))
                i = 24 * layer + b
                if i >= 2:
                    pe.wait_ge(ada_taken, i - 1)
                for j in range(2):
                    for kc in range(KC):
                        m = nc.tensor.matmul(bank[6 + b % 2][:, 2 * j:2 * j + 2], w[:, kc, P * j:P * j + P],
                                             cond[:, kc, :], start=kc == 0, stop=kc == KC - 1)
                m.then_inc(ada_done, 1)

            def norm_sums(i, with_ctx):
                for kc in range(KC):
                    pe.wait_ge(n_sq, NORM_SQ[i] + kc + 1)
                    for a, b, half in halves(with_ctx):
                        m = nc.tensor.matmul(bank[6 + half][:, 0:b - a], ones, sq[:, kc % 2, a:b],
                                             start=kc == 0, stop=kc == KC - 1)
                    m.then_inc(n_used, 1)

            pe.wait_ge(s_load, 16)
            pe.wait_ge(s_tab, 16 * 13)
            nc.tensor.transpose(bank[0][:, 0:N_A], rowA[:, :], kt[0:N_A, K_ID:K_ID + N_A]).then_inc(s_cols_t, 1)
            nc.tensor.transpose(bank[1][:, 0:N_B], rowB[:, :], kt[0:N_B, K_ID:K_ID + N_B]).then_inc(s_cols_t, 1)
            nc.tensor.transpose(bank[2][:, 0:N_C], rowC[:, :], kt[0:N_C, K_ID:K_ID + N_C]).then_inc(s_cols_t, 1)
            pe.wait_ge(s_cond, 2)
            pe.wait_ge(s_x, 64)
            pe.wait_ge(s_x2, 48)
            pe.wait_ge(s_cols, 3)
            for kc in range(KC):
                if kc >= 2:
                    pe.wait_ge(s_xlat, kc - 1)
                    pe.wait_ge(s_xctx, kc - 1)
                for i in range(NT):
                    nc.tensor.transpose(bank[3 * (kc % 2)][:, i * P:(i + 1) * P], xraw[:, i, kc * P:(kc + 1) * P], ident)
                for i in range(2):
                    m = nc.tensor.transpose(bank[3 * (kc % 2) + 2][:, i * P:(i + 1) * P], xraw[:, 4 + i, kc * P:(kc + 1) * P], ident)
                m.then_inc(s_xt, 1)
            for kc in range(KC):
                m = nc.tensor.transpose(bank[1][:, kc * META:(kc + 1) * META], mraw[:, kc * P:(kc + 1) * P],
                                        kt[0:META, K_ID:K_ID + META])
            m.then_inc(s_meta_t, 1)
            norm_sums(0, True)
            pe.wait_ge(n_rstd, 2)
            for b in range(8):
                ada_block(0, b)

            def dft_features(g):
                pe.wait_ge(h_ready, g + 1)
                if g:
                    pe.wait_ge(f_acopy, 3 * g)
                else:
                    pe.wait_ge(s_xlat, KC)
                    pe.wait_ge(s_xctx, KC)
                    pe.wait_ge(s_meta, 1)
                for rt in range(6):
                    m = nc.tensor.matmul(bank[rt // 2][:, 256 * (rt % 2):256 * (rt % 2) + 256],
                                         hT[:, g, rt * P:(rt + 1) * P], dft128, start=True, stop=True)
                    if rt % 2:
                        m.then_inc(f_a, 1)

            def dft_rows(g):
                pe.wait_ge(f_acopy, 3 * g + 3)
                if g == 0:
                    pe.wait_ge(s_dft, 32)
                if g >= 2:
                    pe.wait_ge(f_ycopy, 2 * (g - 1))
                lat, cx = bank[3 + g % 2], bank[5]
                for i in range(NT):
                    for j in range(2):
                        m = nc.tensor.matmul(lat, fa[:, g % 2, i, P * j:P * j + P], dftL[:, i, j, :],
                                             start=i + j == 0, stop=i + j == NT)
                m.then_inc(f_y, 1)
                if g:
                    pe.wait_ge(f_ycopy, 2 * g)
                for i in range(2):
                    for j in range(2):
                        m = nc.tensor.matmul(cx[:, 0:CTX], fa[:, g % 2, 4 + i, P * j:P * j + P], dftC[:, i, j, :],
                                             start=i + j == 0, stop=i + j == 2)
                m.then_inc(f_y, 1)

            dft_features(0)
            for g in range(KC):
                ada_block(0, 8 + 2 * g)
                ada_block(0, 9 + 2 * g)
                dft_rows(g)
                if g + 1 < KC:
                    dft_features(g + 1)
            pe.wait_ge(f_ycopy, 2 * KC)
            for cb in range(4):
                s = begin(("fnet", cb))
                w = weights(("fnet", cb))
                for j in range(2):
                    tile(s, j, [(w[:, kc, P * j:P * j + P], hT[:, kc, :], None) for kc in range(KC)], CTX)
            if stage == 0:
                return

            def ffn(layer, first_h):
                extra = CTX if layer == 0 else 0
                for lo, hi in GROUPS:
                    for p in range(lo, hi):
                        wg = weights(("gate", layer, p))
                        wu = weights(("up", layer, p))
                        for j in range(2):
                            s = begin(("in", layer, p, j))
                            for half, w in ((0, wg), (1, wu)):
                                first = p == 0 and j == 0 and half == 0
                                tile(s, half, [(w[:, kc, P * j:P * j + P], hT[:, kc, :],
                                                (h_ready, first_h + kc + 1) if first else None)
                                               for kc in range(KC)], extra)
                        if layer == 0:
                            for b in ada1_blocks(p):
                                ada_block(1, b)
                    n = 2 * (hi - lo)
                    for cb in range(4):
                        s = begin(("down", layer, lo, cb))
                        w = weights(("down", layer, lo, cb))
                        for j in range(2):
                            tile(s, j, [(w[:, c, P * j:P * j + P], hid[:, c, :],
                                         (g_hid, 22 * layer + 2 * lo + c + 1) if cb + j == 0 else None)
                                        for c in range(n)], extra)

            pe.wait_ge(ada_taken, 24)
            norm_sums(1, True)
            pe.wait_ge(n_rstd, 4)
            ffn(0, KC)
            if stage == 1:
                return

            pe.wait_ge(ada_taken, 48)
            norm_sums(2, True)
            done = [0]

            def stat(i, with_ctx):
                pe.wait_ge(k_sq, i + 1)
                if i:
                    pe.wait_ge(k_rstd, i)
                else:
                    pe.wait_ge(n_rstd, 6)
                for a, b, half in halves(with_ctx):
                    m = nc.tensor.matmul(bank[6 + half][:, 0:b - a], blk, sq[:, i % 2, a:b], start=True, stop=True)
                m.then_inc(k_sum, 1)

            for i, kind in enumerate(["dk"] * 8 + ["dq"] * 8):
                cb, j = (i % 8) // 2, i % 2
                if j == 0:
                    s = begin((kind, cb))
                    w = weights((kind, cb))
                tile(s, j, [(w[:, kc, P * j:P * j + P], hT[:, kc, :], (h_ready, 2 * KC + kc + 1) if i == 0 else None)
                            for kc in range(KC)], CTX if kind == "dk" else 0)
                if i:
                    stat(i - 1, i - 1 < 8)
            for cb in range(4):
                s = begin(("dv", cb))
                w = weights(("dv", cb))
                for rt in range(6):
                    for kc in range(KC):
                        m = nc.tensor.matmul(bank[3 * s + rt // 2][:, 256 * (rt % 2):256 * (rt % 2) + 256],
                                             hT[:, kc, rt * P:(rt + 1) * P], w[:, kc, :], start=kc == 0, stop=kc == KC - 1)
                m.then_inc(tile_done, 2)
                if cb == 0:
                    stat(15, False)
            for cb in (2, 3):
                for w in banks_read(T_OF[("dv", cb)]):
                    pe.wait_ge(*w)
            pe.wait_ge(k_done, 16)
            pe.wait_ge(k_rstd, 16)

            def scores(u):
                h, i = u // NT, u % NT
                for c in range(2):
                    if u:
                        pe.wait_ge(a_exp, 2 * (u - 1) + c + 1)
                    r = slice(DH * c, DH * c + DH)
                    nc.tensor.matmul(two[c][:, 0:LAT], qT[r, h, i * P:(i + 1) * P], kT[r, h, 0:LAT], start=True, stop=True)
                    nc.tensor.matmul(two[c][:, LAT:ROWS], qT[r, h, i * P:(i + 1) * P], kT[r, h, LAT:ROWS],
                                     start=True, stop=True).then_inc(a_s, 1)

            def turn(u):
                pe.wait_ge(a_w, u + 1)
                for c in range(2):
                    if u:
                        pe.wait_ge(a_wtc, 2 * (u - 1) + c + 1)
                    for i in range(3):
                        m = nc.tensor.transpose(bank[4 + c][:, i * P:(i + 1) * P], prob[:, u % 2, 1, (3 * c + i) * P:(3 * c + i + 1) * P], ident)
                    m.then_inc(a_wt, 1)

            def head_stat(h):
                pe.wait_ge(a_sq, h + 1)
                if h:
                    pe.wait_ge(a_rs, h)
                nc.tensor.matmul(bank[7], ones, sq[:, h % 2, 0:LAT], start=True, stop=True).then_inc(a_ms, 1)

            scores(0)
            for u in range(4 * HEADS):
                if u + 1 < 4 * HEADS:
                    scores(u + 1)
                turn(u)
                if u % NT == NT - 1:
                    h = u // NT
                    pe.wait_ge(a_wtc, 2 * u + 2)
                    if h:
                        pe.wait_ge(a_o, h)
                    for i in range(6):
                        m = nc.tensor.matmul(bank[6], V[:, i, h * P:(h + 1) * P], WT[:, i, :], start=i == 0, stop=i == 5)
                    m.then_inc(a_pv, 1)
                    head_stat(h)
            pe.wait_ge(a_exp, 8 * HEADS)
            pe.wait_ge(a_wtc, 8 * HEADS)
            pe.wait_ge(a_o, HEADS)
            for cb in range(4):
                s = begin(("dout", cb))
                w = weights(("dout", cb))
                for j in range(2):
                    tile(s, j, [(w[:, kc, P * j:P * j + P], hT[:, kc, :], None) for kc in range(KC)], 0)
            if stage == 2:
                return
            norm_sums(3, False)
            ffn(1, 3 * KC)
            if stage == 3:
                return

            for kc in range(KC):
                pe.wait_ge(n_sq, NORM_SQ[4] + kc + 1)
                nc.tensor.matmul(bank[6], ones, sqb[:, kc % 2, 0:LAT], start=kc == 0, stop=kc == KC - 1)
                nc.tensor.matmul(bank[7][:, 0:META], ones, sqb[:, kc % 2, LAT:ALL], start=kc == 0, stop=kc == KC - 1) \
                    .then_inc(n_used, 1)
            pe.wait_ge(n_rstd, 9)
            pe.wait_ge(h_ready, 5 * KC)
            pe.wait_ge(s_small, 16 * 8)
            for i in range(5):
                r = slice(i * P, min((i + 1) * P, ALL))
                for kc in range(KC):
                    m = nc.tensor.matmul(bank[6][0:r.stop - r.start, 48 * i:48 * i + 48], uT[:, kc, r], wdtf[:, kc, :],
                                         start=kc == 0, stop=kc == KC - 1)
            m.then_inc(d_raw, 1)

            def gemm(key, extra):
                s = begin(key)
                w = weights(key)
                for j in range(2):
                    tile(s, j, [(w[:, kc, P * j:P * j + P], uT[:, kc, :], None) for kc in range(KC)], extra)

            def rows_gemm(key, src, extra):
                s = begin(key)
                w = weights(key)
                for i in range(NT + (extra > 0)):
                    n = P if i < NT else extra
                    for kc in range(KC):
                        m = nc.tensor.matmul(bank[3 * s + i // 2][0:n, 256 * (i % 2):256 * (i % 2) + 256],
                                             src[:, kc, i * P:i * P + n], w[:, kc, :], start=kc == 0, stop=kc == KC - 1)
                m.then_inc(tile_done, 2)

            def b_rows(g):
                pe.wait_ge(c_out, g + 1)
                if g:
                    pe.wait_ge(c_tev, g)
                else:
                    pe.wait_ge(d_cta, 1)
                for i in range(3):
                    nc.tensor.transpose(bank[6][:, i * P:(i + 1) * P], BT[:, g, META + i * P:META + (i + 1) * P], ident)
                nc.tensor.transpose(bank[6][0:META, 3 * P:4 * P], BT[:, g, 0:META], ident).then_inc(c_t, 1)

            gemm(("B", 0), META)
            gemm(("B", 1), META)
            pe.wait_ge(d_adt, 1)
            for i in range(NT):
                nc.tensor.matmul(bank[6][:, 32 * i:32 * i + 32], upper, adt[:, i, :], start=True, stop=True)
            for i in range(3):
                nc.tensor.matmul(bank[6][:, 128 + 32 * i:160 + 32 * i], lower, adt[:, i, :], start=True, stop=True)
            for i in range(3):
                nc.tensor.matmul(bank[6][:, 224 + 32 * i:256 + 32 * i], ones, adt[:, i, :], start=True, stop=True)
            nc.tensor.matmul(bank[6][0:META, 320:352], lower[0:META, 0:META], adt[0:META, 4, :], start=True, stop=True).then_inc(d_sums, 1)
            for i in range(NT):
                c = slice(i * P, (i + 1) * P)
                nc.tensor.matmul(bank[7][0:16, c], logf[0:META, 4, :], ones[0:META, :], start=True, stop=False)
                for j in range(i):
                    nc.tensor.matmul(bank[7][0:16, c], logf[:, j, :], ones, start=False, stop=False)
                nc.tensor.matmul(bank[7][0:16, c], logf[:, i, :], upper, start=False, stop=True)
            pe.wait_ge(d_dec, 1)
            nc.tensor.matmul(bank[6][0:16, 0:META], logf[0:META, 4, :], upper[0:META, 0:META], start=True, stop=True).then_inc(d_ct, 1)
            gemm(("C", 0), META)
            gemm(("C", 1), META)
            for g in range(4):
                b_rows(g)
            pe.wait_ge(c_out, 8)

            def ssd(g):
                n0 = 4 * g
                for j in range(4):
                    i = 8 + 4 * g + j
                    pe.wait_ge(c_out, i + 1)
                    pe.wait_ge(c_tev, 4 + 2 * (4 * g + j) if g + j else 4)
                    if g and j == 0:
                        pe.wait_ge(e_tev, 4 * g)
                    for k in range(NT):
                        nc.tensor.transpose(bank[6][:, k * P:(k + 1) * P], cacc[:, i % 2, META + k * P:META + (k + 1) * P], ident)
                    nc.tensor.transpose(bank[7][0:META, 0:P], cacc[:, i % 2, 0:META], ident).then_inc(c_t, 1)
                for w in banks_read(T_OF[("xs", g, 0)]) + banks_read(T_OF[("xs", g, 1)]):
                    pe.wait_ge(*w)
                pe.wait_ge(c_tev, 4 + 2 * (4 * g + 4))
                pe.wait_ge(p_xds, n0 + 1)
                nc.tensor.matmul(bank[5], Brow[0:META, 3, g * P:(g + 1) * P], xds[0:META, :], start=True, stop=True).then_inc(e_st, 1)
                for i in range(NT):
                    n = n0 + i
                    pe.wait_ge(p_lseg, n + 1)
                    for h in range(8):
                        m = nc.tensor.matmul(two[0][:, h * P:(h + 1) * P], lseg[:, h * P:(h + 1) * P], upper, start=True, stop=True)
                    m.then_inc(e_seg, 1)
                    nc.tensor.matmul(bank[2], BT[:, g, META + i * P:META + (i + 1) * P], CTt[:, g, i * P:(i + 1) * P],
                                     start=True, stop=True) if False else \
                        nc.tensor.matmul(bank[2][:, 0:P], BT[:, g, META + i * P:META + (i + 1) * P], CTt[:, g, i * P:(i + 1) * P],
                                         start=True, stop=True).then_inc(e_cb, 1)
                    pe.wait_ge(e_h, n + 1)
                    nc.tensor.matmul(bank[4], CTt[:, g, i * P:(i + 1) * P], Hst[:, i % 2, :], start=True, stop=True).then_inc(e_yoff, 1)
                    if i < 3:
                        pe.wait_ge(p_xds, n + 2)
                        nc.tensor.matmul(bank[5], Brow[:, i, g * P:(g + 1) * P], xds[:, :], start=True, stop=True).then_inc(e_st, 1)
                    pe.wait_ge(p_xdt, 5 * g + i + 2)
                    pe.wait_ge(e_m, n + 1)
                    for h in range(8):
                        m = nc.tensor.matmul(bank[3][:, 64 * h:64 * h + 64], Mt[:, h, :], xdt[:, (i + 1) % 2, 64 * h:64 * h + 64],
                                             start=True, stop=True)
                    m.then_inc(e_y, 1)
                    pe.wait_ge(e_un, n + 1)
                    if n:
                        pe.wait_ge(e_tev, n)
                    for j in range(4):
                        m = nc.tensor.transpose(bank[6][:, j * P:(j + 1) * P], yrow[:, j * P:(j + 1) * P], ident)
                    m.then_inc(e_t, 1)

            for g in range(SG):
                if g:
                    pe.wait_ge(e_gated, 4 * g)
                rows_gemm(("z", g, 0), uT, 0)
                rows_gemm(("z", g, 1), uT, 0)
                gemm(("xs", g, 0), META)
                gemm(("xs", g, 1), META)
                ssd(g)
            pe.wait_ge(e_gated, 16)
            pe.wait_ge(e_tev, 16)

            def spans(i):
                n = META + (i + 1) * P
                return [(0, min(n, 512))] + ([(512, n)] if n > 512 else [])

            def fox_scores(u):
                f, i, h = u // 16, u // 4 % 4, u % 4
                S = two[u % 2]
                if u >= 2:
                    pe.wait_ge(b_exp, u - 1)
                n = META + (i + 1) * P
                for a, b in spans(i):
                    nc.tensor.matmul(S[:, a:b], qA[0:DH + 2, h, i * P:(i + 1) * P], kA[0:DH + 2, h, a:b], start=True, stop=False)
                    o = max(a, n - P)
                    m = nc.tensor.matmul(S[:, o:b], ident, negm[:, o - (n - P):b - (n - P)], start=False, stop=True)
                m.then_inc(b_s, 1)

            def fox_turn(u):
                f, i, h = u // 16, u // 4 % 4, u % 4
                pe.wait_ge(b_exp, u + 1)
                if u:
                    pe.wait_ge(b_pta, u)
                    pe.wait_ge(b_ptd, u)
                for j in range(i + 1):
                    nc.tensor.transpose(bank[4][:, j * P:(j + 1) * P], probA[:, u % 2, META + j * P:META + (j + 1) * P], ident)
                nc.tensor.transpose(bank[5][0:META, 0:P], probA[:, u % 2, 0:META], ident).then_inc(b_pt, 1)

            def fox_out(u):
                f, i, h = u // 16, u // 4 % 4, u % 4
                pe.wait_ge(b_pta, u + 1)
                pe.wait_ge(b_ptd, u + 1)
                if h == 0 and u:
                    pe.wait_ge(b_y, u // 4)
                o = bank[7][:, 64 * h:64 * h + 64]
                nc.tensor.matmul(o, PT[0:META, u % 2, 4 * P:5 * P], vA[0:META, 4, 64 * h:64 * h + 64], start=True, stop=False)
                for j in range(i + 1):
                    m = nc.tensor.matmul(o, PT[:, u % 2, j * P:(j + 1) * P], vA[:, j, 64 * h:64 * h + 64], start=False, stop=j == i)
                m.then_inc(b_o, 1)

            def fox_back(v):
                pe.wait_ge(b_y, v + 1)
                if v:
                    pe.wait_ge(b_ytev, v)
                for j in range(2):
                    m = nc.tensor.transpose(bank[6][:, j * P:(j + 1) * P], yA[:, j * P:(j + 1) * P], ident)
                m.then_inc(b_yt, 1)

            for f in range(4):
                if f:
                    pe.wait_ge(b_exp, 16 * f)
                    pe.wait_ge(b_pta, 16 * f)
                    pe.wait_ge(b_ptd, 16 * f)
                gemm(("q", f), 0)
                gemm(("k", f), META)
                rows_gemm(("v", f), uT, META)
                rows_gemm(("za", f), uT, 0)
                pe.wait_ge(b_q, 16 * (f + 1))
                pe.wait_ge(b_k, 16 * (f + 1))
                for w in sum((banks_read(T_OF[(k, f)]) for k in ("k", "v", "za")), []):
                    pe.wait_ge(*w)
                fox_scores(16 * f)
                for u in range(16 * f, 16 * f + 16):
                    if u + 1 < 16 * f + 16:
                        fox_scores(u + 1)
                    fox_turn(u)
                    fox_out(u)
                    if u % 4 == 3:
                        fox_back(u // 4)

            pe.wait_ge(b_exp, 64)
            pe.wait_ge(b_pta, 64)
            pe.wait_ge(b_ptd, 64)
            pe.wait_ge(b_ytev, 16)
            for cb in range(4):
                gemm(("gs", cb), 0)
                gemm(("ga", cb), 0)
                s = begin(("ps", cb))
                w0 = weights(("ps", cb, 0))
                w1 = weights(("ps", cb, 1))
                for j in range(2):
                    tile(s, j, [((w0, w1)[k // KC][:, k % KC, P * j:P * j + P], ysT[:, k, :], None) for k in range(2 * KC)], 0)
                s = begin(("pa", cb))
                w = weights(("pa", cb))
                for j in range(2):
                    tile(s, j, [(w[:, kc, P * j:P * j + P], yaT[:, kc, :], None) for kc in range(KC)], 0)
            pe.wait_ge(m_mix, 8)
            for cb in range(4):
                rows_gemm(("wo", cb), mg, 0)
            for i in range(2 * NT):
                if i >= 2:
                    pe.wait_ge(o_fin, i - 1)
                for j in range(4):
                    m = nc.tensor.transpose(bank[6 + i % 2][:, j * P:(j + 1) * P],
                                            xT[:, 4 * (i % 2) + j, (i // 2) * P:(i // 2 + 1) * P], ident)
                m.then_inc(o_xt, 1)

        @block.scalar
        def _(act):
            link = Chain(act, a_chain)
            def rows(dst, a, n, src):
                act.dma_start(dst[a:a + n, :], src).then_inc(s_tab, 16)

            rows(rowA, ROW_C, 8, io["c"].rearrange("a (m p) -> (a m) p", p=P))
            rows(rowA, ROW_CC, 8, io["c_ctx"].rearrange("(m p) -> m p", p=P))
            rows(rowA, ROW_NG, 32, io["norm_gain"].rearrange("a b (m p) -> (a b m) p", p=P))
            rows(rowA, ROW_FB, 8, io["fnet_b_out"].rearrange("a (m p) -> (a m) p", p=P))
            rows(rowA, ROW_NP, 8, io["norm_pre_2"].rearrange("a (m p) -> (a m) p", p=P))
            rows(rowA, ROW_SN, 16, io["ssd_norm_2"].rearrange("a (m p) -> (a m) p", p=P))
            rows(rowA, ROW_GB, 16, io["gate_bias_2"].rearrange("a (m p) -> (a m) p", p=P))
            rows(rowA, ROW_SUB, 1, io["diff_subln_gain"])
            rows(rowA, ROW_QG, 1, io["diff_q_gain"].rearrange("a b d -> a (b d)"))
            rows(rowA, ROW_KG, 1, io["diff_k_gain"].rearrange("a b d -> a (b d)"))
            act.dma_start(rowB[0:96, :], io["b_ada"].rearrange("a (m p) -> (a m) p", p=P)).then_inc(s_tab, 16)
            act.dma_start(rowB[96:120, :], io["conv_b_2"].rearrange("a (m p) -> (a m) p", p=P)).then_inc(s_tab, 16)
            act.dma_start(rowC[:, :], io["conv_w_2"].rearrange("a k (m p) -> (a k m) p", p=P)).then_inc(s_tab, 16)
            act.dma_start(lamv[:], io["diff_lambda"].rearrange("a b d -> a (b d)").broadcast_to([P, 4 * DH])).then_inc(s_small, 16)
            act.dma_start(wdtf[:, :, 0:32], w_in2[:, COL_DT:COL_DT + 32].rearrange("(c p) n -> p c n", p=P)).then_inc(s_small, 16)
            act.dma_start(wdtf[:, :, 32:48], w_in2[:, COL_F:COL_F + 16].rearrange("(c p) n -> p c n", p=P)).then_inc(s_small, 16)
            act.dma_start(bdtf[:, 0:32], io["dt_bias_2"].broadcast_to([P, 32])).then_inc(s_small, 16)
            act.dma_start(bdtf[:, 32:48], io["fgate_bias_2"].broadcast_to([P, 16])).then_inc(s_small, 16)
            act.dma_start(alog[:], io["a_log_2"].broadcast_to([P, 32])).then_inc(s_small, 16)
            act.dma_start(dskip[:], io["d_skip_2"].broadcast_to([P, 32])).then_inc(s_small, 16)
            act.dma_start(gpost[:], io["norm_post_2"].broadcast_to([P, D])).then_inc(s_small, 16)

            act.wait_ge(s_cols_t, 3)
            for b, c, n in ((0, colA, N_A), (1, colB, N_B), (2, colC, N_C)):
                nc.scalar.activation(c[:], bank[b][:, 0:n], ACT.Copy).then_inc(s_cols, 1)
            act.wait_ge(s_cols, 3)
            for j, r in enumerate((ROW_C, ROW_CC)):
                nc.scalar.activation(cond[:, :, j], colA[:, r:r + 8], ACT.Silu).then_inc(s_cond, 1)
            for kc in range(KC):
                act.wait_ge(s_xt, kc + 1)
                nc.scalar.activation(xT[:, kc, LAT:ROWS], bank[3 * (kc % 2) + 2][:, 0:CTX], ACT.Copy).then_inc(s_xctx, 1)
            act.wait_ge(s_meta_t, 1)
            nc.scalar.activation(metaT[:].rearrange("p c r -> p (c r)"), bank[1][:, 0:P], ACT.Copy).then_inc(s_meta, 1)

            def norm(i, with_ctx, ready=None):
                end = ROWS if with_ctx else LAT
                for kc in range(KC):
                    if ready is not None:
                        act.wait_ge(*ready(kc))
                    k = NORM_SQ[i] + kc
                    if k >= 2:
                        act.wait_ge(n_used, k - 1)
                    nc.scalar.activation(sq[:, kc % 2, 0:end], xT[:, kc, 0:end], ACT.Square).then_inc(n_sq, 1)
                act.wait_ge(n_used, NORM_SQ[i] + KC)
                for a, b, half in halves(with_ctx):
                    link(nc.scalar.activation(rstd[:, a:b], bank[6 + half][:, 0:b - a], ACT.Ln, bias=epsc[:], scale=1.0 / D))
                    link.wait()
                    nc.scalar.activation(rstd[:, a:b], rstd[:, a:b], ACT.Exp, scale=-0.5).then_inc(n_rstd, 1)

            act.wait_ge(s_xlat, KC)
            act.wait_ge(s_xctx, KC)
            norm(0, True)

            for g in range(KC):
                act.wait_ge(f_a, 3 * g + 2)
                if g >= 2:
                    act.wait_ge(f_y, 2 * (g - 1))
                act.wait_ge(f_acopy, 3 * g + 1)
                nc.scalar.activation(fa[:, g % 2, 2:4, :].rearrange("p a n -> p (a n)"), bank[1], ACT.Copy).then_inc(f_acopy, 1)
                act.wait_ge(f_y, 2 * g + 1)
                nc.scalar.activation(hT[:, g, 0:LAT], bank[3 + g % 2], ACT.Copy).then_inc(f_ycopy, 1)
                act.wait_ge(f_y, 2 * g + 2)
                nc.scalar.activation(hT[:, g, LAT:ROWS], bank[5][:, 0:CTX], ACT.Copy).then_inc(f_ycopy, 1)
            for cb in range(4):
                t = T_OF[("fnet", cb)]
                s = t % 2
                act.wait_ge(tile_done, 2 * t + 2)
                for j in range(2):
                    m = 2 * cb + j
                    if m >= 2:
                        act.wait_ge(r_res, m - 1)
                    link(nc.scalar.activation(tmpF[:, j, 0:LAT], bank[3 * s + j], ACT.Identity, bias=colA[:, ROW_FB + m:ROW_FB + m + 1]))
                    nc.scalar.activation(tmpF[:, j, LAT:ROWS], bank[3 * s + 2][:, 256 * j:256 * j + 256], ACT.Identity,
                                         bias=colA[:, ROW_FB + m:ROW_FB + m + 1]).then_inc(r_tmp, 1)
            if stage == 0:
                return

            def ffn(layer):
                end = ROWS if layer == 0 else LAT
                for lo, hi in GROUPS:
                    for p in range(lo, hi):
                        for j in range(2):
                            t = T_OF[("in", layer, p, j)]
                            s, c = t % 2, 22 * layer + 2 * p + j
                            act.wait_ge(tile_done, 2 * t + (2 if layer == 0 else 1))
                            if c >= 2:
                                act.wait_ge(g_hid, c - 1)
                            m = nc.scalar.activation(gateS[:, c % 2, 0:LAT], bank[3 * s], ACT.Silu)
                            if layer == 0:
                                link(m)
                                m = nc.scalar.activation(gateS[:, c % 2, LAT:ROWS], bank[3 * s + 2][:, 0:CTX], ACT.Silu)
                            m.then_inc(g_silu, 1)

            norm(1, True, lambda kc: (r_res, kc + 1))
            ffn(0)
            if stage == 1:
                return
            norm(2, True, lambda kc: (r_res, 24 + kc + 1))

            def stats(i):
                with_ctx = i < 8
                t, j = T_OF[("dk", 0)] + i // 2, i % 2
                act.wait_ge(tile_done, 2 * t + 2)
                if i >= 2:
                    act.wait_ge(k_sum, i - 1)
                else:
                    act.wait_ge(n_used, NORM_SQ[2] + KC)
                m = nc.scalar.activation(sq[:, i % 2, 0:LAT], bank[3 * (t % 2) + j], ACT.Square)
                if with_ctx:
                    link(m)
                    m = nc.scalar.activation(sq[:, i % 2, LAT:ROWS], bank[3 * (t % 2) + 2][:, 256 * j:256 * j + 256], ACT.Square)
                m.then_inc(k_sq, 1)

            def finish(i):
                with_ctx = i < 8
                act.wait_ge(k_sum, i + 1)
                if i:
                    act.wait_ge(k_norm, i)
                for a, b, half in halves(with_ctx):
                    link(nc.scalar.activation(rstd[:, a:b], bank[6 + half][:, 0:b - a], ACT.Ln, bias=epsc[:], scale=1.0 / DH))
                    link.wait()
                    m = nc.scalar.activation(rstd[:, a:b], rstd[:, a:b], ACT.Exp, scale=-0.5)
                    if with_ctx and half == 0:
                        link(m)
                m.then_inc(k_rstd, 1)
                act.wait_ge(k_norm, i + 1)
                if i:
                    act.wait_ge(k_done, i)
                for q in range(4):
                    o = 32 * (q ^ 1)
                    m = nc.scalar.activation(krot[32 * q:32 * q + 32, :], kraw[o:o + 32, :], ACT.Copy)
                    if q < 3:
                        link(m)
                m.then_inc(k_rot, 1)

            act.wait_ge(h_ready, 3 * KC)
            for i in range(16):
                stats(i)
                if i % 2:
                    finish(i - 1)
                    finish(i)
            for cb in range(4):
                t = T_OF[("dv", cb)]
                act.wait_ge(tile_done, 2 * t + 2)
                nc.scalar.activation(V[:, 2:4, 256 * cb:256 * cb + 256], bank[3 * (t % 2) + 1].rearrange("p (a n) -> p a n", a=2), ACT.Copy) \
                    .then_inc(v_copy, 1)

            def head_end(h):
                act.wait_ge(a_pv, h + 1)
                nc.scalar.activation(sq[:, h % 2, 0:LAT], bank[6], ACT.Square).then_inc(a_sq, 1)
                act.wait_ge(a_ms, h + 1)
                if h:
                    act.wait_ge(a_o, h)
                link(nc.scalar.activation(rstd[:, 0:LAT], bank[7], ACT.Ln, bias=epsc[:], scale=1.0 / P))
                link.wait()
                nc.scalar.activation(rstd[:, 0:LAT], rstd[:, 0:LAT], ACT.Exp, scale=-0.5).then_inc(a_rs, 1)

            act.wait_ge(s_lam, 1)
            nc.scalar.activation(lams[:, 2:4], lams[:, 4:6], ACT.Exp).then_inc(s_lamx, 1)
            act.wait_ge(k_done, 16)
            for u in range(4 * HEADS):
                for c in range(2):
                    act.wait_ge(a_max, 2 * u + c + 1)
                    if u >= 2:
                        act.wait_ge(a_wt, 2 * (u - 1))
                    nc.scalar.activation(prob[:, u % 2, c, :], two[c][:, 0:ROWS], ACT.Exp, bias=attmx[:, u % 2, c, 1:2],
                                         scale=DH ** -0.5, accum_out=attmx[:, u % 2, c, 2:3]).then_inc(a_exp, 1)
                h, i = u // NT, u % NT
                act.wait_ge(a_wt, 2 * u + 1)
                if i == 0 and h:
                    act.wait_ge(a_pv, h)
                nc.scalar.activation(WT[:, 0:3, i * P:(i + 1) * P], bank[4][:, 0:3 * P].rearrange("p (a n) -> p a n", a=3), ACT.Copy) \
                    .then_inc(a_wtc, 1)
                if i == NT - 1:
                    head_end(h)
            if stage == 2:
                return
            norm(3, False, lambda kc: (r_res, 32 + kc + 1))
            ffn(1)
            if stage == 3:
                return

            for kc in range(KC):
                act.wait_ge(r_res, 56 + kc + 1)
                k = NORM_SQ[4] + kc
                act.wait_ge(n_used, k - 1)
                link(nc.scalar.activation(sqb[:, kc % 2, 0:LAT], xT[:, kc, 0:LAT], ACT.Square))
                nc.scalar.activation(sqb[:, kc % 2, LAT:ALL], metaT[:, kc, :], ACT.Square).then_inc(n_sq, 1)
            act.wait_ge(n_used, NORM_SQ[4] + KC)
            for a, b, half in ((0, LAT, 0), (LAT, ALL, 1)):
                link(nc.scalar.activation(rstdb[:, a:b], bank[6 + half][:, 0:b - a], ACT.Ln, bias=epsc[:], scale=1.0 / D))
                link.wait()
                nc.scalar.activation(rstdb[:, a:b], rstdb[:, a:b], ACT.Exp, scale=-0.5).then_inc(n_rstd, 1)
            nc.scalar.activation(expa[:], alog[:], ACT.Exp).then_inc(d_expa, 1)
            act.wait_ge(d_biased, 1)
            nc.scalar.activation(dtu, dta, ACT.Exp, scale=-1.0).then_inc(d_u, 1)
            act.wait_ge(d_w, 1)
            nc.scalar.activation(dtl, dtw, ACT.Ln).then_inc(d_ln, 1)

            def conv_in(kind, key):
                t = T_OF[key]
                act.wait_ge(tile_done, 2 * t + 2)
                for j in range(2):
                    i = conv_tile(kind, key, j)
                    if i >= 2:
                        act.wait_ge(c_acc, i - 1)
                    else:
                        act.wait_ge(d_zero, 1)
                    link(nc.scalar.activation(cin[:, i % 2, 3:3 + META], bank[3 * (t % 2) + 2][:, 256 * j:256 * j + META], ACT.Copy))
                    nc.scalar.activation(cin[:, i % 2, 3 + META:3 + ALL], bank[3 * (t % 2) + j], ACT.Copy).then_inc(c_in, 1)

            def conv_out(kind, key):
                for j in range(2):
                    i = conv_tile(kind, key, j)
                    ch = {"B": 16, "C": 20 - 4, "xs": -8}[kind] + i
                    bias = colB[:, ROW_CB + ch:ROW_CB + ch + 1]
                    act.wait_ge(c_acc, i + 1)
                    if kind == "B":
                        m = nc.scalar.activation(BT[:, i, :], cacc[:, i % 2, :], ACT.Silu, bias=bias)
                    elif kind == "C":
                        m = nc.scalar.activation(CTt[:, i - 4, :], cacc[:, i % 2, META:ALL], ACT.Silu, bias=bias)
                    else:
                        m = nc.scalar.activation(cacc[:, i % 2, :], cacc[:, i % 2, :], ACT.Silu, bias=bias)
                    m.then_inc(c_out, 1)

            def conv(kind, key):
                conv_in(kind, key)
                conv_out(kind, key)

            conv("B", ("B", 0))
            act.wait_ge(d_sums, 1)
            link(nc.scalar.activation(dec[:, 0:320], bank[6][:, 0:320], ACT.Exp))
            nc.scalar.activation(dec[0:META, 320:352], bank[6][0:META, 320:352], ACT.Exp).then_inc(d_dec, 1)
            act.wait_ge(d_ct, 1)
            link(nc.scalar.activation(ckT[:, META:ALL], bank[7][0:16, :], ACT.Copy, scale=-8.0))
            link(nc.scalar.activation(cqT[:, :], bank[7][0:16, :], ACT.Copy, scale=8.0))
            nc.scalar.activation(ckT[:, 0:META], bank[6][0:16, 0:META], ACT.Copy, scale=-8.0).then_inc(d_cta, 1)
            conv("B", ("B", 1))
            conv("C", ("C", 0))
            conv("C", ("C", 1))
            for g in range(SG):
                for j in range(2):
                    t = T_OF[("z", g, j)]
                    act.wait_ge(tile_done, 2 * t + 2)
                    if g and j == 0:
                        act.wait_ge(e_gated, 4 * g)
                    for i in range(2):
                        m = nc.scalar.activation(zrow[:, 2 * i:2 * i + 2, 256 * j:256 * j + 256],
                                                 bank[3 * (t % 2) + i].rearrange("p (a n) -> p a n", a=2), ACT.Silu)
                        if i == 0:
                            link(m)
                    m.then_inc(z_act, 1)
                for j in range(2):
                    conv("xs", ("xs", g, j))
                    for jj in range(2):
                        i = 4 * g + 2 * j + jj
                        act.wait_ge(c_t, 4 + i + 1)
                        nc.scalar.activation(xrow[0:META, 4, P * (i % 4):P * (i % 4) + P], bank[7][0:META, 0:P], ACT.Copy).then_inc(c_tev, 1)
                for i in range(NT):
                    n = 4 * g + i
                    act.wait_ge(e_seg, n + 1)
                    if n:
                        act.wait_ge(e_y, n)
                    nc.scalar.activation(Mt[:].rearrange("p a n -> p (a n)"), two[0][:, :], ACT.Exp).then_inc(e_exp, 1)
                    act.wait_ge(e_ss, n + 1)
                    link(nc.scalar.activation(stt4[:, 1:2], stt4[:, 0:1], ACT.Ln, bias=epsc[:], scale=1.0 / 512))
                    link.wait()
                    nc.scalar.activation(stt4[:, 2:3], stt4[:, 1:2], ACT.Exp, scale=-0.5).then_inc(e_rs, 1)

            for f in range(4):
                for k, kind in enumerate("qk"):
                    t = T_OF[(kind, f)]
                    dst = qA if kind == "q" else kA
                    o = 0 if kind == "q" else META
                    act.wait_ge(tile_done, 2 * t + 1)
                    if f:
                        act.wait_ge(b_s, 16 * f)
                    link(nc.scalar.activation(dst[0:DH, 0, o:o + LAT], bank[3 * (t % 2)][0:DH, :], ACT.Copy))
                    nc.scalar.activation(dst[0:DH, 1, o:o + LAT], bank[3 * (t % 2)][DH:P, :], ACT.Copy).then_inc(x_act, 1)
                t = T_OF[("v", f)]
                act.wait_ge(tile_done, 2 * t + 2)
                if f:
                    act.wait_ge(b_o, 16 * f)
                nc.scalar.activation(vA[:, 0:2, :], bank[3 * (t % 2)].rearrange("p (a n) -> p a n", a=2), ACT.Copy).then_inc(x_act, 1)
                t = T_OF[("za", f)]
                act.wait_ge(tile_done, 2 * t + 2)
                if f:
                    act.wait_ge(b_y, 4 * f)
                link(nc.scalar.activation(zA[:, 0:2, :], bank[3 * (t % 2)].rearrange("p (a n) -> p a n", a=2), ACT.Silu))
                nc.scalar.activation(zA[:, 2:4, :], bank[3 * (t % 2) + 1].rearrange("p (a n) -> p a n", a=2), ACT.Silu).then_inc(z_act, 1)
                for u in range(16 * f, 16 * f + 16):
                    i, h = u // 4 % 4, u % 4
                    n = META + (i + 1) * P
                    act.wait_ge(b_max, u + 1)
                    if u >= 2:
                        act.wait_ge(b_pt, u - 1)
                    if h == 0 and u >= 16:
                        act.wait_ge(b_y, u // 4 - 3)
                    nc.scalar.activation(probA[:, u % 2, 0:n], two[u % 2][:, 0:n], ACT.Exp, bias=amx[:, u % 2, 1:2],
                                         scale=DH ** -0.5, accum_out=asum[:, i, h:h + 1]).then_inc(b_exp, 1)
                    act.wait_ge(b_pt, u + 1)
                    if u >= 2:
                        act.wait_ge(b_o, u - 1)
                    nc.scalar.activation(PT[:, u % 2, 0:(i + 1) * P], bank[4][:, 0:(i + 1) * P], ACT.Copy).then_inc(b_pta, 1)

            for cb in range(4):
                for k, (kind, dst) in enumerate((("gs", gsb), ("ga", gab))):
                    t = T_OF[(kind, cb)]
                    for j in range(2):
                        act.wait_ge(tile_done, 2 * t + 1 + j)
                        if cb:
                            act.wait_ge(m_mix, 2 * (cb - 1) + k + 1)
                        c = ROW_GB + 8 * k + 2 * cb + j
                        m = nc.scalar.activation(dst[:, j, :], bank[3 * (t % 2) + j], ACT.Sigmoid, bias=colA[:, c:c + 1])
                        if j == 0:
                            link(m)
                    m.then_inc(m_gate, 1)
            for cb in range(4):
                t = T_OF[("wo", cb)]
                act.wait_ge(tile_done, 2 * t + 2)
                for i in range(2):
                    m = nc.scalar.activation(orow[:, 2 * i:2 * i + 2, 256 * cb:256 * cb + 256],
                                             bank[3 * (t % 2) + i].rearrange("p (a n) -> p a n", a=2), ACT.Copy)
                    if i == 0:
                        link(m)
                m.then_inc(o_act, 1)
            act.wait_ge(o_ss, 4)
            link(nc.scalar.activation(stt4[:, 4:8], stt4[:, 0:4], ACT.Ln, bias=epsc[:], scale=1.0 / D))
            link.wait()
            nc.scalar.activation(stt4[:, 4:8], stt4[:, 4:8], ACT.Exp, scale=-0.5).then_inc(o_rs, 1)

        @block.vector
        def _(dve):
            link = Chain(dve, v_chain)
            nc.vector.memset(epsc[:], EPS)
            for kc in range(KC):
                dve.wait_ge(s_xt, kc + 1)
                nc.vector.tensor_copy(xT[:, kc, 0:LAT], bank[3 * (kc % 2)]).then_inc(s_xlat, 1)

            def take_ada(layer, b):
                dve.wait_ge(ada_done, 24 * layer + b + 1)
                o = 48 * layer + 2 * b
                nc.vector.tensor_tensor(ada[layer][:, 2 * b:2 * b + 2, :],
                                        bank[6 + b % 2][:, 0:4].rearrange("p (a n) -> p a n", a=2),
                                        colB[:, o:o + 2].unsqueeze(2).broadcast_to([P, 2, 2]), ALU.add).then_inc(ada_taken, 1)

            def multipliers(i):
                layer, w = i // 2, i % 2
                dve.wait_ge(ada_taken, 24 * layer + 12 * w + 8)
                nc.vector.scalar_tensor_tensor(out=mult[:, i], in0=ada[layer][:, 24 * w + 8:24 * w + 16, :], scalar=1.0,
                                               in1=colA[:, ROW_NG + 8 * i:ROW_NG + 8 * i + 8].unsqueeze(2).broadcast_to([P, KC, 2]),
                                               op0=ALU.add, op1=ALU.mult).then_inc(s_mult, 1)
                dve.wait_ge(s_mult, i + 1)

            def modulated(i, with_ctx):
                layer, w = i // 2, i % 2
                end = ROWS if with_ctx else LAT
                dve.wait_ge(n_rstd, {0: 2, 1: 4, 2: 6, 3: 7}[i])
                for kc in range(KC):
                    link(nc.vector.tensor_tensor(hT[:, kc, 0:end], xT[:, kc, 0:end], rstd[:, 0:end], ALU.mult))
                    if kc:
                        scale_shift(i, kc - 1, with_ctx)
                scale_shift(i, KC - 1, with_ctx)

            def scale_shift(i, kc, with_ctx):
                layer, w = i // 2, i % 2
                link.wait()
                for a, b, half in halves(with_ctx):
                    m = nc.vector.tensor_scalar(hT[:, kc, a:b], hT[:, kc, a:b], mult[:, i, kc, half:half + 1],
                                                ada[layer][:, 24 * w + kc, half:half + 1], ALU.mult, ALU.add)
                m.then_inc(h_ready, 1)

            dve.wait_ge(s_cols, 3)
            for b in range(8):
                take_ada(0, b)
            multipliers(0)
            dve.wait_ge(s_xctx, KC)
            modulated(0, True)
            for g in range(KC):
                if g >= 2:
                    dve.wait_ge(f_y, 2 * (g - 1))
                dve.wait_ge(f_a, 3 * g + 1)
                nc.vector.tensor_copy(fa[:, g % 2, 0:2, :].rearrange("p a n -> p (a n)"), bank[0]).then_inc(f_acopy, 1)
                dve.wait_ge(f_acopy, 3 * g + 2)
                dve.wait_ge(f_a, 3 * g + 3)
                nc.vector.tensor_copy(fa[:, g % 2, 4:6, :].rearrange("p a n -> p (a n)"), bank[2]).then_inc(f_acopy, 1)
                take_ada(0, 8 + 2 * g)
                take_ada(0, 9 + 2 * g)
            multipliers(1)
            for cb in range(4):
                for j in range(2):
                    m = 2 * cb + j
                    dve.wait_ge(r_tmp, m + 1)
                    for a, b, half in halves(True):
                        i = nc.vector.scalar_tensor_tensor(out=xT[:, m, a:b], in0=tmpF[:, j, a:b], scalar=ada[0][:, 16 + m, half:half + 1],
                                                           in1=xT[:, m, a:b], op0=ALU.mult, op1=ALU.add)
                        if half == 0:
                            link(i)
                    i.then_inc(r_res, 1)
                dve.wait_ge(r_res, m + 1)
            if stage == 0:
                return

            def residual(t, layer, piece, cb, with_ctx):
                s = t % 2
                dve.wait_ge(tile_done, 2 * t + 2)
                for j in range(2):
                    m = 2 * cb + j
                    for a, b, half in halves(with_ctx):
                        src = bank[3 * s + 2][:, 256 * j:256 * j + 256] if half else bank[3 * s + j]
                        i = nc.vector.scalar_tensor_tensor(out=xT[:, m, a:b], in0=src, scalar=ada[layer][:, 8 * piece + m, half:half + 1],
                                                           in1=xT[:, m, a:b], op0=ALU.mult, op1=ALU.add)
                        if with_ctx and not half:
                            link(i)
                    i.then_inc(r_res, 1)

            def ffn(layer):
                extra = CTX if layer == 0 else 0
                for g, (lo, hi) in enumerate(GROUPS):
                    for p in range(lo, hi):
                        for j in range(2):
                            t = T_OF[("in", layer, p, j)]
                            s, c = t % 2, 22 * layer + 2 * p + j
                            k = 2 * (p - lo) + j
                            dve.wait_ge(tile_done, 2 * t + 2)
                            dve.wait_ge(g_silu, c + 1)
                            m = nc.vector.tensor_tensor(hid[:, k, 0:LAT], gateS[:, c % 2, 0:LAT], bank[3 * s + 1], ALU.mult)
                            if layer == 0:
                                link(m)
                                m = nc.vector.tensor_tensor(hid[:, k, LAT:ROWS], gateS[:, c % 2, LAT:ROWS],
                                                            bank[3 * s + 2][:, 256:512], ALU.mult)
                            m.then_inc(g_hid, 1)
                        if layer == 0:
                            for b in ada1_blocks(p):
                                take_ada(1, b)
                    for cb in range(4):
                        residual(T_OF[("down", layer, lo, cb)], layer, 5, cb, layer == 0)

            modulated(1, True)
            ffn(0)
            if stage == 1:
                return

            dve.wait_ge(s_small, 16 * 8)
            multipliers(2)
            multipliers(3)
            modulated(2, True)

            def normed(i):
                with_ctx = i < 8
                gain = colA[:, ROW_KG:ROW_KG + 1] if i < 8 else colA[:, ROW_QG:ROW_QG + 1]
                t, j = T_OF[("dk", 0)] + i // 2, i % 2
                dst = kT if i < 8 else qT
                h = i % 8
                dve.wait_ge(k_rstd, i + 1)
                if i:
                    dve.wait_ge(k_rot, i)
                if with_ctx:
                    link(nc.vector.scalar_tensor_tensor(out=kT[:, h, LAT:ROWS], in0=bank[3 * (t % 2) + 2][:, 256 * j:256 * j + 256],
                                                        scalar=gain, in1=rstd[:, LAT:ROWS], op0=ALU.mult, op1=ALU.mult))
                nc.vector.scalar_tensor_tensor(out=kraw[:], in0=bank[3 * (t % 2) + j], scalar=gain,
                                               in1=rstd[:, 0:LAT], op0=ALU.mult, op1=ALU.mult).then_inc(k_norm, 1)
                dve.wait_ge(k_norm, i + 1)
                link(nc.vector.tensor_tensor(dst[:, h, 0:LAT], kraw[:], cosT, ALU.mult))
                dve.wait_ge(k_rot, i + 1)
                link(nc.vector.tensor_tensor(krot[:], krot[:], sinT, ALU.mult))
                link.wait()
                nc.vector.tensor_tensor(dst[:, h, 0:LAT], dst[:, h, 0:LAT], krot[:], ALU.add).then_inc(k_done, 1)

            for i in range(16):
                normed(i)
            for cb in range(4):
                t = T_OF[("dv", cb)]
                dve.wait_ge(tile_done, 2 * t + 2)
                for b in (0, 2):
                    m = nc.vector.tensor_copy(V[:, 2 * b:2 * b + 2, 256 * cb:256 * cb + 256],
                                              bank[3 * (t % 2) + b].rearrange("p (a n) -> p a n", a=2))
                m.then_inc(v_copyd, 1)
            for j in range(2):
                link(nc.vector.tensor_tensor_reduce(lamt[:], lamv[:, 2 * j * DH:(2 * j + 1) * DH], lamv[:, (2 * j + 1) * DH:(2 * j + 2) * DH],
                                                    1.0, 0.0, ALU.mult, ALU.add, lams[:, j:j + 1]))
                link.wait()
            nc.vector.tensor_copy(lams[:, 4:6], lams[:, 0:2]).then_inc(s_lam, 1)
            dve.wait_ge(s_lamx, 1)
            link(nc.vector.tensor_tensor(lams[:, 0:1], lams[:, 3:4], lams[:, 2:3], ALU.subtract))
            link.wait()
            link(nc.vector.tensor_scalar(lams[:, 6:7], lams[:, 0:1], -LAM_INIT, None, ALU.add))
            link(nc.vector.tensor_scalar(lamt[:, 0:1], colA[:, ROW_SUB:ROW_SUB + 1], 1.0 - LAM_INIT, None, ALU.mult))

            def combine(u):
                dve.wait_ge(a_exp, 2 * u + 2)
                m = attmx[:, u % 2]
                link(nc.vector.reciprocal(m[:, :, 3:4], m[:, :, 2:3]))
                link.wait()
                link(nc.vector.tensor_scalar(m[:, 1, 3:4], m[:, 1, 3:4], lams[:, 6:7], None, ALU.mult))
                link(nc.vector.tensor_scalar(prob[:, u % 2, 0, :], prob[:, u % 2, 0, :], m[:, 0, 3:4], None, ALU.mult))
                link.wait()
                nc.vector.scalar_tensor_tensor(out=prob[:, u % 2, 1, :], in0=prob[:, u % 2, 1, :], scalar=m[:, 1, 3:4],
                                               in1=prob[:, u % 2, 0, :], op0=ALU.mult, op1=ALU.add).then_inc(a_w, 1)

            def maxima(u):
                for c in range(2):
                    dve.wait_ge(a_s, 2 * u + c + 1)
                    m = attmx[:, u % 2, c]
                    link(nc.vector.tensor_reduce(m[:, 0:1], two[c][:, 0:ROWS], AX.X, ALU.max))
                    link.wait()
                    nc.vector.tensor_scalar(m[:, 1:2], m[:, 0:1], -DH ** -0.5, None, ALU.mult).then_inc(a_max, 1)

            maxima(0)
            for u in range(4 * HEADS):
                combine(u)
                if u + 1 < 4 * HEADS:
                    maxima(u + 1)
                h, i = u // NT, u % NT
                dve.wait_ge(a_wt, 2 * u + 2)
                dve.wait_ge(a_wtc, 2 * u + 1)
                if i == 0 and h:
                    dve.wait_ge(a_pv, h)
                nc.vector.tensor_copy(WT[:, 3:6, i * P:(i + 1) * P], bank[5][:, 0:3 * P].rearrange("p (a n) -> p a n", a=3)).then_inc(a_wtc, 1)
                if i == NT - 1:
                    dve.wait_ge(a_rs, h + 1)
                    nc.vector.scalar_tensor_tensor(out=hT[:, h, 0:LAT], in0=bank[6], scalar=lamt[:, 0:1], in1=rstd[:, 0:LAT],
                                                   op0=ALU.mult, op1=ALU.mult).then_inc(a_o, 1)
            for cb in range(4):
                residual(T_OF[("dout", cb)], 1, 2, cb, False)
            if stage == 2:
                return
            modulated(3, False)
            ffn(1)
            if stage == 3:
                return

            dve.wait_ge(n_rstd, 9)
            for kc in range(KC):
                gain = colA[:, ROW_NP + kc:ROW_NP + kc + 1]
                link(nc.vector.scalar_tensor_tensor(out=uT[:, kc, 0:LAT], in0=xT[:, kc, 0:LAT], scalar=gain, in1=rstdb[:, 0:LAT],
                                               op0=ALU.mult, op1=ALU.mult))
                nc.vector.scalar_tensor_tensor(out=uT[:, kc, LAT:ALL], in0=metaT[:, kc, :], scalar=gain, in1=rstdb[:, LAT:ALL],
                                               op0=ALU.mult, op1=ALU.mult).then_inc(h_ready, 1)
            dve.wait_ge(d_raw, 1)
            dve.wait_ge(d_zero, 2)
            link(nc.vector.tensor_tensor(dtr[:, 0:4, :], bank[6][:, 0:192].rearrange("p (a n) -> p a n", a=4),
                                    bdtf[:].unsqueeze(1).broadcast_to([P, 4, 48]), ALU.add))
            link(nc.vector.tensor_tensor(dtr[0:META, 4, :], bank[6][0:META, 192:240], bdtf[0:META, :], ALU.add))
            link.wait()
            nc.vector.scalar_tensor_tensor(out=dta, in0=dtr[:], scalar=-1.0, in1=dtr[:], op0=ALU.mult, op1=ALU.max).then_inc(d_biased, 1)
            dve.wait_ge(d_u, 1)
            nc.vector.tensor_scalar(dtw, dtu, 1.0, None, ALU.add).then_inc(d_w, 1)
            dve.wait_ge(d_w, 1)
            link(nc.vector.reciprocal(dta, dtw))
            link(nc.vector.scalar_tensor_tensor(out=dtu, in0=dtw, scalar=-1.0, in1=dtu, op0=ALU.add, op1=ALU.subtract))
            link.wait()
            link(nc.vector.scalar_tensor_tensor(out=dtu, in0=dtu, scalar=-1.0, in1=dta, op0=ALU.mult, op1=ALU.mult))
            link.wait()
            dve.wait_ge(d_ln, 1)
            link(nc.vector.tensor_tensor(dtl, dtl, dtu, ALU.add))
            link.wait()
            link(nc.vector.scalar_tensor_tensor(out=dtv[:], in0=dtr[:, :, 0:32], scalar=0.0, in1=dtl[:, :, 0:32], op0=ALU.max, op1=ALU.add))
            link(nc.vector.scalar_tensor_tensor(out=logf[:], in0=dtr[:, :, 32:48], scalar=0.0, in1=dtl[:, :, 32:48], op0=ALU.min, op1=ALU.subtract))
            link.wait()
            dve.wait_ge(d_expa, 1)
            nc.vector.scalar_tensor_tensor(out=adt[:], in0=dtv[:], scalar=-1.0, in1=expa[:].unsqueeze(1).broadcast_to([P, 5, 32]),
                                           op0=ALU.mult, op1=ALU.mult).then_inc(d_adt, 1)

            def conv(i):
                ch = 16 + i if i < 8 else i - 8
                dve.wait_ge(c_in, i + 1)
                if i >= 2:
                    dve.wait_ge(c_out, i - 1)
                if i >= 10:
                    dve.wait_ge(c_t, 4 + (i - 8) - 1)
                for k in range(4):
                    w = colC[:, 24 * k + ch:24 * k + ch + 1]
                    x = cin[:, i % 2, k:k + ALL]
                    if k == 0:
                        m = nc.vector.tensor_scalar(cacc[:, i % 2, :], x, w, None, ALU.mult)
                    else:
                        m = nc.vector.scalar_tensor_tensor(out=cacc[:, i % 2, :], in0=x, scalar=w, in1=cacc[:, i % 2, :],
                                                           op0=ALU.mult, op1=ALU.add)
                    if k < 3:
                        link(m)
                        link.wait()
                m.then_inc(c_acc, 1)

            for i in range(8):
                conv(i)
            for g in range(4):
                dve.wait_ge(c_t, g + 1)
                link(nc.vector.tensor_copy(Brow[:, 0:3, g * P:(g + 1) * P], bank[6][:, 0:384].rearrange("p (a n) -> p a n", a=3)))
                nc.vector.tensor_copy(Brow[0:META, 3, g * P:(g + 1) * P], bank[6][0:META, 384:512]).then_inc(c_tev, 1)

            def wide(x, n, k):
                return x.unsqueeze(2).broadcast_to([n, 8, k])

            def heads(x):
                return x.rearrange("p (h d) -> p h d", h=8)

            for g in range(SG):
                hs = slice(8 * g, 8 * g + 8)
                for j in range(4):
                    i = 8 + 4 * g + j
                    conv(i)
                    if j % 2:
                        for jj in (j - 1, j):
                            dve.wait_ge(c_t, 4 + 4 * g + jj + 1)
                            nc.vector.tensor_copy(xrow[:, 0:4, P * jj:P * jj + P], bank[6].rearrange("p (a n) -> p a n", a=4)).then_inc(c_tev, 1)
                dve.wait_ge(e_st, 4 * g + 1)
                if g:
                    dve.wait_ge(e_yoff, 4 * g)
                nc.vector.tensor_copy(Hst[:, 0, :], bank[5]).then_inc(e_h, 1)
                for i in range(NT):
                    n = 4 * g + i
                    dve.wait_ge(e_cb, n + 1)
                    link(nc.vector.tensor_tensor(CBm[:], bank[2][:, 0:P], upper, ALU.mult))
                    link.wait()
                    dve.wait_ge(e_exp, n + 1)
                    nc.vector.tensor_tensor(Mt[:], Mt[:], CBm[:].unsqueeze(1).broadcast_to([P, 8, P]), ALU.mult).then_inc(e_m, 1)
                    if i < 3:
                        if n >= 2:
                            dve.wait_ge(e_yoff, n)
                        dve.wait_ge(e_h, n + 1)
                        c = 224 + 32 * i + 8 * g
                        link(nc.vector.tensor_tensor(heads(Hst[:, (i + 1) % 2, :]), heads(Hst[:, i % 2, :]), wide(dec[:, c:c + 8], P, 64), ALU.mult))
                        link.wait()
                        dve.wait_ge(e_st, n + 2)
                        nc.vector.tensor_tensor(Hst[:, (i + 1) % 2, :], Hst[:, (i + 1) % 2, :], bank[5], ALU.add).then_inc(e_h, 1)
                    c = 32 * i + 8 * g
                    dve.wait_ge(e_yoff, n + 1)
                    if n:
                        dve.wait_ge(e_t, n)
                    link(nc.vector.tensor_tensor(heads(yrow[:]), heads(bank[4]), wide(dec[:, c:c + 8], P, 64), ALU.mult))
                    link.wait()
                    dve.wait_ge(p_xd, n + 1)
                    link(nc.vector.tensor_tensor(yrow[:], yrow[:], xd[:], ALU.add))
                    link.wait()
                    dve.wait_ge(e_y, n + 1)
                    link(nc.vector.tensor_tensor(yrow[:], yrow[:], bank[3], ALU.add))
                    link.wait()
                    dve.wait_ge(z_act, 2 * g + 2)
                    nc.vector.tensor_tensor(yrow[:], yrow[:], zrow[:, i, :], ALU.mult).then_inc(e_gated, 1)
                    dve.wait_ge(e_gated, n + 1)
                    nc.vector.tensor_tensor_reduce(ysq, yrow[:], yrow[:], 1.0, 0.0, ALU.mult, ALU.add, stt4[:, 0:1]).then_inc(e_ss, 1)
                    dve.wait_ge(e_rs, n + 1)
                    nc.vector.tensor_scalar(yrow[:], yrow[:], stt4[:, 2:3], None, ALU.mult).then_inc(e_un, 1)
                    dve.wait_ge(e_t, n + 1)
                    c = ROW_SN + 4 * g
                    nc.vector.tensor_tensor(ysT[:, 4 * g:4 * g + 4, i * P:(i + 1) * P], bank[6].rearrange("p (a n) -> p a n", a=4),
                                            colA[:, c:c + 4].unsqueeze(2).broadcast_to([P, 4, P]), ALU.mult).then_inc(e_tev, 1)

            for f in range(4):
                for kind in "qk":
                    t = T_OF[(kind, f)]
                    dst = qA if kind == "q" else kA
                    o = 0 if kind == "q" else META
                    dve.wait_ge(tile_done, 2 * t + 2)
                    if f:
                        dve.wait_ge(b_s, 16 * f)
                    link(nc.vector.tensor_copy(dst[0:DH, 2, o:o + LAT], bank[3 * (t % 2) + 1][0:DH, :]))
                    m = nc.vector.tensor_copy(dst[0:DH, 3, o:o + LAT], bank[3 * (t % 2) + 1][DH:P, :])
                    if kind == "k":
                        link(m)
                        for j in range(4):
                            r = DH * (j % 2)
                            m = nc.vector.tensor_copy(kA[0:DH, j, 0:META],
                                                      bank[3 * (t % 2) + 2][r:r + DH, 256 * (j // 2):256 * (j // 2) + META])
                            if j < 3:
                                link(m)
                    m.then_inc(x_dve, 1)
                t = T_OF[("v", f)]
                dve.wait_ge(tile_done, 2 * t + 2)
                if f:
                    dve.wait_ge(b_o, 16 * f)
                link(nc.vector.tensor_copy(vA[:, 2:4, :], bank[3 * (t % 2) + 1].rearrange("p (a n) -> p a n", a=2)))
                nc.vector.tensor_copy(vA[0:META, 4, :], bank[3 * (t % 2) + 2][0:META, 0:256]).then_inc(x_dve, 1)

                def fox_max(u):
                    i = u // 4 % 4
                    dve.wait_ge(b_s, u + 1)
                    link(nc.vector.tensor_reduce(amx[:, u % 2, 0:1], two[u % 2][:, 0:META + (i + 1) * P], AX.X, ALU.max))
                    link.wait()
                    if u >= 2:
                        dve.wait_ge(b_exp, u - 1)
                    nc.vector.tensor_scalar(amx[:, u % 2, 1:2], amx[:, u % 2, 0:1], -DH ** -0.5, None, ALU.mult).then_inc(b_max, 1)

                fox_max(16 * f)
                for u in range(16 * f, 16 * f + 16):
                    i, h = u // 4 % 4, u % 4
                    if u + 1 < 16 * f + 16:
                        fox_max(u + 1)
                    dve.wait_ge(b_pt, u + 1)
                    if u >= 2:
                        dve.wait_ge(b_o, u - 1)
                    nc.vector.tensor_copy(PT[0:META, u % 2, 4 * P:5 * P], bank[5][0:META, 0:P]).then_inc(b_ptd, 1)
                    if h == 3:
                        v = u // 4
                        dve.wait_ge(b_exp, u + 1)
                        link(nc.vector.reciprocal(asum[:, i, :], asum[:, i, :]))
                        link.wait()
                        dve.wait_ge(b_o, u + 1)
                        if v:
                            dve.wait_ge(b_yt, v)
                        link(nc.vector.tensor_tensor(yA[:].rearrange("p (h d) -> p h d", h=4), bank[7][:, 0:256].rearrange("p (h d) -> p h d", h=4),
                                                asum[:, i, :].unsqueeze(2).broadcast_to([P, 4, 64]), ALU.mult))
                        link.wait()
                        dve.wait_ge(z_act, 2 * SG + f + 1)
                        nc.vector.tensor_tensor(yA[:], yA[:], zA[:, i, :], ALU.mult).then_inc(b_y, 1)
                        dve.wait_ge(b_yt, v + 1)
                        nc.vector.tensor_copy(yaT[:, 2 * f:2 * f + 2, i * P:(i + 1) * P], bank[6][:, 0:256].rearrange("p (a n) -> p a n", a=2)) \
                            .then_inc(b_ytev, 1)

            for cb in range(4):
                for k, (kind, gate) in enumerate((("ps", gsb), ("pa", gab))):
                    t = T_OF[(kind, cb)]
                    dve.wait_ge(m_gate, 2 * cb + k + 1)
                    for j in range(2):
                        dve.wait_ge(tile_done, 2 * t + 1 + j)
                        if k == 0:
                            m = nc.vector.tensor_tensor(mg[:, 2 * cb + j, :], gate[:, j, :], bank[3 * (t % 2) + j], ALU.mult)
                        else:
                            link(nc.vector.tensor_tensor(gate[:, j, :], gate[:, j, :], bank[3 * (t % 2) + j], ALU.mult))
                            link.wait()
                            dve.wait_ge(m_mix, 2 * cb + 1)
                            m = nc.vector.tensor_tensor(mg[:, 2 * cb + j, :], mg[:, 2 * cb + j, :], gate[:, j, :], ALU.add)
                        if j == 0:
                            link(m)
                    m.then_inc(m_mix, 1)
            dve.wait_ge(o_act, 4)
            junk = mg[:].rearrange("p a n -> p (a n)")
            dve.wait_ge(tile_done, 2 * T_OF[("wo", 3)] + 2)
            for i in range(NT):
                nc.vector.tensor_tensor_reduce(junk[:, D * i:D * i + D], orow[:, i, :], orow[:, i, :], 1.0, 0.0, ALU.mult, ALU.add, stt4[:, i:i + 1]) \
                    .then_inc(o_ss, 1)
            dve.wait_ge(o_rs, 1)
            for i in range(NT):
                link(nc.vector.scalar_tensor_tensor(out=orow[:, i, :], in0=orow[:, i, :], scalar=stt4[:, 4 + i:5 + i], in1=gpost[:],
                                               op0=ALU.mult, op1=ALU.mult))
                link.wait()
                for j in range(2):
                    dve.wait_ge(o_xt, 2 * i + j + 1)
                    nc.vector.tensor_tensor(orow[:, i, 512 * j:512 * j + 512], orow[:, i, 512 * j:512 * j + 512], bank[6 + j], ALU.add) \
                        .then_inc(o_fin, 1)

        @block.gpsimd
        def _(pool):
            if stage < 4:
                return
            pool.wait_ge(r_res, 64)
            nc.gpsimd.memset(cin[:, :, 0:3], 0.0).then_inc(d_zero, 1)
            nc.gpsimd.memset(dtr[:], 0.0).then_inc(d_zero, 1)

            def wide(x, n, k):
                return x.unsqueeze(2).broadcast_to([n, 8, k])

            def heads(x):
                return x.rearrange("p (h d) -> p h d", h=8)

            pool.wait_ge(d_dec, 1)
            for g in range(SG):
                hs = slice(8 * g, 8 * g + 8)

                def decays(i):
                    n = 4 * g + i
                    if n:
                        pool.wait_ge(e_seg, n)
                    else:
                        pool.wait_ge(d_adt, 1)
                    nc.gpsimd.tensor_tensor(lseg[:, 0:8 * P].rearrange("p (h s) -> p h s", h=8), wide(adt[:, i, hs], P, P),
                                            lower.unsqueeze(1).broadcast_to([P, 8, P]), ALU.mult).then_inc(p_lseg, 1)

                decays(0)
                pool.wait_ge(c_tev, 4 + 8 * g + 8)
                if g:
                    pool.wait_ge(e_st, 4 * g)
                    pool.wait_ge(e_y, 4 * g)
                nc.gpsimd.tensor_tensor(heads(xdt[0:META, 0, :]), heads(xrow[0:META, 4, :]), wide(dtv[0:META, 4, hs], META, 64), ALU.mult) \
                    .then_inc(p_xdt, 1)
                pool.wait_ge(p_xdt, 5 * g + 1)
                nc.gpsimd.tensor_tensor(heads(xds[0:META, :]), heads(xdt[0:META, 0, :]), wide(dec[0:META, 320 + 8 * g:328 + 8 * g], META, 64), ALU.mult) \
                    .then_inc(p_xds, 1)
                for i in range(NT):
                    n = 4 * g + i
                    if i >= 2:
                        pool.wait_ge(e_y, n - 1)
                    if i == 1:
                        pool.wait_ge(p_xds, n)
                    nc.gpsimd.tensor_tensor(heads(xdt[:, (i + 1) % 2, :]), heads(xrow[:, i, :]), wide(dtv[:, i, hs], P, 64), ALU.mult) \
                        .then_inc(p_xdt, 1)
                    if i < 3:
                        pool.wait_ge(p_xdt, 5 * g + i + 2)
                        pool.wait_ge(e_st, n + 1)
                        c = 128 + 32 * i + 8 * g
                        nc.gpsimd.tensor_tensor(heads(xds[:]), heads(xdt[:, (i + 1) % 2, :]), wide(dec[:, c:c + 8], P, 64), ALU.mult) \
                            .then_inc(p_xds, 1)
                    if n:
                        pool.wait_ge(e_gated, n)
                    nc.gpsimd.tensor_tensor(heads(xd[:]), heads(xrow[:, i, :]), wide(dskip[:, hs], P, 64), ALU.mult).then_inc(p_xd, 1)
                    if i + 1 < NT:
                        decays(i + 1)
            pool.wait_ge(e_tev, 16)
            nc.gpsimd.memset(qA[DH:DH + 2, :, :], 1.0).then_inc(b_one, 1)
            nc.gpsimd.memset(kA[DH:DH + 2, :, :], 1.0).then_inc(b_one, 1)
            pool.wait_ge(b_one, 2)
            for f in range(4):
                if f:
                    pool.wait_ge(b_s, 16 * f)
                pool.dma_start(kA[DH:DH + 1, :, :], ckT[4 * f:4 * f + 4, :]).then_inc(b_k, 16)
                pool.dma_start(qA[DH + 1:DH + 2, :, :], cqT[4 * f:4 * f + 4, :]).then_inc(b_q, 16)


INPUTS = ['x', 'c', 'ctx', 'c_ctx', 'w_ada', 'b_ada', 'norm_gain', 'ffn_w_in', 'ffn_w_out', 'fnet_w_out', 'fnet_b_out',
          'diff_w_in', 'diff_q_gain', 'diff_k_gain', 'diff_lambda', 'diff_subln_gain', 'diff_w_out',
          'meta_tokens_2', 'norm_pre_2', 'w_in_2', 'conv_w_2', 'conv_b_2', 'dt_bias_2', 'a_log_2', 'd_skip_2',
          'ssd_norm_2', 'fgate_bias_2', 'gate_bias_2', 'w_proj_ssd_2', 'w_proj_att_2', 'w_out_2', 'norm_post_2']
STAGE = 99


def kernel(**inputs):
    import concourse.bacc as bacc
    from concourse.bass_utils import run_bass_kernel_spmd

    nc = bacc.Bacc("TRN2", target_bir_lowering=False, num_devices=1)
    arrays, io = {}, {}
    for name in INPUTS:
        a = np.ascontiguousarray(inputs[name])
        arrays[f"in_{name}"] = a
        io[name] = nc.dram_tensor(f"in_{name}", a.shape, F32, kind="ExternalInput").ap()
    tables = []
    for name, a in zip(("table", "dft_lat", "dft_ctx"), constants()):
        arrays[name] = a
        tables.append(nc.dram_tensor(name, a.shape, F32, kind="ExternalInput").ap())
    out = nc.dram_tensor("out_0", (1, LAT, D), F32, kind="ExternalOutput").ap()
    dump = nc.dram_tensor("dump", (P, KC * ROWS), F32, kind="ExternalOutput").ap() if STAGE < 99 else None
    bass_two_blocks_kernel(nc, io, *tables, out, dump, STAGE)
    result = run_bass_kernel_spmd(nc, [arrays], core_ids=[0])
    return result.results[0]["out_0"]
```

```python
from contextlib import ExitStack

import numpy as np
import concourse.bass as bass
from concourse import mybir

F32 = mybir.dt.float32
F32R = mybir.dt.float32r
ALU = mybir.AluOpType
ACT = mybir.ActivationFunctionType
AX = mybir.AxisListType

P = 128
D = 1024
KC = D // P
LAT, CTX, META = 512, 256, 16
NT = LAT // P
ROWS = LAT + CTX
F = 2816
FC = F // P
GROUPS = [(0, 8), (8, 16), (16, FC)]
HEADS = 8
DH = 64
EPS = 1e-6
LAM_INIT = 0.8 - 0.6 * float(np.exp(-0.3))
SG = 4
COL_Z, COL_X, COL_B, COL_C, COL_DT = 0, 2048, 4096, 4608, 5120
COL_ZA, COL_Q, COL_K, COL_V, COL_F, COL_G = 5152, 6176, 7200, 8224, 9248, 9264
NR = 2
NS = 2
NEG = -1e30
SPLIT_KINDS = ("fnet", "in", "down", "dk", "dq", "dv", "dout")

ROW_C, ROW_CC, ROW_NG, ROW_FB, ROW_NP, ROW_SN, ROW_GB, ROW_SUB, ROW_QG, ROW_KG, N_A = 0, 8, 16, 48, 56, 64, 80, 96, 97, 98, 99
ROW_ADA, ROW_CB, N_B = 0, 96, 120
N_C = 96
(K_ID, K_ONE, K_BLK, K_UP, K_LOW, K_NEG, K_DFT, K_COS, K_SIN, N_K) = (0, 128, 256, 384, 512, 640, 768, 1024, 1536, 2048)


def constants():
    i = np.arange(P)
    k = np.zeros((P, N_K), np.float32)
    k[:, K_ID:K_ID + P] = np.eye(P)
    k[:, K_ONE:K_ONE + P] = 1.0
    k[:, K_BLK:K_BLK + P] = (i[:, None] // DH == i[None, :] // DH)
    k[:, K_UP:K_UP + P] = i[:, None] <= i[None, :]
    k[:, K_LOW:K_LOW + P] = i[:, None] > i[None, :]
    k[:, K_NEG:K_NEG + P] = np.where(i[None, :] > i[:, None], NEG, 0.0)
    a = 2 * np.pi * (np.outer(i, i) % P) / P
    k[:, K_DFT:K_DFT + P] = np.cos(a)
    k[:, K_DFT + P:K_DFT + 2 * P] = np.sin(a)
    row = np.repeat(np.arange(LAT // 64, dtype=np.float32), 64)
    col = np.tile(np.arange(64, dtype=np.float32), LAT // 64)
    nf = DH // 4
    inv = (np.float32(10000.0) ** (-np.arange(nf, dtype=np.float32) / np.float32(nf))).astype(np.float32)
    ang = np.concatenate([row[:, None] * inv, col[:, None] * inv], axis=-1).astype(np.float32).astype(np.float64).T
    k[:, K_COS:K_COS + LAT] = np.tile(np.cos(ang), (4, 1))
    k[:, K_SIN:K_SIN + LAT] = np.tile(np.concatenate([-np.sin(ang), np.sin(ang)]), (2, 1))

    def dft(n):
        j = np.arange(n)
        a = 2 * np.pi * (np.outer(j, j) % n) / n
        t = np.stack([np.cos(a), -np.sin(a)], axis=1) / np.sqrt(n * P)
        return np.ascontiguousarray(t.reshape(n // P, P, 2 * n).transpose(1, 0, 2).reshape(P, -1), np.float32)

    return k, dft(LAT), dft(CTX)


def stream_plan():
    plan = [("ada", 0, b) for b in range(8)]
    for g in range(KC):
        plan += [("ada", 0, 8 + 2 * g), ("ada", 0, 9 + 2 * g)]
    plan += [("fnet", cb) for cb in range(4)]
    for layer in range(2):
        for lo, hi in GROUPS:
            for c in range(lo, hi):
                plan += [("in", layer, c)] + ([("ada", 1, c)] if layer == 0 else [])
            for cb in range(4):
                plan += [("down", layer, lo, cb)] + ([("ada", 1, FC + cb)] if (layer, hi) == (0, FC) and cb < 2 else [])
        if layer == 0:
            plan += [(w, cb) for w in ("dk", "dq", "dv") for cb in range(4)]
            plan += [("dout", cb) for cb in range(4)]
    plan += [("B", j) for j in range(2)] + [("C", j) for j in range(2)]
    for g in range(SG):
        plan += [("z", g, j) for j in range(2)] + [("xs", g, j) for j in range(2)]
    for f in range(4):
        plan += [("q", f), ("k", f), ("v", f), ("za", f)]
    for cb in range(4):
        plan += [("gs", cb), ("ga", cb), ("ps", cb, 0), ("ps", cb, 1), ("pa", cb)]
    plan += [("wo", cb) for cb in range(4)]
    return plan


def step_plan():
    steps = [(("fnet", cb), [("fnet", cb)]) for cb in range(4)]
    for layer in range(2):
        for lo, hi in GROUPS:
            steps += [(("in", layer, c), [("in", layer, c)]) for c in range(lo, hi)]
            steps += [(("down", layer, lo, cb), [("down", layer, lo, cb)]) for cb in range(4)]
        if layer == 0:
            steps += [((w, cb), [(w, cb)]) for w in ("dk", "dq", "dv") for cb in range(4)]
            steps += [(("dout", cb), [("dout", cb)]) for cb in range(4)]
    steps += [((w, j), [(w, j)]) for w in ("B", "C") for j in range(2)]
    for g in range(SG):
        steps += [((w, g, j), [(w, g, j)]) for w in ("z", "xs") for j in range(2)]
    for f in range(4):
        steps += [((w, f), [(w, f)]) for w in ("q", "k", "v", "za")]
    for cb in range(4):
        steps += [(("gs", cb), [("gs", cb)]), (("ga", cb), [("ga", cb)]),
                  (("ps", cb), [("ps", cb, 0), ("ps", cb, 1)]), (("pa", cb), [("pa", cb)])]
    steps += [(("wo", cb), [("wo", cb)]) for cb in range(4)]
    return steps


def bass_two_blocks_kernel(nc, io, kt_d, dl_d, dc_d, out, dump=None, stage=99):
    PLAN = stream_plan()
    N_OF = {key: n for n, key in enumerate(PLAN)}
    STEPS = step_plan()
    T_OF = {key: t for t, (key, _) in enumerate(STEPS)}
    SPLIT = [key for key in PLAN if key[0] in SPLIT_KINDS]
    S_OF = {key: n for n, key in enumerate(SPLIT)}
    w_ada, w_in2 = io["w_ada"], io["w_in_2"][0]

    def source(key):
        kind = key[0]
        if kind == "ada":
            return w_ada[key[1]], 0, KC, 256 * key[2]
        if kind == "fnet":
            return io["fnet_w_out"][0], 0, KC, 256 * key[1]
        if kind == "down":
            _, layer, lo, cb = key
            return io["ffn_w_out"][layer], P * lo, dict(GROUPS)[lo] - lo, 256 * cb
        if kind in ("dq", "dk", "dv"):
            return io["diff_w_in"][0], 0, KC, {"dq": 0, "dk": D, "dv": 2 * D}[kind] + 256 * key[1]
        if kind == "dout":
            return io["diff_w_out"][0], 0, KC, 256 * key[1]
        if kind in ("B", "C"):
            return w_in2, 0, KC, {"B": COL_B, "C": COL_C}[kind] + 256 * key[1]
        if kind in ("xs", "z"):
            return w_in2, 0, KC, {"xs": COL_X, "z": COL_Z}[kind] + 512 * key[1] + 256 * key[2]
        if kind in ("q", "k", "v", "za"):
            return w_in2, 0, KC, {"q": COL_Q, "k": COL_K, "v": COL_V, "za": COL_ZA}[kind] + 256 * key[1]
        if kind in ("gs", "ga"):
            return w_in2, 0, KC, COL_G + (D if kind == "ga" else 0) + 256 * key[1]
        if kind == "ps":
            return io["w_proj_ssd_2"][0], D * key[2], KC, 256 * key[1]
        if kind == "pa":
            return io["w_proj_att_2"][0], 0, KC, 256 * key[1]
        return io["w_out_2"][0], 0, KC, 256 * key[1]

    with ExitStack() as ctx:
        here = [ctx]

        def sb(name, shape, dt=F32):
            return here[-1].enter_context(nc.sbuf_tensor(name, shape, dt))

        def sem(name):
            return ctx.enter_context(nc.semaphore(name))

        bank = [ctx.enter_context(nc.psum_tensor(f"bank{i}", [P, 512], F32)) for i in range(4, 8)]
        two = [ctx.enter_context(nc.psum_tensor(f"two{i}", [P, 1024], F32)) for i in range(2)]
        bank = [two[0][:, 0:512], two[0][:, 512:1024], two[1][:, 0:512], two[1][:, 512:1024]] + [b[:, :] for b in bank]

        kt = sb("kt", [P, N_K])
        ident, ones, blk = kt[:, K_ID:K_ID + P], kt[:, K_ONE:K_ONE + P], kt[:, K_BLK:K_BLK + P]
        upper, lower, negm = kt[:, K_UP:K_UP + P], kt[:, K_LOW:K_LOW + P], kt[:, K_NEG:K_NEG + P]
        dft128, cosT, sinT = kt[:, K_DFT:K_DFT + 2 * P], kt[:, K_COS:K_COS + LAT], kt[:, K_SIN:K_SIN + LAT]
        colA, colB, colC = sb("colA", [P, N_A]), sb("colB", [P, N_B]), sb("colC", [P, N_C])
        cond = sb("cond", [P, KC, 2])
        ada = [sb(f"ada{i}", [P, 48, 2]) for i in range(2)]
        mult = sb("mult", [P, 4, KC, 2])
        gbias = sb("gbias", [P, KC, 2])
        epsc = sb("epsc", [P, 1])
        xT = sb("xT", [P, KC, ROWS])
        metaT = sb("metaT", [P, KC, META])
        wdtf = sb("wdtf", [P, KC, 48])
        bdtf = sb("bdtf", [P, 48])
        alog = sb("alog", [P, 32])
        dskip = sb("dskip", [P, 32])
        lamv = sb("lamv", [P, 4 * DH])
        lamt = sb("lamt", [P, DH])
        lams = sb("lams", [P, 8])
        gpost = sb("gpost", [P, D])
        ring = sb("ring", [P, NR, KC, 256])

        def apart(name, shape):
            return sb(name + "H", shape, F32R), sb(name + "L", shape, F32R)

        def phase():
            s = ExitStack()
            here.append(s)
            return s

        def leave():
            here.pop().close()

        phase()
        wH, wL = apart("w", [P, NS, KC, 256])
        phase()
        sq0, rstd0 = sb("sq0", [P, 2, ROWS]), sb("rstd0", [P, ROWS])
        hT = sb("hT", [P, KC, ROWS])
        phase()
        xraw = sb("xraw", [P, 6, D])
        mraw = sb("mraw", [META, D])
        rowA, rowB, rowC = sb("rowA", [N_A, P]), sb("rowB", [N_B, P]), sb("rowC", [N_C, P])
        leave()
        yT = apart("yT", [P, KC, ROWS])
        dftL = sb("dftL", [P, NT, 2, LAT])
        dftC = sb("dftC", [P, 2, 2, CTX])
        fa = sb("fa", [P, 6, 256])
        gb = sb("gb", [P, KC, 2])
        leave()
        phase()
        sq1, rstd1 = sb("sq1", [P, 2, ROWS]), sb("rstd1", [P, ROWS])
        h1 = apart("h1", [P, KC, ROWS])
        hid = apart("hid", [P, 8, ROWS])
        gateS = sb("gateS", [P, 2, ROWS])
        leave()
        phase()
        kT = sb("kT", [P, HEADS, ROWS])
        qT = sb("qT", [P, HEADS, LAT])
        phase()
        sq2, rstd2 = sb("sq2", [P, 2, ROWS]), sb("rstd2", [P, ROWS])
        krot = sb("krot", [P, LAT])
        kraw = sb("kraw", [P, LAT])
        htmp = sb("htmp", [P, 2, ROWS])
        leave()
        V = sb("V", [P, 6, D])
        phase()
        h2 = apart("h2", [P, KC, ROWS])
        leave()
        prob = sb("prob", [P, 2, 2, ROWS])
        WT = sb("WT", [P, 6, LAT])
        sq3, rstd3 = sb("sq3", [P, 2, LAT]), sb("rstd3", [P, LAT])
        attmx = sb("attmx", [P, 2, 2, 4])
        aoL = sb("aoL", [P, HEADS, LAT], F32R)
        leave()
        phase()
        under_q = sb("under_q", [P, HEADS, ROWS])
        aoH = sb("aoH", [P, HEADS, LAT], F32R)
        leave()
        ao = (aoH, aoL)
        leave()
        here.append(ctx)
        phase()
        ALL = LAT + META
        uT = sb("uT", [P, KC, ALL])
        ysT = sb("ysT", [P, 2 * KC, LAT])
        dtr = sb("dtr", [P, 5, 48])
        dtt = sb("dtt", [P, 4 * 240])
        dta, dtu, dtw, dtl = (dtt[:, 240 * k:240 * k + 240].rearrange("p (a n) -> p a n", a=5) for k in range(4))
        ysq = dtt[:, 0:512]
        dtv = sb("dtv", [P, 5, 32])
        logf = sb("logf", [P, 5, 16])
        expa = sb("expa", [P, 32])
        adt = sb("adt", [P, 5, 32])
        dec = sb("dec", [P, 352])
        ckT, cqT = sb("ckT", [16, ALL]), sb("cqT", [16, LAT])
        stt4 = sb("stt4", [P, 8])
        phase()
        Brow = sb("Brow", [P, 4, 4 * P])
        BT = sb("BT", [P, 4, ALL])
        CTt = sb("CTt", [P, 4, LAT])
        cin = sb("cin", [P, 2, ALL + 3])
        cacc = sb("cacc", [P, 2, ALL])
        xrow = sb("xrow", [P, 5, 512])
        xdt, xds = sb("xdt", [P, 2, 512]), sb("xds", [P, 512])
        xd = sb("xd", [P, 512])
        lseg = sb("lseg", [P, 1056])
        sqb = lseg[:].rearrange("p (a n) -> p a n", a=2)
        Mt = sb("Mt", [P, 2, 8, P])
        rstdb = Mt[:].rearrange("p b a n -> p (b a n)")[:, 0:ALL]
        CBm = sb("CBm", [P, P])
        Hst = sb("Hst", [P, 2, 512])
        yrow = sb("yrow", [P, 2, 512])
        zrow = sb("zrow", [P, 4, 512])
        leave()
        phase()
        yaT = sb("yaT", [P, KC, LAT])
        phase()
        qA = sb("qA", [P, 4, LAT])
        kA = sb("kA", [P, 4, ALL])
        vA = sb("vA", [P, 5, 256])
        zA = sb("zA", [P, 4, 256])
        probA = sb("probA", [P, 2, ALL])
        PT = sb("PT", [P, 2, 5 * P])
        amx = sb("amx", [P, 2, 4])
        asum = sb("asum", [P, 4, 4])
        yA = sb("yA", [P, 256])
        leave()
        phase()
        mg = sb("mg", [P, KC, LAT])
        gsb, gab = sb("gsb", [P, 2, LAT]), sb("gab", [P, 2, LAT])
        orow = sb("orow", [P, 4, D])
        leave()
        leave()
        leave()

        s_load, s_tab, s_x = sem("s_load"), sem("s_tab"), sem("s_x")
        s_x2, s_dft, s_small = sem("s_x2"), sem("s_dft"), sem("s_small")
        ring_ready = [sem(f"ring_ready{i}") for i in range(NR)]
        s_cols_t, s_cols = sem("s_cols_t"), sem("s_cols")
        s_cond, s_xt, s_xlat, s_xctx, s_meta_t, s_meta = sem("s_cond"), sem("s_xt"), sem("s_xlat"), sem("s_xctx"), sem("s_meta_t"), sem("s_meta")
        ada_done, ada_taken, s_mult = sem("ada_done"), sem("ada_taken"), sem("s_mult")
        n_sq, n_used, n_sum, n_ln, n_rstd, h_ready = sem("n_sq"), sem("n_used"), sem("n_sum"), sem("n_ln"), sem("n_rstd"), sem("h_ready")
        tile_done = sem("tile_done")
        f_a, f_acopy, f_y, f_ycopy = sem("f_a"), sem("f_acopy"), sem("f_y"), sem("f_ycopy")
        r_tmp, r_res = sem("r_tmp"), sem("r_res")
        g_silu, g_hid = sem("g_silu"), sem("g_hid")
        v_chain, a_chain = sem("v_chain"), sem("a_chain")
        s_dump = sem("s_dump")
        w_hi, w_lo = sem("w_hi"), sem("w_lo")
        h_full, h_hi, g_full, g_hi = sem("h_full"), sem("h_hi"), sem("g_full"), sem("g_hi")
        f_ylo, a_of, a_ohi = sem("f_ylo"), sem("a_of"), sem("a_ohi")
        a_wtd = sem("a_wtd")
        k_sq, k_sum, k_rstd, k_norm, k_rot, k_done = sem("k_sq"), sem("k_sum"), sem("k_rstd"), sem("k_norm"), sem("k_rot"), sem("k_done")
        v_copy, v_copyd, s_lam, s_lamx = sem("v_copy"), sem("v_copyd"), sem("s_lam"), sem("s_lamx")
        a_s, a_max, a_exp, a_w, a_wt, a_wtc, a_pv, a_sq, a_ms, a_rs, a_o = (sem(x) for x in (
            "a_s", "a_max", "a_exp", "a_w", "a_wt", "a_wtc", "a_pv", "a_sq", "a_ms", "a_rs", "a_o"))

        (c_in, c_acc, c_out, c_t, c_tev, z_act, x_act, x_dve, m_gate, m_mix, o_act) = (sem(x) for x in (
            "c_in", "c_acc", "c_out", "c_t", "c_tev", "z_act", "x_act", "x_dve", "m_gate", "m_mix", "o_act"))
        (d_zero, d_raw, d_biased, d_u, d_w, d_ln, d_expa, d_adt, d_sums, d_dec, d_ct, d_cta) = (sem(x) for x in (
            "d_zero", "d_raw", "d_biased", "d_u", "d_w", "d_ln", "d_expa", "d_adt", "d_sums", "d_dec", "d_ct", "d_cta"))
        (p_lseg, p_xdt, p_xds, p_xd, e_seg, e_exp, e_cb, e_cbm, e_m, e_y, e_yoff, e_st, e_h, e_gated, e_ss, e_rs, e_un, e_t, e_tev) = (sem(x) for x in (
            "p_lseg", "p_xdt", "p_xds", "p_xd", "e_seg", "e_exp", "e_cb", "e_cbm", "e_m", "e_y", "e_yoff", "e_st", "e_h",
            "e_gated", "e_ss", "e_rs", "e_un", "e_t", "e_tev"))
        (b_one, b_k, b_q, b_s, b_max, b_exp, b_pt, b_pta, b_ptd, b_o, b_y, b_yt, b_ytev) = (sem(x) for x in (
            "b_one", "b_k", "b_q", "b_s", "b_max", "b_exp", "b_pt", "b_pta", "b_ptd", "b_o", "b_y", "b_yt", "b_ytev"))
        (o_ss, o_rs, o_xt, o_fin, s_out) = (sem(x) for x in ("o_ss", "o_rs", "o_xt", "o_fin", "s_out"))

        block = ctx.enter_context(nc.Block())

        class Chain:

            def __init__(self, eng, s):
                self.eng, self.s, self.n = eng, s, 0

            def __call__(self, ins):
                self.n += 1
                ins.then_inc(self.s, 1)

            def wait(self):
                self.eng.wait_ge(self.s, self.n)

        def blocks_used(key):
            if key[0] == "ada":
                return ada_done, 24 * key[1] + key[2] + 1
            if key in S_OF:
                return w_lo, S_OF[key] + 1
            for t, (_, ends) in enumerate(STEPS):
                if key in ends:
                    return tile_done, 2 * t + 2
            raise KeyError(key)

        def banks_read(t):
            key = STEPS[t][0]
            kind = key[0]
            if kind == "fnet":
                return [(r_res, 2 * key[1] + 2)]
            if kind == "in":
                return [(g_full, FC * key[1] + key[2] + 1)]
            if kind == "down":
                _, layer, lo, cb = key
                return [(r_res, (8, 40)[layer] + 8 * [a for a, _ in GROUPS].index(lo) + 2 * cb + 2)]
            if kind == "dout":
                return [(r_res, 32 + 2 * key[1] + 2)]
            if kind in ("dk", "dq"):
                return [(k_norm, (8 if kind == "dq" else 0) + 2 * key[1] + 2)]
            if kind == "dv":
                return [(v_copy, key[1] + 1), (v_copyd, key[1] + 1)]
            if kind in ("B", "C", "xs"):
                return [(c_in, conv_tile(kind, key, 1) + 1)]
            if kind == "z":
                return [(z_act, 2 * key[1] + key[2] + 1)]
            if kind in ("q", "k", "v"):
                i = 3 * key[1] + "qkv".index(kind) + 1
                return [(x_act, i), (x_dve, i)]
            if kind == "za":
                return [(z_act, 2 * SG + key[1] + 1)]
            if kind in ("gs", "ga"):
                return [(m_gate, 2 * key[1] + (kind == "ga") + 1)]
            if kind in ("ps", "pa"):
                return [(m_mix, 2 * key[1] + (kind == "pa") + 1)]
            if kind == "wo":
                return [(o_act, key[1] + 1)]
            raise KeyError(key)

        def conv_tile(kind, key, j):
            return {"B": 2 * key[1], "C": 4 + 2 * key[1], "xs": 8 + 4 * key[1] + (2 * key[2] if len(key) > 2 else 0)}[kind] + j

        def halves(with_ctx):
            return [(0, LAT, 0), (LAT, ROWS, 1)] if with_ctx else [(0, LAT, 0)]

        NORM_SQ = {0: 0, 1: KC, 2: 2 * KC, 3: 3 * KC, 4: 4 * KC}
        last_stage = stage

        def arrived(n):
            return sum(32 if PLAN[m][0] == "in" else 16 for m in range(n % NR, n + 1, NR))

        def split_block(n):
            key = SPLIT[n]
            kc = source(key)[2] if key[0] != "in" else KC
            r = N_OF[key] % NR
            return ring[:, r, 0:kc], wH[:, n % NS, 0:kc], wL[:, n % NS, 0:kc]

        @block.sync
        def _(sp):
            sp.dma_start(kt[:], kt_d).then_inc(s_load, 16)
            for i in range(4):
                sp.dma_start(xraw[:, i, :], io["x"][0, i * P:(i + 1) * P, :]).then_inc(s_x, 16)

            def stream(n):
                key = PLAN[n]
                if n >= NR:
                    s, v = blocks_used(PLAN[n - NR])
                    sp.wait_ge(s, v)
                if key[0] == "in":
                    w = io["ffn_w_in"][key[1]].rearrange("(c p) (h n) -> p c h n", p=P, h=2)
                    for h in range(2):
                        sp.dma_start(ring[:, n % NR, :, P * h:P * h + P], w[:, :, h, P * key[2]:P * key[2] + P]) \
                            .then_inc(ring_ready[n % NR], 16)
                    return
                w, r0, kc, c0 = source(key)
                sp.dma_start(ring[:, n % NR, 0:kc, :],
                             w[r0:r0 + kc * P, c0:c0 + 256].rearrange("(c p) n -> p c n", p=P)) \
                    .then_inc(ring_ready[n % NR], 16)

            for n in range(NR):
                stream(n)
            for i in range(2):
                sp.dma_start(xraw[:, 4 + i, :], io["ctx"][0, i * P:(i + 1) * P, :]).then_inc(s_x2, 16)
            sp.dma_start(mraw[:, :], io["meta_tokens_2"]).then_inc(s_x2, 16)
            for n in range(NR, 8):
                stream(n)
            sp.dma_start(dftL[:].rearrange("p a b n -> p (a b n)"), dl_d).then_inc(s_dft, 16)
            sp.dma_start(dftC[:].rearrange("p a b n -> p (a b n)"), dc_d).then_inc(s_dft, 16)
            end = {0: N_OF[("in", 0, 0)], 1: N_OF[("dk", 0)], 2: N_OF[("in", 1, 0)], 3: N_OF[("B", 0)]}.get(stage, len(PLAN))
            end += {0: 3, 1: 2, 2: 3, 3: 0}.get(stage, 0)
            for n in range(8, end):
                stream(n)
            if stage == 0:
                sp.wait_ge(r_res, 8)
            elif stage == 1:
                sp.wait_ge(r_res, 8 + 24)
            elif stage == 2:
                sp.wait_ge(r_res, 8 + 24 + 8)
            elif stage == 3:
                sp.wait_ge(r_res, 8 + 24 + 8 + 24)
            sp.wait_ge(s_small, 128)
            if stage < 4:
                sp.dma_start(dump, xT[:].rearrange("p c r -> p (c r)")).then_inc(s_dump, 16)
                sp.dma_start(out[0, 0:P, :], kt[:, 0:D]).then_inc(s_dump, 16)
                sp.wait_ge(s_dump, 32)
                return
            for i in range(NT):
                sp.wait_ge(o_fin, 2 * i + 2)
                sp.dma_start(out[0, i * P:(i + 1) * P, :], orow[:, i, :]).then_inc(s_out, 16)
            sp.wait_ge(s_out, 16 * NT)

        @block.tensor
        def _(pe):
            used = [0]
            step = [0]

            def weights(key):
                n = used[0]
                assert PLAN[n] == key, (PLAN[n], key)
                used[0] += 1
                if key in S_OF:
                    pe.wait_ge(w_lo, S_OF[key] + 1)
                    return wH[:, S_OF[key] % NS], wL[:, S_OF[key] % NS]
                pe.wait_ge(ring_ready[n % NR], arrived(n))
                return ring[:, n % NR]

            def begin(key):
                t = step[0]
                assert STEPS[t][0] == key, (STEPS[t][0], key)
                step[0] += 1
                if t >= 2:
                    for w in banks_read(t - 2):
                        pe.wait_ge(*w)
                return t % 2

            def tile(s, half, parts, extra):
                n = len(parts)
                for i, (w, r, wait) in enumerate(parts):
                    if wait is not None:
                        pe.wait_ge(*wait)
                    m = nc.tensor.matmul(bank[3 * s + half], w, r[:, 0:LAT], start=i == 0, stop=i == n - 1)
                if extra:
                    for i, (w, r, _) in enumerate(parts):
                        m = nc.tensor.matmul(bank[3 * s + 2][:, 256 * half:256 * half + extra], w,
                                             r[:, LAT:LAT + extra], start=i == 0, stop=i == n - 1)
                m.then_inc(tile_done, 1)

            def exact(w, a, n, c, wait=None, first=0):
                parts = []
                for k in range(n):
                    on = (wait[0], wait[1] + k + 1) if wait else None
                    parts += [(w[0][:, k, c:c + P], a[0][:, k, :], on), (w[0][:, k, c:c + P], a[1][:, k, :], None),
                              (w[1][:, k, c:c + P], a[0][:, k, :], None)]
                return parts

            def ada_block(layer, b):
                w = weights(("ada", layer, b))
                i = 24 * layer + b
                if i >= 2:
                    pe.wait_ge(ada_taken, i - 1)
                for j in range(2):
                    for kc in range(KC):
                        m = nc.tensor.matmul(bank[6 + b % 2][:, 2 * j:2 * j + 2], w[:, kc, P * j:P * j + P],
                                             cond[:, kc, :], start=kc == 0, stop=kc == KC - 1)
                m.then_inc(ada_done, 1)

            def norm_sums(i, with_ctx):
                sq = (sq0, sq1, sq2, sq1)[i]
                """Sums of squares over the features, on all partitions."""
                for kc in range(KC):
                    pe.wait_ge(n_sq, NORM_SQ[i] + kc + 1)
                    for a, b, half in halves(with_ctx):
                        m = nc.tensor.matmul(bank[6 + half][:, 0:b - a], ones, sq[:, kc % 2, a:b],
                                             start=kc == 0, stop=kc == KC - 1)
                    m.then_inc(n_used, 1)

            pe.wait_ge(s_load, 16)
            pe.wait_ge(s_tab, 16 * 13)
            nc.tensor.transpose(bank[0][:, 0:N_A], rowA[:, :], kt[0:N_A, K_ID:K_ID + N_A]).then_inc(s_cols_t, 1)
            nc.tensor.transpose(bank[1][:, 0:N_B], rowB[:, :], kt[0:N_B, K_ID:K_ID + N_B]).then_inc(s_cols_t, 1)
            nc.tensor.transpose(bank[2][:, 0:N_C], rowC[:, :], kt[0:N_C, K_ID:K_ID + N_C]).then_inc(s_cols_t, 1)
            pe.wait_ge(s_cond, 2)
            pe.wait_ge(s_x, 64)
            pe.wait_ge(s_x2, 48)
            pe.wait_ge(s_cols, 3)
            for kc in range(KC):
                if kc >= 2:
                    pe.wait_ge(s_xlat, kc - 1)
                    pe.wait_ge(s_xctx, kc - 1)
                for i in range(NT):
                    nc.tensor.transpose(bank[3 * (kc % 2)][:, i * P:(i + 1) * P], xraw[:, i, kc * P:(kc + 1) * P], ident)
                for i in range(2):
                    m = nc.tensor.transpose(bank[3 * (kc % 2) + 2][:, i * P:(i + 1) * P], xraw[:, 4 + i, kc * P:(kc + 1) * P], ident)
                m.then_inc(s_xt, 1)
            for kc in range(KC):
                m = nc.tensor.transpose(bank[1][:, kc * META:(kc + 1) * META], mraw[:, kc * P:(kc + 1) * P],
                                        kt[0:META, K_ID:K_ID + META])
            m.then_inc(s_meta_t, 1)
            norm_sums(0, True)
            pe.wait_ge(n_rstd, 2)
            for b in range(8):
                ada_block(0, b)

            def dft_features(g):
                pe.wait_ge(h_ready, g + 1)
                if g:
                    pe.wait_ge(f_acopy, 3 * g)
                    pe.wait_ge(f_y, 2 * g)
                else:
                    pe.wait_ge(s_xlat, KC)
                    pe.wait_ge(s_xctx, KC)
                    pe.wait_ge(s_meta, 1)
                for rt in range(6):
                    m = nc.tensor.matmul(bank[rt // 2][:, 256 * (rt % 2):256 * (rt % 2) + 256],
                                         hT[:, g, rt * P:(rt + 1) * P], dft128, start=True, stop=True)
                    if rt % 2:
                        m.then_inc(f_a, 1)

            def dft_rows(g):
                pe.wait_ge(f_acopy, 3 * g + 3)
                if g == 0:
                    pe.wait_ge(s_dft, 32)
                if g >= 2:
                    pe.wait_ge(f_ylo, 2 * (g - 1))
                lat, cx = bank[3 + g % 2], bank[5]
                for i in range(NT):
                    for j in range(2):
                        m = nc.tensor.matmul(lat, fa[:, i, P * j:P * j + P], dftL[:, i, j, :],
                                             start=i + j == 0, stop=i + j == NT)
                m.then_inc(f_y, 1)
                if g:
                    pe.wait_ge(f_ylo, 2 * g)
                for i in range(2):
                    for j in range(2):
                        m = nc.tensor.matmul(cx[:, 0:CTX], fa[:, 4 + i, P * j:P * j + P], dftC[:, i, j, :],
                                             start=i + j == 0, stop=i + j == 2)
                m.then_inc(f_y, 1)

            dft_features(0)
            for g in range(KC):
                ada_block(0, 8 + 2 * g)
                ada_block(0, 9 + 2 * g)
                dft_rows(g)
                if g + 1 < KC:
                    dft_features(g + 1)
            pe.wait_ge(f_ylo, 2 * KC)
            for cb in range(4):
                s = begin(("fnet", cb))
                w = weights(("fnet", cb))
                for j in range(2):
                    tile(s, j, exact(w, yT, KC, P * j), CTX)
            if stage == 0:
                return

            def ffn(layer, first_h):
                extra = CTX if layer == 0 else 0
                for lo, hi in GROUPS:
                    for c in range(lo, hi):
                        s = begin(("in", layer, c))
                        w = weights(("in", layer, c))
                        for half in range(2):
                            tile(s, half, exact(w, h1, KC, P * half, (h_ready, first_h) if c + half == 0 else None), extra)
                        if layer == 0:
                            ada_block(1, c)
                    for cb in range(4):
                        s = begin(("down", layer, lo, cb))
                        w = weights(("down", layer, lo, cb))
                        for j in range(2):
                            tile(s, j, exact(w, hid, hi - lo, P * j, (g_hid, FC * layer + lo) if cb + j == 0 else None), extra)
                        if (layer, hi) == (0, FC) and cb < 2:
                            ada_block(1, FC + cb)

            pe.wait_ge(ada_taken, 24)
            norm_sums(1, True)
            pe.wait_ge(n_rstd, 4)
            ffn(0, KC)
            if stage == 1:
                return

            pe.wait_ge(ada_taken, 48)
            norm_sums(2, True)
            done = [0]

            def stat(i, with_ctx):
                pe.wait_ge(k_sq, i + 1)
                if i:
                    pe.wait_ge(k_rstd, i)
                else:
                    pe.wait_ge(n_rstd, 6)
                for a, b, half in halves(with_ctx):
                    m = nc.tensor.matmul(bank[6 + half][:, 0:b - a], blk, sq2[:, i % 2, a:b], start=True, stop=True)
                m.then_inc(k_sum, 1)

            for i, kind in enumerate(["dk"] * 8 + ["dq"] * 8):
                cb, j = (i % 8) // 2, i % 2
                if j == 0:
                    s = begin((kind, cb))
                    w = weights((kind, cb))
                tile(s, j, exact(w, h2, KC, P * j, (h_ready, 2 * KC) if i == 0 else None), CTX if kind == "dk" else 0)
                if i:
                    stat(i - 1, i - 1 < 8)
            for cb in range(4):
                s = begin(("dv", cb))
                w = weights(("dv", cb))
                for rt in range(6):
                    for k in range(3 * KC):
                        kc, a, b = k // 3, *((0, 0), (0, 1), (1, 0))[k % 3]
                        m = nc.tensor.matmul(bank[3 * s + rt // 2][:, 256 * (rt % 2):256 * (rt % 2) + 256],
                                             h2[a][:, kc, rt * P:(rt + 1) * P], w[b][:, kc, :], start=k == 0, stop=k == 3 * KC - 1)
                m.then_inc(tile_done, 2)
                if cb == 0:
                    stat(15, False)
            for cb in (2, 3):
                for w in banks_read(T_OF[("dv", cb)]):
                    pe.wait_ge(*w)
            pe.wait_ge(k_done, 16)
            pe.wait_ge(k_rstd, 16)

            def scores(u):
                h, i = u // NT, u % NT
                for c in range(2):
                    if u:
                        pe.wait_ge(a_exp, 2 * (u - 1) + c + 1)
                    r = slice(DH * c, DH * c + DH)
                    nc.tensor.matmul(two[c][:, 0:LAT], qT[r, h, i * P:(i + 1) * P], kT[r, h, 0:LAT], start=True, stop=True)
                    nc.tensor.matmul(two[c][:, LAT:ROWS], qT[r, h, i * P:(i + 1) * P], kT[r, h, LAT:ROWS],
                                     start=True, stop=True).then_inc(a_s, 1)

            def turn(u):
                pe.wait_ge(a_w, u + 1)
                for c in range(2):
                    if u:
                        pe.wait_ge((a_wtc, a_wtd)[c], u)
                    for i in range(3):
                        m = nc.tensor.transpose(bank[4 + c][:, i * P:(i + 1) * P], prob[:, u % 2, 1, (3 * c + i) * P:(3 * c + i + 1) * P], ident)
                    m.then_inc(a_wt, 1)

            def head_stat(h):
                pe.wait_ge(a_sq, h + 1)
                if h:
                    pe.wait_ge(a_rs, h)
                nc.tensor.matmul(bank[7], ones, sq3[:, h % 2, 0:LAT], start=True, stop=True).then_inc(a_ms, 1)

            def after(u):
                turn(u)
                h, i = u // NT, u % NT
                if i == 1 and h:
                    head_stat(h - 1)
                if i == NT - 1:
                    pe.wait_ge(a_wtc, u + 1)
                    pe.wait_ge(a_wtd, u + 1)
                    if h:
                        pe.wait_ge(a_o, h)
                    for i in range(6):
                        m = nc.tensor.matmul(bank[6], V[:, i, h * P:(h + 1) * P], WT[:, i, :], start=i == 0, stop=i == 5)
                    m.then_inc(a_pv, 1)

            scores(0)
            for u in range(4 * HEADS):
                if u + 1 < 4 * HEADS:
                    scores(u + 1)
                if u:
                    after(u - 1)
            after(4 * HEADS - 1)
            head_stat(HEADS - 1)
            pe.wait_ge(a_exp, 8 * HEADS)
            pe.wait_ge(a_wtc, 4 * HEADS)
            pe.wait_ge(a_wtd, 4 * HEADS)
            pe.wait_ge(a_o, HEADS)
            for cb in range(4):
                s = begin(("dout", cb))
                w = weights(("dout", cb))
                for j in range(2):
                    tile(s, j, exact(w, ao, KC, P * j), 0)
            if stage == 2:
                return
            norm_sums(3, False)
            ffn(1, 3 * KC)
            if stage == 3:
                return

            for kc in range(KC):
                pe.wait_ge(n_sq, NORM_SQ[4] + kc + 1)
                nc.tensor.matmul(bank[6], ones, sqb[:, kc % 2, 0:LAT], start=kc == 0, stop=kc == KC - 1)
                nc.tensor.matmul(bank[7][:, 0:META], ones, sqb[:, kc % 2, LAT:ALL], start=kc == 0, stop=kc == KC - 1) \
                    .then_inc(n_used, 1)
            pe.wait_ge(n_rstd, 9)
            pe.wait_ge(h_ready, 5 * KC)
            pe.wait_ge(s_small, 16 * 8)
            for i in range(5):
                r = slice(i * P, min((i + 1) * P, ALL))
                for kc in range(KC):
                    m = nc.tensor.matmul(bank[6][0:r.stop - r.start, 48 * i:48 * i + 48], uT[:, kc, r], wdtf[:, kc, :],
                                         start=kc == 0, stop=kc == KC - 1)
            m.then_inc(d_raw, 1)

            def gemm(key, extra):
                s = begin(key)
                w = weights(key)
                for j in range(2):
                    tile(s, j, [(w[:, kc, P * j:P * j + P], uT[:, kc, :], None) for kc in range(KC)], extra)

            def rows_gemm(key, src, extra):
                s = begin(key)
                w = weights(key)
                for i in range(NT + (extra > 0)):
                    n = P if i < NT else extra
                    for kc in range(KC):
                        m = nc.tensor.matmul(bank[3 * s + i // 2][0:n, 256 * (i % 2):256 * (i % 2) + 256],
                                             src[:, kc, i * P:i * P + n], w[:, kc, :], start=kc == 0, stop=kc == KC - 1)
                m.then_inc(tile_done, 2)

            def b_rows(g):
                pe.wait_ge(c_out, g + 1)
                if g:
                    pe.wait_ge(c_tev, g)
                else:
                    pe.wait_ge(d_cta, 1)
                for i in range(3):
                    nc.tensor.transpose(bank[6][:, i * P:(i + 1) * P], BT[:, g, META + i * P:META + (i + 1) * P], ident)
                nc.tensor.transpose(bank[6][0:META, 3 * P:4 * P], BT[:, g, 0:META], ident).then_inc(c_t, 1)

            gemm(("B", 0), META)
            gemm(("B", 1), META)
            pe.wait_ge(d_adt, 1)
            for i in range(NT):
                nc.tensor.matmul(bank[6][:, 32 * i:32 * i + 32], upper, adt[:, i, :], start=True, stop=True)
            for i in range(3):
                nc.tensor.matmul(bank[6][:, 128 + 32 * i:160 + 32 * i], lower, adt[:, i, :], start=True, stop=True)
            for i in range(3):
                nc.tensor.matmul(bank[6][:, 224 + 32 * i:256 + 32 * i], ones, adt[:, i, :], start=True, stop=True)
            nc.tensor.matmul(bank[6][0:META, 320:352], lower[0:META, 0:META], adt[0:META, 4, :], start=True, stop=True).then_inc(d_sums, 1)
            for i in range(NT):
                c = slice(i * P, (i + 1) * P)
                nc.tensor.matmul(bank[7][0:16, c], logf[0:META, 4, :], ones[0:META, :], start=True, stop=False)
                for j in range(i):
                    nc.tensor.matmul(bank[7][0:16, c], logf[:, j, :], ones, start=False, stop=False)
                nc.tensor.matmul(bank[7][0:16, c], logf[:, i, :], upper, start=False, stop=True)
            pe.wait_ge(d_dec, 1)
            nc.tensor.matmul(bank[6][0:16, 0:META], logf[0:META, 4, :], upper[0:META, 0:META], start=True, stop=True).then_inc(d_ct, 1)
            gemm(("C", 0), META)
            gemm(("C", 1), META)
            for g in range(4):
                b_rows(g)
            pe.wait_ge(c_out, 8)

            def ssd(g):
                n0 = 4 * g
                for j in range(4):
                    i = 8 + 4 * g + j
                    pe.wait_ge(c_out, i + 1)
                    pe.wait_ge(c_tev, 4 + 2 * (4 * g + j) if g + j else 4)
                    if g and j == 0:
                        pe.wait_ge(e_tev, 4 * g)
                    for k in range(NT):
                        nc.tensor.transpose(bank[6][:, k * P:(k + 1) * P], cacc[:, i % 2, META + k * P:META + (k + 1) * P], ident)
                    nc.tensor.transpose(bank[7][0:META, 0:P], cacc[:, i % 2, 0:META], ident).then_inc(c_t, 1)
                for w in banks_read(T_OF[("xs", g, 0)]) + banks_read(T_OF[("xs", g, 1)]):
                    pe.wait_ge(*w)
                pe.wait_ge(c_tev, 4 + 2 * (4 * g + 4))
                pe.wait_ge(p_xds, n0 + 1)
                nc.tensor.matmul(bank[5], Brow[0:META, 3, g * P:(g + 1) * P], xds[0:META, :], start=True, stop=True).then_inc(e_st, 1)

                def segments(i):
                    pe.wait_ge(p_lseg, n0 + i + 1)
                    if i:
                        pe.wait_ge(e_exp, n0 + i)
                    for h in range(8):
                        m = nc.tensor.matmul(two[0][:, h * P:(h + 1) * P], lseg[:, h * P:(h + 1) * P], upper, start=True, stop=True)
                    m.then_inc(e_seg, 1)

                def products(i):
                    if i:
                        pe.wait_ge(e_m, n0 + i)
                    nc.tensor.matmul(bank[2][:, 0:P], BT[:, g, META + i * P:META + (i + 1) * P], CTt[:, g, i * P:(i + 1) * P],
                                     start=True, stop=True).then_inc(e_cb, 1)

                def back(n):
                    pe.wait_ge(e_un, n + 1)
                    if n:
                        pe.wait_ge(e_tev, n)
                    for j in range(4):
                        m = nc.tensor.transpose(bank[6][:, j * P:(j + 1) * P], yrow[:, n % 2, j * P:(j + 1) * P], ident)
                    m.then_inc(e_t, 1)

                segments(0)
                products(0)
                for i in range(NT):
                    n = n0 + i
                    pe.wait_ge(e_h, n + 1)
                    if i:
                        pe.wait_ge(e_gated, n)
                    nc.tensor.matmul(bank[4], CTt[:, g, i * P:(i + 1) * P], Hst[:, i % 2, :], start=True, stop=True).then_inc(e_yoff, 1)
                    if i < 3:
                        pe.wait_ge(p_xds, n + 2)
                        nc.tensor.matmul(bank[5], Brow[:, i, g * P:(g + 1) * P], xds[:, :], start=True, stop=True).then_inc(e_st, 1)
                        segments(i + 1)
                    pe.wait_ge(p_xdt, 5 * g + i + 2)
                    pe.wait_ge(e_m, n + 1)
                    for h in range(8):
                        m = nc.tensor.matmul(bank[3][:, 64 * h:64 * h + 64], Mt[:, i % 2, h, :], xdt[:, (i + 1) % 2, 64 * h:64 * h + 64],
                                             start=True, stop=True)
                    m.then_inc(e_y, 1)
                    if i < 3:
                        products(i + 1)
                    if i:
                        back(n - 1)
                back(n0 + 3)

            for g in range(SG):
                if g:
                    pe.wait_ge(e_gated, 4 * g)
                rows_gemm(("z", g, 0), uT, 0)
                rows_gemm(("z", g, 1), uT, 0)
                gemm(("xs", g, 0), META)
                gemm(("xs", g, 1), META)
                ssd(g)
            pe.wait_ge(e_gated, 16)
            pe.wait_ge(e_tev, 16)

            def spans(i):
                n = META + (i + 1) * P
                return [(0, min(n, 512))] + ([(512, n)] if n > 512 else [])

            def fox_scores(u):
                f, i, h = u // 16, u // 4 % 4, u % 4
                S = two[u % 2]
                if u >= 2:
                    pe.wait_ge(b_exp, u - 1)
                n = META + (i + 1) * P
                for a, b in spans(i):
                    nc.tensor.matmul(S[:, a:b], qA[0:DH + 2, h, i * P:(i + 1) * P], kA[0:DH + 2, h, a:b], start=True, stop=False)
                    o = max(a, n - P)
                    m = nc.tensor.matmul(S[:, o:b], ident, negm[:, o - (n - P):b - (n - P)], start=False, stop=True)
                m.then_inc(b_s, 1)

            def fox_turn(u):
                f, i, h = u // 16, u // 4 % 4, u % 4
                pe.wait_ge(b_exp, u + 1)
                if u:
                    pe.wait_ge(b_pta, u)
                    pe.wait_ge(b_ptd, u)
                for j in range(i + 1):
                    nc.tensor.transpose(bank[4][:, j * P:(j + 1) * P], probA[:, u % 2, META + j * P:META + (j + 1) * P], ident)
                nc.tensor.transpose(bank[5][0:META, 0:P], probA[:, u % 2, 0:META], ident).then_inc(b_pt, 1)

            def fox_out(u):
                f, i, h = u // 16, u // 4 % 4, u % 4
                pe.wait_ge(b_pta, u + 1)
                pe.wait_ge(b_ptd, u + 1)
                if h == 0 and u:
                    pe.wait_ge(b_y, u // 4)
                o = bank[7][:, 64 * h:64 * h + 64]
                nc.tensor.matmul(o, PT[0:META, u % 2, 4 * P:5 * P], vA[0:META, 4, 64 * h:64 * h + 64], start=True, stop=False)
                for j in range(i + 1):
                    m = nc.tensor.matmul(o, PT[:, u % 2, j * P:(j + 1) * P], vA[:, j, 64 * h:64 * h + 64], start=False, stop=j == i)
                m.then_inc(b_o, 1)

            def fox_back(v):
                pe.wait_ge(b_y, v + 1)
                if v:
                    pe.wait_ge(b_ytev, v)
                for j in range(2):
                    m = nc.tensor.transpose(bank[6][:, j * P:(j + 1) * P], yA[:, j * P:(j + 1) * P], ident)
                m.then_inc(b_yt, 1)

            for f in range(4):
                if f:
                    pe.wait_ge(b_exp, 16 * f)
                    pe.wait_ge(b_pta, 16 * f)
                    pe.wait_ge(b_ptd, 16 * f)
                gemm(("q", f), 0)
                gemm(("k", f), META)
                rows_gemm(("v", f), uT, META)
                rows_gemm(("za", f), uT, 0)
                pe.wait_ge(b_q, 16 * (f + 1))
                pe.wait_ge(b_k, 16 * (f + 1))
                for w in sum((banks_read(T_OF[(k, f)]) for k in ("k", "v", "za")), []):
                    pe.wait_ge(*w)
                fox_scores(16 * f)
                for u in range(16 * f, 16 * f + 16):
                    if u + 1 < 16 * f + 16:
                        fox_scores(u + 1)
                    fox_turn(u)
                    if u > 16 * f:
                        fox_out(u - 1)
                    if u % 4 == 1 and u > 16 * f + 1:
                        fox_back(u // 4 - 1)
                fox_out(16 * f + 15)
                fox_back(4 * f + 3)

            pe.wait_ge(b_exp, 64)
            pe.wait_ge(b_pta, 64)
            pe.wait_ge(b_ptd, 64)
            pe.wait_ge(b_ytev, 16)
            for cb in range(4):
                gemm(("gs", cb), 0)
                gemm(("ga", cb), 0)
                s = begin(("ps", cb))
                w0 = weights(("ps", cb, 0))
                w1 = weights(("ps", cb, 1))
                for j in range(2):
                    tile(s, j, [((w0, w1)[k // KC][:, k % KC, P * j:P * j + P], ysT[:, k, :], None) for k in range(2 * KC)], 0)
                s = begin(("pa", cb))
                w = weights(("pa", cb))
                for j in range(2):
                    tile(s, j, [(w[:, kc, P * j:P * j + P], yaT[:, kc, :], None) for kc in range(KC)], 0)
            pe.wait_ge(m_mix, 8)
            for cb in range(4):
                rows_gemm(("wo", cb), mg, 0)
            for i in range(2 * NT):
                if i >= 2:
                    pe.wait_ge(o_fin, i - 1)
                for j in range(4):
                    m = nc.tensor.transpose(bank[6 + i % 2][:, j * P:(j + 1) * P],
                                            xT[:, 4 * (i % 2) + j, (i // 2) * P:(i // 2 + 1) * P], ident)
                m.then_inc(o_xt, 1)

        @block.scalar
        def _(act):
            link = Chain(act, a_chain)
            def rows(dst, a, n, src):
                act.dma_start(dst[a:a + n, :], src).then_inc(s_tab, 16)

            rows(rowA, ROW_C, 8, io["c"].rearrange("a (m p) -> (a m) p", p=P))
            rows(rowA, ROW_CC, 8, io["c_ctx"].rearrange("(m p) -> m p", p=P))
            rows(rowA, ROW_NG, 32, io["norm_gain"].rearrange("a b (m p) -> (a b m) p", p=P))
            rows(rowA, ROW_FB, 8, io["fnet_b_out"].rearrange("a (m p) -> (a m) p", p=P))
            rows(rowA, ROW_NP, 8, io["norm_pre_2"].rearrange("a (m p) -> (a m) p", p=P))
            rows(rowA, ROW_SN, 16, io["ssd_norm_2"].rearrange("a (m p) -> (a m) p", p=P))
            rows(rowA, ROW_GB, 16, io["gate_bias_2"].rearrange("a (m p) -> (a m) p", p=P))
            rows(rowA, ROW_SUB, 1, io["diff_subln_gain"])
            rows(rowA, ROW_QG, 1, io["diff_q_gain"].rearrange("a b d -> a (b d)"))
            rows(rowA, ROW_KG, 1, io["diff_k_gain"].rearrange("a b d -> a (b d)"))
            act.dma_start(rowB[0:96, :], io["b_ada"].rearrange("a (m p) -> (a m) p", p=P)).then_inc(s_tab, 16)
            act.dma_start(rowB[96:120, :], io["conv_b_2"].rearrange("a (m p) -> (a m) p", p=P)).then_inc(s_tab, 16)
            act.dma_start(rowC[:, :], io["conv_w_2"].rearrange("a k (m p) -> (a k m) p", p=P)).then_inc(s_tab, 16)
            act.dma_start(lamv[:], io["diff_lambda"].rearrange("a b d -> a (b d)").broadcast_to([P, 4 * DH])).then_inc(s_small, 16)
            act.dma_start(wdtf[:, :, 0:32], w_in2[:, COL_DT:COL_DT + 32].rearrange("(c p) n -> p c n", p=P)).then_inc(s_small, 16)
            act.dma_start(wdtf[:, :, 32:48], w_in2[:, COL_F:COL_F + 16].rearrange("(c p) n -> p c n", p=P)).then_inc(s_small, 16)
            act.dma_start(bdtf[:, 0:32], io["dt_bias_2"].broadcast_to([P, 32])).then_inc(s_small, 16)
            act.dma_start(bdtf[:, 32:48], io["fgate_bias_2"].broadcast_to([P, 16])).then_inc(s_small, 16)
            act.dma_start(alog[:], io["a_log_2"].broadcast_to([P, 32])).then_inc(s_small, 16)
            act.dma_start(dskip[:], io["d_skip_2"].broadcast_to([P, 32])).then_inc(s_small, 16)
            act.dma_start(gpost[:], io["norm_post_2"].broadcast_to([P, D])).then_inc(s_small, 16)

            act.wait_ge(s_cols_t, 3)
            for b, c, n in ((0, colA, N_A), (1, colB, N_B), (2, colC, N_C)):
                nc.scalar.activation(c[:], bank[b][:, 0:n], ACT.Copy).then_inc(s_cols, 1)
            act.wait_ge(s_cols, 3)
            for j, r in enumerate((ROW_C, ROW_CC)):
                nc.scalar.activation(cond[:, :, j], colA[:, r:r + 8], ACT.Silu).then_inc(s_cond, 1)
            for kc in range(KC):
                act.wait_ge(s_xt, kc + 1)
                nc.scalar.activation(xT[:, kc, LAT:ROWS], bank[3 * (kc % 2) + 2][:, 0:CTX], ACT.Copy).then_inc(s_xctx, 1)
            act.wait_ge(s_meta_t, 1)
            nc.scalar.activation(metaT[:].rearrange("p c r -> p (c r)"), bank[1][:, 0:P], ACT.Copy).then_inc(s_meta, 1)

            def split_hi(n):
                if n >= len(SPLIT):
                    return
                at = N_OF[SPLIT[n]]
                act.wait_ge(ring_ready[at % NR], arrived(at))
                if n >= NS:
                    act.wait_ge(tile_done, 2 * T_OF[SPLIT[n - NS]] + 2)
                raw, hi, _ = split_block(n)
                nc.scalar.activation(hi, raw, ACT.Copy).then_inc(w_hi, 1)

            def modulated_hi(i):
                if i == 0:
                    return
                h = h2 if i == 2 else h1
                end = LAT if i == 3 else ROWS
                tmp = htmp if i == 2 else gateS
                o = 24 * (i % 2)
                for kc in range(KC):
                    act.wait_ge(h_full, KC * (i - 1) + kc + 1)
                    for a, b, half in halves(i < 3):
                        m = nc.scalar.activation(h[0][:, kc, a:b], tmp[:, kc % 2, a:b], ACT.Identity, bias=ada[i // 2][:, o + kc, half:half + 1])
                        if i < 3 and not half:
                            link(m)
                    m.then_inc(h_hi, 1)

            def norm(i, with_ctx, ready=None):
                sq, rstd = ((sq0, rstd0), (sq1, rstd1), (sq2, rstd2), (sq1, rstd1))[i]
                """Squares for TensorE to sum, then 1 / sqrt(mean + eps) on all partitions."""
                end = ROWS if with_ctx else LAT
                for kc in range(KC):
                    if ready is not None:
                        act.wait_ge(*ready(kc))
                    k = NORM_SQ[i] + kc
                    if k >= 2:
                        act.wait_ge(n_used, k - 1)
                    nc.scalar.activation(sq[:, kc % 2, 0:end], xT[:, kc, 0:end], ACT.Square).then_inc(n_sq, 1)
                act.wait_ge(n_used, NORM_SQ[i] + KC)
                for a, b, half in halves(with_ctx):
                    link(nc.scalar.activation(rstd[:, a:b], bank[6 + half][:, 0:b - a], ACT.Ln, bias=epsc[:], scale=1.0 / D))
                    link.wait()
                    nc.scalar.activation(rstd[:, a:b], rstd[:, a:b], ACT.Exp, scale=-0.5).then_inc(n_rstd, 1)

            act.wait_ge(s_xlat, KC)
            act.wait_ge(s_xctx, KC)
            norm(0, True)

            for g in range(KC):
                act.wait_ge(f_a, 3 * g + 2)
                if g:
                    act.wait_ge(f_y, 2 * g)
                act.wait_ge(f_acopy, 3 * g + 1)
                nc.scalar.activation(fa[:, 2:4, :].rearrange("p a n -> p (a n)"), bank[1], ACT.Copy).then_inc(f_acopy, 1)
                act.wait_ge(f_y, 2 * g + 1)
                nc.scalar.activation(yT[0][:, g, 0:LAT], bank[3 + g % 2], ACT.Copy).then_inc(f_ycopy, 1)
                act.wait_ge(f_y, 2 * g + 2)
                nc.scalar.activation(yT[0][:, g, LAT:ROWS], bank[5][:, 0:CTX], ACT.Copy).then_inc(f_ycopy, 1)
            for n in range(4 + NS):
                split_hi(n)
            if stage == 0:
                return

            def ffn(layer):
                for lo, hi in GROUPS:
                    for k in range(lo, hi):
                        t = T_OF[("in", layer, k)]
                        s, c = t % 2, FC * layer + k
                        act.wait_ge(tile_done, 2 * t + (2 if layer == 0 else 1))
                        if c >= 2:
                            act.wait_ge(g_hid, c - 1)
                        m = nc.scalar.activation(gateS[:, c % 2, 0:LAT], bank[3 * s], ACT.Silu)
                        if layer == 0:
                            link(m)
                            m = nc.scalar.activation(gateS[:, c % 2, LAT:ROWS], bank[3 * s + 2][:, 0:CTX], ACT.Silu)
                        m.then_inc(g_silu, 1)
                        end = ROWS if layer == 0 else LAT
                        act.wait_ge(g_full, c + 1)
                        nc.scalar.activation(hid[0][:, k - lo, 0:end], gateS[:, c % 2, 0:end], ACT.Copy).then_inc(g_hi, 1)
                        split_hi(S_OF[("in", layer, k)] + NS)
                    for cb in range(4):
                        split_hi(S_OF[("down", layer, lo, cb)] + NS)

            norm(1, True, lambda kc: (r_res, kc + 1))
            modulated_hi(1)
            ffn(0)
            if stage == 1:
                return
            norm(2, True, lambda kc: (r_res, 24 + kc + 1))
            modulated_hi(2)

            def stats(i):
                with_ctx = i < 8
                t, j = T_OF[("dk", 0)] + i // 2, i % 2
                act.wait_ge(tile_done, 2 * t + 2)
                if i >= 2:
                    act.wait_ge(k_sum, i - 1)
                else:
                    act.wait_ge(n_used, NORM_SQ[2] + KC)
                m = nc.scalar.activation(sq2[:, i % 2, 0:LAT], bank[3 * (t % 2) + j], ACT.Square)
                if with_ctx:
                    link(m)
                    m = nc.scalar.activation(sq2[:, i % 2, LAT:ROWS], bank[3 * (t % 2) + 2][:, 256 * j:256 * j + 256], ACT.Square)
                m.then_inc(k_sq, 1)

            def finish(i):
                with_ctx = i < 8
                act.wait_ge(k_sum, i + 1)
                if i:
                    act.wait_ge(k_norm, i)
                for a, b, half in halves(with_ctx):
                    link(nc.scalar.activation(rstd2[:, a:b], bank[6 + half][:, 0:b - a], ACT.Ln, bias=epsc[:], scale=1.0 / DH))
                    link.wait()
                    m = nc.scalar.activation(rstd2[:, a:b], rstd2[:, a:b], ACT.Exp, scale=-0.5)
                    if with_ctx and half == 0:
                        link(m)
                m.then_inc(k_rstd, 1)
                act.wait_ge(k_norm, i + 1)
                if i:
                    act.wait_ge(k_done, i)
                for q in range(4):
                    o = 32 * (q ^ 1)
                    m = nc.scalar.activation(krot[32 * q:32 * q + 32, :], kraw[o:o + 32, :], ACT.Copy)
                    if q < 3:
                        link(m)
                m.then_inc(k_rot, 1)

            act.wait_ge(h_ready, 3 * KC)
            for i in range(16):
                stats(i)
                if i % 2:
                    split_hi(S_OF[("dk", 0)] + i // 2 + NS)
                    finish(i - 1)
                    finish(i)
            for cb in range(4):
                t = T_OF[("dv", cb)]
                act.wait_ge(tile_done, 2 * t + 2)
                act.wait_ge(k_done, 16)
                nc.scalar.activation(V[:, 2:4, 256 * cb:256 * cb + 256], bank[3 * (t % 2) + 1].rearrange("p (a n) -> p a n", a=2), ACT.Copy) \
                    .then_inc(v_copy, 1)
                split_hi(S_OF[("dv", cb)] + NS)

            def weights_of(u):
                for c in range(2):
                    act.wait_ge(a_max, 2 * u + c + 1)
                    if u >= 2:
                        act.wait_ge(a_wt, 2 * (u - 1))
                    nc.scalar.activation(prob[:, u % 2, c, :], two[c][:, 0:ROWS], ACT.Exp, bias=attmx[:, u % 2, c, 1:2],
                                         scale=DH ** -0.5, accum_out=attmx[:, u % 2, c, 2:3]).then_inc(a_exp, 1)

            def head_end(h):
                act.wait_ge(a_pv, h + 1)
                nc.scalar.activation(sq3[:, h % 2, 0:LAT], bank[6], ACT.Square).then_inc(a_sq, 1)
                act.wait_ge(a_ms, h + 1)
                if h:
                    act.wait_ge(a_o, h)
                link(nc.scalar.activation(rstd3[:, 0:LAT], bank[7], ACT.Ln, bias=epsc[:], scale=1.0 / P))
                link.wait()
                nc.scalar.activation(rstd3[:, 0:LAT], rstd3[:, 0:LAT], ACT.Exp, scale=-0.5).then_inc(a_rs, 1)

            def head_hi(h):
                act.wait_ge(a_of, h + 1)
                nc.scalar.activation(aoH[:, h, :], sq3[:, h % 2, :], ACT.Copy).then_inc(a_ohi, 1)

            def keep_turned(u):
                h, i = u // NT, u % NT
                act.wait_ge(a_wt, 2 * u + 1)
                if i == 0 and h:
                    act.wait_ge(a_pv, h)
                nc.scalar.activation(WT[:, 0:3, i * P:(i + 1) * P], bank[4][:, 0:3 * P].rearrange("p (a n) -> p a n", a=3), ACT.Copy) \
                    .then_inc(a_wtc, 1)
                if i == 1 and h:
                    head_end(h - 1)
                if i == 2 and h:
                    head_hi(h - 1)

            act.wait_ge(s_lam, 1)
            nc.scalar.activation(lams[:, 2:4], lams[:, 4:6], ACT.Exp).then_inc(s_lamx, 1)
            act.wait_ge(k_done, 16)
            weights_of(0)
            for u in range(4 * HEADS):
                if u + 1 < 4 * HEADS:
                    weights_of(u + 1)
                if u:
                    keep_turned(u - 1)
            keep_turned(4 * HEADS - 1)
            head_end(HEADS - 1)
            head_hi(HEADS - 1)
            for cb in range(4):
                split_hi(S_OF[("dout", cb)] + NS)
            if stage == 2:
                return
            norm(3, False, lambda kc: (r_res, 32 + kc + 1))
            modulated_hi(3)
            ffn(1)
            if stage == 3:
                return

            for kc in range(KC):
                act.wait_ge(r_res, 64)
                k = NORM_SQ[4] + kc
                act.wait_ge(n_used, k - 1)
                link(nc.scalar.activation(sqb[:, kc % 2, 0:LAT], xT[:, kc, 0:LAT], ACT.Square))
                nc.scalar.activation(sqb[:, kc % 2, LAT:ALL], metaT[:, kc, :], ACT.Square).then_inc(n_sq, 1)
            act.wait_ge(n_used, NORM_SQ[4] + KC)
            for a, b, half in ((0, LAT, 0), (LAT, ALL, 1)):
                link(nc.scalar.activation(rstdb[:, a:b], bank[6 + half][:, 0:b - a], ACT.Ln, bias=epsc[:], scale=1.0 / D))
                link.wait()
                nc.scalar.activation(rstdb[:, a:b], rstdb[:, a:b], ACT.Exp, scale=-0.5).then_inc(n_rstd, 1)
            nc.scalar.activation(expa[:], alog[:], ACT.Exp).then_inc(d_expa, 1)
            act.wait_ge(d_biased, 1)
            nc.scalar.activation(dtu, dta, ACT.Exp, scale=-1.0).then_inc(d_u, 1)
            act.wait_ge(d_w, 1)
            nc.scalar.activation(dtl, dtw, ACT.Ln).then_inc(d_ln, 1)

            def conv_in(kind, key):
                t = T_OF[key]
                act.wait_ge(tile_done, 2 * t + 2)
                for j in range(2):
                    i = conv_tile(kind, key, j)
                    if i >= 2:
                        act.wait_ge(c_acc, i - 1)
                    else:
                        act.wait_ge(d_zero, 1)
                    link(nc.scalar.activation(cin[:, i % 2, 3:3 + META], bank[3 * (t % 2) + 2][:, 256 * j:256 * j + META], ACT.Copy))
                    nc.scalar.activation(cin[:, i % 2, 3 + META:3 + ALL], bank[3 * (t % 2) + j], ACT.Copy).then_inc(c_in, 1)

            def conv_out(kind, key):
                for j in range(2):
                    i = conv_tile(kind, key, j)
                    ch = {"B": 16, "C": 20 - 4, "xs": -8}[kind] + i
                    bias = colB[:, ROW_CB + ch:ROW_CB + ch + 1]
                    act.wait_ge(c_acc, i + 1)
                    if kind == "B":
                        m = nc.scalar.activation(BT[:, i, :], cacc[:, i % 2, :], ACT.Silu, bias=bias)
                    elif kind == "C":
                        m = nc.scalar.activation(CTt[:, i - 4, :], cacc[:, i % 2, META:ALL], ACT.Silu, bias=bias)
                    else:
                        m = nc.scalar.activation(cacc[:, i % 2, :], cacc[:, i % 2, :], ACT.Silu, bias=bias)
                    m.then_inc(c_out, 1)

            def conv(kind, key):
                conv_in(kind, key)
                conv_out(kind, key)

            conv("B", ("B", 0))
            act.wait_ge(d_sums, 1)
            link(nc.scalar.activation(dec[:, 0:320], bank[6][:, 0:320], ACT.Exp))
            nc.scalar.activation(dec[0:META, 320:352], bank[6][0:META, 320:352], ACT.Exp).then_inc(d_dec, 1)
            act.wait_ge(d_ct, 1)
            link(nc.scalar.activation(ckT[:, META:ALL], bank[7][0:16, :], ACT.Copy, scale=-8.0))
            link(nc.scalar.activation(cqT[:, :], bank[7][0:16, :], ACT.Copy, scale=8.0))
            nc.scalar.activation(ckT[:, 0:META], bank[6][0:16, 0:META], ACT.Copy, scale=-8.0).then_inc(d_cta, 1)
            conv("B", ("B", 1))
            conv("C", ("C", 0))
            conv("C", ("C", 1))
            for g in range(SG):
                for j in range(2):
                    t = T_OF[("z", g, j)]
                    act.wait_ge(tile_done, 2 * t + 2)
                    if g and j == 0:
                        act.wait_ge(e_gated, 4 * g)
                    for i in range(2):
                        m = nc.scalar.activation(zrow[:, 2 * i:2 * i + 2, 256 * j:256 * j + 256],
                                                 bank[3 * (t % 2) + i].rearrange("p (a n) -> p a n", a=2), ACT.Silu)
                        if i == 0:
                            link(m)
                    m.then_inc(z_act, 1)
                for j in range(2):
                    conv("xs", ("xs", g, j))
                    for jj in range(2):
                        i = 4 * g + 2 * j + jj
                        act.wait_ge(c_t, 4 + i + 1)
                        nc.scalar.activation(xrow[0:META, 4, P * (i % 4):P * (i % 4) + P], bank[7][0:META, 0:P], ACT.Copy).then_inc(c_tev, 1)

                def decay_exp(i):
                    n = 4 * g + i
                    act.wait_ge(e_seg, n + 1)
                    if n >= 2:
                        act.wait_ge(e_y, n - 1)
                    nc.scalar.activation(Mt[:, i % 2].rearrange("p a n -> p (a n)"), two[0][:, :], ACT.Exp).then_inc(e_exp, 1)

                decay_exp(0)
                for i in range(NT):
                    n = 4 * g + i
                    if i + 1 < NT:
                        decay_exp(i + 1)
                    act.wait_ge(e_gated, n + 1)
                    link(nc.scalar.activation(ysq, yrow[:, i % 2, :], ACT.Square, accum_out=stt4[:, 0:1]))
                    link.wait()
                    link(nc.scalar.activation(stt4[:, 1:2], stt4[:, 0:1], ACT.Ln, bias=epsc[:], scale=1.0 / 512))
                    link.wait()
                    link(nc.scalar.activation(stt4[:, 2:3], stt4[:, 1:2], ACT.Exp, scale=-0.5))
                    link.wait()
                    nc.scalar.activation(yrow[:, i % 2, :], yrow[:, i % 2, :], ACT.Copy, scale=stt4[:, 2:3]).then_inc(e_un, 1)

            for f in range(4):
                for k, kind in enumerate("qk"):
                    t = T_OF[(kind, f)]
                    dst = qA if kind == "q" else kA
                    o = 0 if kind == "q" else META
                    act.wait_ge(tile_done, 2 * t + 1)
                    if f:
                        act.wait_ge(b_s, 16 * f)
                    link(nc.scalar.activation(dst[0:DH, 0, o:o + LAT], bank[3 * (t % 2)][0:DH, :], ACT.Copy))
                    nc.scalar.activation(dst[0:DH, 1, o:o + LAT], bank[3 * (t % 2)][DH:P, :], ACT.Copy).then_inc(x_act, 1)
                t = T_OF[("v", f)]
                act.wait_ge(tile_done, 2 * t + 2)
                if f:
                    act.wait_ge(b_o, 16 * f)
                nc.scalar.activation(vA[:, 0:2, :], bank[3 * (t % 2)].rearrange("p (a n) -> p a n", a=2), ACT.Copy).then_inc(x_act, 1)
                t = T_OF[("za", f)]
                act.wait_ge(tile_done, 2 * t + 2)
                if f:
                    act.wait_ge(b_y, 4 * f)
                link(nc.scalar.activation(zA[:, 0:2, :], bank[3 * (t % 2)].rearrange("p (a n) -> p a n", a=2), ACT.Silu))
                nc.scalar.activation(zA[:, 2:4, :], bank[3 * (t % 2) + 1].rearrange("p (a n) -> p a n", a=2), ACT.Silu).then_inc(z_act, 1)

                def fox_exp(u):
                    i, h = u // 4 % 4, u % 4
                    n = META + (i + 1) * P
                    act.wait_ge(b_max, u + 1)
                    if u >= 2:
                        act.wait_ge(b_pt, u - 1)
                    if h == 0 and u >= 16:
                        act.wait_ge(b_y, u // 4 - 3)
                    nc.scalar.activation(probA[:, u % 2, 0:n], two[u % 2][:, 0:n], ACT.Exp, bias=amx[:, u % 2, 1:2],
                                         scale=DH ** -0.5, accum_out=asum[:, i, h:h + 1]).then_inc(b_exp, 1)

                fox_exp(16 * f)
                for u in range(16 * f, 16 * f + 16):
                    i = u // 4 % 4
                    if u + 1 < 16 * f + 16:
                        fox_exp(u + 1)
                    act.wait_ge(b_pt, u + 1)
                    if u >= 2:
                        act.wait_ge(b_o, u - 1)
                    nc.scalar.activation(PT[:, u % 2, 0:(i + 1) * P], bank[4][:, 0:(i + 1) * P], ACT.Copy).then_inc(b_pta, 1)

            for cb in range(4):
                for k, (kind, dst) in enumerate((("gs", gsb), ("ga", gab))):
                    t = T_OF[(kind, cb)]
                    for j in range(2):
                        act.wait_ge(tile_done, 2 * t + 1 + j)
                        if cb:
                            act.wait_ge(m_mix, 2 * (cb - 1) + k + 1)
                        c = ROW_GB + 8 * k + 2 * cb + j
                        m = nc.scalar.activation(dst[:, j, :], bank[3 * (t % 2) + j], ACT.Sigmoid, bias=colA[:, c:c + 1])
                        if j == 0:
                            link(m)
                    m.then_inc(m_gate, 1)
            for cb in range(4):
                t = T_OF[("wo", cb)]
                act.wait_ge(tile_done, 2 * t + 2)
                for i in range(2):
                    m = nc.scalar.activation(orow[:, 2 * i:2 * i + 2, 256 * cb:256 * cb + 256],
                                             bank[3 * (t % 2) + i].rearrange("p (a n) -> p a n", a=2), ACT.Copy)
                    if i == 0:
                        link(m)
                m.then_inc(o_act, 1)
            act.wait_ge(o_ss, 4)
            link(nc.scalar.activation(stt4[:, 4:8], stt4[:, 0:4], ACT.Ln, bias=epsc[:], scale=1.0 / D))
            link.wait()
            nc.scalar.activation(stt4[:, 4:8], stt4[:, 4:8], ACT.Exp, scale=-0.5).then_inc(o_rs, 1)

        @block.vector
        def _(dve):
            link = Chain(dve, v_chain)
            nc.vector.memset(epsc[:], EPS)
            for kc in range(KC):
                dve.wait_ge(s_xt, kc + 1)
                nc.vector.tensor_copy(xT[:, kc, 0:LAT], bank[3 * (kc % 2)]).then_inc(s_xlat, 1)

            def take_ada(layer, b):
                dve.wait_ge(ada_done, 24 * layer + b + 1)
                o = 48 * layer + 2 * b
                nc.vector.tensor_tensor(ada[layer][:, 2 * b:2 * b + 2, :],
                                        bank[6 + b % 2][:, 0:4].rearrange("p (a n) -> p a n", a=2),
                                        colB[:, o:o + 2].unsqueeze(2).broadcast_to([P, 2, 2]), ALU.add).then_inc(ada_taken, 1)

            def multipliers(i):
                layer, w = i // 2, i % 2
                dve.wait_ge(ada_taken, 24 * layer + 12 * w + 8)
                nc.vector.scalar_tensor_tensor(out=mult[:, i], in0=ada[layer][:, 24 * w + 8:24 * w + 16, :], scalar=1.0,
                                               in1=colA[:, ROW_NG + 8 * i:ROW_NG + 8 * i + 8].unsqueeze(2).broadcast_to([P, KC, 2]),
                                               op0=ALU.add, op1=ALU.mult).then_inc(s_mult, 1)
                dve.wait_ge(s_mult, i + 1)

            def modulated_full():
                dve.wait_ge(n_rstd, 2)
                for kc in range(KC):
                    link(nc.vector.tensor_tensor(hT[:, kc, :], xT[:, kc, :], rstd0[:], ALU.mult))
                    if kc:
                        scale_shift(kc - 1)
                scale_shift(KC - 1)

            def scale_shift(kc):
                link.wait()
                for a, b, half in halves(True):
                    m = nc.vector.tensor_scalar(hT[:, kc, a:b], hT[:, kc, a:b], mult[:, 0, kc, half:half + 1],
                                                ada[0][:, kc, half:half + 1], ALU.mult, ALU.add)
                m.then_inc(h_ready, 1)

            def modulated(i, with_ctx):
                layer, w = i // 2, i % 2
                h, rstd, tmp = (None, (h1, rstd1, gateS), (h2, rstd2, htmp), (h1, rstd1, gateS))[i]
                dve.wait_ge(n_rstd, {1: 4, 2: 6, 3: 7}[i])

                def low(kc):
                    dve.wait_ge(h_hi, KC * (i - 1) + kc + 1)
                    for a, b, half in halves(with_ctx):
                        m = nc.vector.scalar_tensor_tensor(out=h[1][:, kc, a:b], in0=tmp[:, kc % 2, a:b], scalar=ada[layer][:, 24 * w + kc, half:half + 1],
                                                           in1=h[0][:, kc, a:b].bitcast(F32), op0=ALU.add, op1=ALU.subtract)
                        if with_ctx and not half:
                            link(m)
                    m.then_inc(h_ready, 1)

                for kc in range(KC):
                    if kc >= 2:
                        dve.wait_ge(h_ready, KC * i + kc - 1)
                    for a, b, half in halves(with_ctx):
                        m = nc.vector.scalar_tensor_tensor(out=tmp[:, kc % 2, a:b], in0=xT[:, kc, a:b], scalar=mult[:, i, kc, half:half + 1],
                                                           in1=rstd[:, a:b], op0=ALU.mult, op1=ALU.mult)
                        if with_ctx and not half:
                            link(m)
                    m.then_inc(h_full, 1)
                    if kc:
                        low(kc - 1)
                low(KC - 1)

            def split_lo(n):
                if n >= len(SPLIT):
                    return
                dve.wait_ge(w_hi, n + 1)
                raw, hi, lo = split_block(n)
                nc.vector.tensor_tensor(lo, raw, hi.bitcast(F32), ALU.subtract).then_inc(w_lo, 1)

            dve.wait_ge(s_cols, 3)
            for b in range(8):
                take_ada(0, b)
            multipliers(0)
            dve.wait_ge(s_xctx, KC)
            modulated_full()
            for g in range(KC):
                if g:
                    dve.wait_ge(f_y, 2 * g)
                dve.wait_ge(f_a, 3 * g + 1)
                nc.vector.tensor_copy(fa[:, 0:2, :].rearrange("p a n -> p (a n)"), bank[0]).then_inc(f_acopy, 1)
                dve.wait_ge(f_acopy, 3 * g + 2)
                dve.wait_ge(f_a, 3 * g + 3)
                nc.vector.tensor_copy(fa[:, 4:6, :].rearrange("p a n -> p (a n)"), bank[2]).then_inc(f_acopy, 1)
                take_ada(0, 8 + 2 * g)
                take_ada(0, 9 + 2 * g)
                dve.wait_ge(f_ycopy, 2 * g + 1)
                nc.vector.tensor_tensor(yT[1][:, g, 0:LAT], bank[3 + g % 2], yT[0][:, g, 0:LAT].bitcast(F32), ALU.subtract).then_inc(f_ylo, 1)
                dve.wait_ge(f_ycopy, 2 * g + 2)
                nc.vector.tensor_tensor(yT[1][:, g, LAT:ROWS], bank[5][:, 0:CTX], yT[0][:, g, LAT:ROWS].bitcast(F32), ALU.subtract).then_inc(f_ylo, 1)
            multipliers(1)
            link(nc.vector.tensor_tensor(gb[:], ada[0][:, 16:24, :], colA[:, ROW_FB:ROW_FB + KC].unsqueeze(2).broadcast_to([P, KC, 2]), ALU.mult))
            link.wait()
            split_lo(0)
            split_lo(1)
            for m in range(KC):
                for a, b, half in halves(True):
                    link(nc.vector.tensor_scalar(xT[:, m, a:b], xT[:, m, a:b], gb[:, m, half:half + 1], None, ALU.add))
            link.wait()

            def residual(t, layer, piece, cb, with_ctx):
                s = t % 2
                dve.wait_ge(tile_done, 2 * t + 2)
                for j in range(2):
                    m = 2 * cb + j
                    for a, b, half in halves(with_ctx):
                        src = bank[3 * s + 2][:, 256 * j:256 * j + 256] if half else bank[3 * s + j]
                        i = nc.vector.scalar_tensor_tensor(out=xT[:, m, a:b], in0=src, scalar=ada[layer][:, 8 * piece + m, half:half + 1],
                                                           in1=xT[:, m, a:b], op0=ALU.mult, op1=ALU.add)
                        if with_ctx and not half:
                            link(i)
                    i.then_inc(r_res, 1)

            for cb in range(4):
                residual(T_OF[("fnet", cb)], 0, 2, cb, True)
                split_lo(cb + NS)
            if stage == 0:
                return

            def ffn(layer):
                end = ROWS if layer == 0 else LAT
                for g, (lo, hi) in enumerate(GROUPS):
                    for k in range(lo, hi):
                        t = T_OF[("in", layer, k)]
                        s, c = t % 2, FC * layer + k
                        dve.wait_ge(tile_done, 2 * t + 2)
                        dve.wait_ge(g_silu, c + 1)
                        m = nc.vector.tensor_tensor(gateS[:, c % 2, 0:LAT], gateS[:, c % 2, 0:LAT], bank[3 * s + 1], ALU.mult)
                        if layer == 0:
                            link(m)
                            m = nc.vector.tensor_tensor(gateS[:, c % 2, LAT:ROWS], gateS[:, c % 2, LAT:ROWS],
                                                        bank[3 * s + 2][:, 256:512], ALU.mult)
                        m.then_inc(g_full, 1)
                        dve.wait_ge(g_hi, c + 1)
                        nc.vector.tensor_tensor(hid[1][:, k - lo, 0:end], gateS[:, c % 2, 0:end], hid[0][:, k - lo, 0:end].bitcast(F32), ALU.subtract) \
                            .then_inc(g_hid, 1)
                        split_lo(S_OF[("in", layer, k)] + NS)
                        if layer == 0:
                            take_ada(1, k)
                    for cb in range(4):
                        residual(T_OF[("down", layer, lo, cb)], layer, 5, cb, layer == 0)
                        split_lo(S_OF[("down", layer, lo, cb)] + NS)
                        if (layer, hi) == (0, FC) and cb < 2:
                            take_ada(1, FC + cb)

            modulated(1, True)
            ffn(0)
            if stage == 1:
                return

            dve.wait_ge(s_small, 16 * 8)
            multipliers(2)
            multipliers(3)
            modulated(2, True)

            def normed(i):
                with_ctx = i < 8
                gain = colA[:, ROW_KG:ROW_KG + 1] if i < 8 else colA[:, ROW_QG:ROW_QG + 1]
                t, j = T_OF[("dk", 0)] + i // 2, i % 2
                dst = kT if i < 8 else qT
                h = i % 8
                dve.wait_ge(k_rstd, i + 1)
                if i:
                    dve.wait_ge(k_rot, i)
                if with_ctx:
                    link(nc.vector.scalar_tensor_tensor(out=kT[:, h, LAT:ROWS], in0=bank[3 * (t % 2) + 2][:, 256 * j:256 * j + 256],
                                                        scalar=gain, in1=rstd2[:, LAT:ROWS], op0=ALU.mult, op1=ALU.mult))
                nc.vector.scalar_tensor_tensor(out=kraw[:], in0=bank[3 * (t % 2) + j], scalar=gain,
                                               in1=rstd2[:, 0:LAT], op0=ALU.mult, op1=ALU.mult).then_inc(k_norm, 1)
                dve.wait_ge(k_norm, i + 1)
                link(nc.vector.tensor_tensor(dst[:, h, 0:LAT], kraw[:], cosT, ALU.mult))
                dve.wait_ge(k_rot, i + 1)
                link(nc.vector.tensor_tensor(krot[:], krot[:], sinT, ALU.mult))
                link.wait()
                nc.vector.tensor_tensor(dst[:, h, 0:LAT], dst[:, h, 0:LAT], krot[:], ALU.add).then_inc(k_done, 1)

            for i in range(16):
                normed(i)
                if i % 2:
                    split_lo(S_OF[("dk", 0)] + i // 2 + NS)
            for cb in range(4):
                t = T_OF[("dv", cb)]
                dve.wait_ge(tile_done, 2 * t + 2)
                for b in (0, 2):
                    m = nc.vector.tensor_copy(V[:, 2 * b:2 * b + 2, 256 * cb:256 * cb + 256],
                                              bank[3 * (t % 2) + b].rearrange("p (a n) -> p a n", a=2))
                m.then_inc(v_copyd, 1)
                split_lo(S_OF[("dv", cb)] + NS)
            for j in range(2):
                link(nc.vector.tensor_tensor_reduce(lamt[:], lamv[:, 2 * j * DH:(2 * j + 1) * DH], lamv[:, (2 * j + 1) * DH:(2 * j + 2) * DH],
                                                    1.0, 0.0, ALU.mult, ALU.add, lams[:, j:j + 1]))
                link.wait()
            nc.vector.tensor_copy(lams[:, 4:6], lams[:, 0:2]).then_inc(s_lam, 1)
            dve.wait_ge(s_lamx, 1)
            link(nc.vector.tensor_tensor(lams[:, 0:1], lams[:, 3:4], lams[:, 2:3], ALU.subtract))
            link.wait()
            link(nc.vector.tensor_scalar(lams[:, 6:7], lams[:, 0:1], -LAM_INIT, None, ALU.add))
            link(nc.vector.tensor_scalar(lamt[:, 0:1], colA[:, ROW_SUB:ROW_SUB + 1], 1.0 - LAM_INIT, None, ALU.mult))

            def combine(u):
                dve.wait_ge(a_exp, 2 * u + 2)
                m = attmx[:, u % 2]
                link(nc.vector.reciprocal(m[:, :, 3:4], m[:, :, 2:3]))
                link.wait()
                link(nc.vector.tensor_scalar(m[:, 1, 3:4], m[:, 1, 3:4], lams[:, 6:7], None, ALU.mult))
                link(nc.vector.tensor_scalar(prob[:, u % 2, 0, :], prob[:, u % 2, 0, :], m[:, 0, 3:4], None, ALU.mult))
                link.wait()
                nc.vector.scalar_tensor_tensor(out=prob[:, u % 2, 1, :], in0=prob[:, u % 2, 1, :], scalar=m[:, 1, 3:4],
                                               in1=prob[:, u % 2, 0, :], op0=ALU.mult, op1=ALU.add).then_inc(a_w, 1)

            def maxima(u):
                for c in range(2):
                    dve.wait_ge(a_s, 2 * u + c + 1)
                    m = attmx[:, u % 2, c]
                    link(nc.vector.tensor_reduce(m[:, 0:1], two[c][:, 0:ROWS], AX.X, ALU.max))
                    link.wait()
                    nc.vector.tensor_scalar(m[:, 1:2], m[:, 0:1], -DH ** -0.5, None, ALU.mult).then_inc(a_max, 1)

            def head_out(h):
                dve.wait_ge(a_rs, h + 1)
                nc.vector.scalar_tensor_tensor(out=sq3[:, h % 2, :], in0=bank[6], scalar=lamt[:, 0:1], in1=rstd3[:],
                                               op0=ALU.mult, op1=ALU.mult).then_inc(a_of, 1)

            def head_lo(h):
                dve.wait_ge(a_ohi, h + 1)
                nc.vector.tensor_tensor(aoL[:, h, :], sq3[:, h % 2, :], aoH[:, h, :].bitcast(F32), ALU.subtract).then_inc(a_o, 1)

            def keep_turned(u):
                h, i = u // NT, u % NT
                dve.wait_ge(a_wt, 2 * u + 2)
                if i == 0 and h:
                    dve.wait_ge(a_pv, h)
                nc.vector.tensor_copy(WT[:, 3:6, i * P:(i + 1) * P], bank[5][:, 0:3 * P].rearrange("p (a n) -> p a n", a=3)).then_inc(a_wtd, 1)
                if i == 2 and h:
                    head_out(h - 1)
                if i == 3 and h:
                    head_lo(h - 1)

            maxima(0)
            for u in range(4 * HEADS):
                if u + 1 < 4 * HEADS:
                    maxima(u + 1)
                combine(u)
                if u:
                    keep_turned(u - 1)
            keep_turned(4 * HEADS - 1)
            head_out(HEADS - 1)
            head_lo(HEADS - 1)
            for cb in range(4):
                residual(T_OF[("dout", cb)], 1, 2, cb, False)
                split_lo(S_OF[("dout", cb)] + NS)
            if stage == 2:
                return
            modulated(3, False)
            ffn(1)
            if stage == 3:
                return

            dve.wait_ge(n_rstd, 9)
            for kc in range(KC):
                gain = colA[:, ROW_NP + kc:ROW_NP + kc + 1]
                link(nc.vector.scalar_tensor_tensor(out=uT[:, kc, 0:LAT], in0=xT[:, kc, 0:LAT], scalar=gain, in1=rstdb[:, 0:LAT],
                                               op0=ALU.mult, op1=ALU.mult))
                nc.vector.scalar_tensor_tensor(out=uT[:, kc, LAT:ALL], in0=metaT[:, kc, :], scalar=gain, in1=rstdb[:, LAT:ALL],
                                               op0=ALU.mult, op1=ALU.mult).then_inc(h_ready, 1)
            dve.wait_ge(d_raw, 1)
            dve.wait_ge(d_zero, 2)
            link(nc.vector.tensor_tensor(dtr[:, 0:4, :], bank[6][:, 0:192].rearrange("p (a n) -> p a n", a=4),
                                    bdtf[:].unsqueeze(1).broadcast_to([P, 4, 48]), ALU.add))
            link(nc.vector.tensor_tensor(dtr[0:META, 4, :], bank[6][0:META, 192:240], bdtf[0:META, :], ALU.add))
            link.wait()
            nc.vector.scalar_tensor_tensor(out=dta, in0=dtr[:], scalar=-1.0, in1=dtr[:], op0=ALU.mult, op1=ALU.max).then_inc(d_biased, 1)
            dve.wait_ge(d_u, 1)
            nc.vector.tensor_scalar(dtw, dtu, 1.0, None, ALU.add).then_inc(d_w, 1)
            dve.wait_ge(d_w, 1)
            link(nc.vector.reciprocal(dta, dtw))
            link(nc.vector.scalar_tensor_tensor(out=dtu, in0=dtw, scalar=-1.0, in1=dtu, op0=ALU.add, op1=ALU.subtract))
            link.wait()
            link(nc.vector.scalar_tensor_tensor(out=dtu, in0=dtu, scalar=-1.0, in1=dta, op0=ALU.mult, op1=ALU.mult))
            link.wait()
            dve.wait_ge(d_ln, 1)
            link(nc.vector.tensor_tensor(dtl, dtl, dtu, ALU.add))
            link.wait()
            link(nc.vector.scalar_tensor_tensor(out=dtv[:], in0=dtr[:, :, 0:32], scalar=0.0, in1=dtl[:, :, 0:32], op0=ALU.max, op1=ALU.add))
            link(nc.vector.scalar_tensor_tensor(out=logf[:], in0=dtr[:, :, 32:48], scalar=0.0, in1=dtl[:, :, 32:48], op0=ALU.min, op1=ALU.subtract))
            link.wait()
            dve.wait_ge(d_expa, 1)
            nc.vector.scalar_tensor_tensor(out=adt[:], in0=dtv[:], scalar=-1.0, in1=expa[:].unsqueeze(1).broadcast_to([P, 5, 32]),
                                           op0=ALU.mult, op1=ALU.mult).then_inc(d_adt, 1)

            def conv(i):
                ch = 16 + i if i < 8 else i - 8
                dve.wait_ge(c_in, i + 1)
                if i >= 2:
                    dve.wait_ge(c_out, i - 1)
                if i >= 10:
                    dve.wait_ge(c_t, 4 + (i - 8) - 1)
                for k in range(4):
                    w = colC[:, 24 * k + ch:24 * k + ch + 1]
                    x = cin[:, i % 2, k:k + ALL]
                    if k == 0:
                        m = nc.vector.tensor_scalar(cacc[:, i % 2, :], x, w, None, ALU.mult)
                    else:
                        m = nc.vector.scalar_tensor_tensor(out=cacc[:, i % 2, :], in0=x, scalar=w, in1=cacc[:, i % 2, :],
                                                           op0=ALU.mult, op1=ALU.add)
                    if k < 3:
                        link(m)
                        link.wait()
                m.then_inc(c_acc, 1)

            for i in range(8):
                conv(i)
            for g in range(4):
                dve.wait_ge(c_t, g + 1)
                link(nc.vector.tensor_copy(Brow[:, 0:3, g * P:(g + 1) * P], bank[6][:, 0:384].rearrange("p (a n) -> p a n", a=3)))
                nc.vector.tensor_copy(Brow[0:META, 3, g * P:(g + 1) * P], bank[6][0:META, 384:512]).then_inc(c_tev, 1)

            def wide(x, n, k):
                return x.unsqueeze(2).broadcast_to([n, 8, k])

            def heads(x):
                return x.rearrange("p (h d) -> p h d", h=8)

            for g in range(SG):
                hs = slice(8 * g, 8 * g + 8)
                for j in range(4):
                    i = 8 + 4 * g + j
                    conv(i)
                    if j % 2:
                        for jj in (j - 1, j):
                            dve.wait_ge(c_t, 4 + 4 * g + jj + 1)
                            nc.vector.tensor_copy(xrow[:, 0:4, P * jj:P * jj + P], bank[6].rearrange("p (a n) -> p a n", a=4)).then_inc(c_tev, 1)
                dve.wait_ge(e_st, 4 * g + 1)
                if g:
                    dve.wait_ge(e_yoff, 4 * g)
                nc.vector.tensor_copy(Hst[:, 0, :], bank[5]).then_inc(e_h, 1)

                def keep(n):
                    dve.wait_ge(e_t, n + 1)
                    c = ROW_SN + 4 * (n // 4)
                    nc.vector.tensor_tensor(ysT[:, 4 * (n // 4):4 * (n // 4) + 4, (n % 4) * P:(n % 4 + 1) * P],
                                            bank[6].rearrange("p (a n) -> p a n", a=4),
                                            colA[:, c:c + 4].unsqueeze(2).broadcast_to([P, 4, P]), ALU.mult).then_inc(e_tev, 1)

                for i in range(NT):
                    n = 4 * g + i
                    y = yrow[:, i % 2, :]
                    dve.wait_ge(e_cb, n + 1)
                    link(nc.vector.tensor_tensor(CBm[:], bank[2][:, 0:P], upper, ALU.mult))
                    link.wait()
                    dve.wait_ge(e_exp, n + 1)
                    nc.vector.tensor_tensor(Mt[:, i % 2], Mt[:, i % 2], CBm[:].unsqueeze(1).broadcast_to([P, 8, P]), ALU.mult).then_inc(e_m, 1)
                    if i < 3:
                        if n >= 2:
                            dve.wait_ge(e_yoff, n)
                        dve.wait_ge(e_h, n + 1)
                        c = 224 + 32 * i + 8 * g
                        link(nc.vector.tensor_tensor(heads(Hst[:, (i + 1) % 2, :]), heads(Hst[:, i % 2, :]), wide(dec[:, c:c + 8], P, 64), ALU.mult))
                        link.wait()
                        dve.wait_ge(e_st, n + 2)
                        nc.vector.tensor_tensor(Hst[:, (i + 1) % 2, :], Hst[:, (i + 1) % 2, :], bank[5], ALU.add).then_inc(e_h, 1)
                    c = 32 * i + 8 * g
                    dve.wait_ge(e_yoff, n + 1)
                    if n >= 2:
                        dve.wait_ge(e_t, n - 1)
                    link(nc.vector.tensor_tensor(heads(y), heads(bank[4]), wide(dec[:, c:c + 8], P, 64), ALU.mult))
                    link.wait()
                    dve.wait_ge(p_xd, n + 1)
                    link(nc.vector.tensor_tensor(y, y, xd[:], ALU.add))
                    link.wait()
                    dve.wait_ge(e_y, n + 1)
                    link(nc.vector.tensor_tensor(y, y, bank[3], ALU.add))
                    link.wait()
                    dve.wait_ge(z_act, 2 * g + 2)
                    nc.vector.tensor_tensor(y, y, zrow[:, i, :], ALU.mult).then_inc(e_gated, 1)
                    if i:
                        keep(n - 1)
                keep(4 * g + 3)

            for f in range(4):
                for kind in "qk":
                    t = T_OF[(kind, f)]
                    dst = qA if kind == "q" else kA
                    o = 0 if kind == "q" else META
                    dve.wait_ge(tile_done, 2 * t + 2)
                    if f:
                        dve.wait_ge(b_s, 16 * f)
                    link(nc.vector.tensor_copy(dst[0:DH, 2, o:o + LAT], bank[3 * (t % 2) + 1][0:DH, :]))
                    m = nc.vector.tensor_copy(dst[0:DH, 3, o:o + LAT], bank[3 * (t % 2) + 1][DH:P, :])
                    if kind == "k":
                        link(m)
                        for j in range(4):
                            r = DH * (j % 2)
                            m = nc.vector.tensor_copy(kA[0:DH, j, 0:META],
                                                      bank[3 * (t % 2) + 2][r:r + DH, 256 * (j // 2):256 * (j // 2) + META])
                            if j < 3:
                                link(m)
                    m.then_inc(x_dve, 1)
                t = T_OF[("v", f)]
                dve.wait_ge(tile_done, 2 * t + 2)
                if f:
                    dve.wait_ge(b_o, 16 * f)
                link(nc.vector.tensor_copy(vA[:, 2:4, :], bank[3 * (t % 2) + 1].rearrange("p (a n) -> p a n", a=2)))
                nc.vector.tensor_copy(vA[0:META, 4, :], bank[3 * (t % 2) + 2][0:META, 0:256]).then_inc(x_dve, 1)

                def fox_max(u):
                    i = u // 4 % 4
                    dve.wait_ge(b_s, u + 1)
                    link(nc.vector.tensor_reduce(amx[:, u % 2, 0:1], two[u % 2][:, 0:META + (i + 1) * P], AX.X, ALU.max))
                    link.wait()
                    if u >= 2:
                        dve.wait_ge(b_exp, u - 1)
                    nc.vector.tensor_scalar(amx[:, u % 2, 1:2], amx[:, u % 2, 0:1], -DH ** -0.5, None, ALU.mult).then_inc(b_max, 1)

                def fox_gate(v):
                    i = v % 4
                    dve.wait_ge(b_exp, 4 * v + 4)
                    link(nc.vector.reciprocal(asum[:, i, :], asum[:, i, :]))
                    link.wait()
                    dve.wait_ge(b_o, 4 * v + 4)
                    if v:
                        dve.wait_ge(b_yt, v)
                    link(nc.vector.tensor_tensor(yA[:].rearrange("p (h d) -> p h d", h=4), bank[7][:, 0:256].rearrange("p (h d) -> p h d", h=4),
                                                 asum[:, i, :].unsqueeze(2).broadcast_to([P, 4, 64]), ALU.mult))
                    link.wait()
                    dve.wait_ge(z_act, 2 * SG + f + 1)
                    nc.vector.tensor_tensor(yA[:], yA[:], zA[:, i, :], ALU.mult).then_inc(b_y, 1)

                def fox_keep(v):
                    i = v % 4
                    dve.wait_ge(b_yt, v + 1)
                    nc.vector.tensor_copy(yaT[:, 2 * f:2 * f + 2, i * P:(i + 1) * P], bank[6][:, 0:256].rearrange("p (a n) -> p a n", a=2)) \
                        .then_inc(b_ytev, 1)

                fox_max(16 * f)
                for u in range(16 * f, 16 * f + 16):
                    i, h = u // 4 % 4, u % 4
                    if u + 1 < 16 * f + 16:
                        fox_max(u + 1)
                    dve.wait_ge(b_pt, u + 1)
                    if u >= 2:
                        dve.wait_ge(b_o, u - 1)
                    nc.vector.tensor_copy(PT[0:META, u % 2, 4 * P:5 * P], bank[5][0:META, 0:P]).then_inc(b_ptd, 1)
                    if h == 0 and u > 16 * f:
                        fox_gate(u // 4 - 1)
                    if h == 2 and u > 16 * f + 2:
                        fox_keep(u // 4 - 1)
                fox_gate(4 * f + 3)
                fox_keep(4 * f + 3)

            for cb in range(4):
                for k, (kind, gate) in enumerate((("ps", gsb), ("pa", gab))):
                    t = T_OF[(kind, cb)]
                    dve.wait_ge(m_gate, 2 * cb + k + 1)
                    for j in range(2):
                        dve.wait_ge(tile_done, 2 * t + 1 + j)
                        if k == 0:
                            m = nc.vector.tensor_tensor(mg[:, 2 * cb + j, :], gate[:, j, :], bank[3 * (t % 2) + j], ALU.mult)
                        else:
                            link(nc.vector.tensor_tensor(gate[:, j, :], gate[:, j, :], bank[3 * (t % 2) + j], ALU.mult))
                            link.wait()
                            dve.wait_ge(m_mix, 2 * cb + 1)
                            m = nc.vector.tensor_tensor(mg[:, 2 * cb + j, :], mg[:, 2 * cb + j, :], gate[:, j, :], ALU.add)
                        if j == 0:
                            link(m)
                    m.then_inc(m_mix, 1)
            dve.wait_ge(o_act, 4)
            junk = mg[:].rearrange("p a n -> p (a n)")
            dve.wait_ge(tile_done, 2 * T_OF[("wo", 3)] + 2)
            for i in range(NT):
                nc.vector.tensor_tensor_reduce(junk[:, D * i:D * i + D], orow[:, i, :], orow[:, i, :], 1.0, 0.0, ALU.mult, ALU.add, stt4[:, i:i + 1]) \
                    .then_inc(o_ss, 1)
            dve.wait_ge(o_rs, 1)
            for i in range(NT):
                link(nc.vector.scalar_tensor_tensor(out=orow[:, i, :], in0=orow[:, i, :], scalar=stt4[:, 4 + i:5 + i], in1=gpost[:],
                                               op0=ALU.mult, op1=ALU.mult))
                link.wait()
                for j in range(2):
                    dve.wait_ge(o_xt, 2 * i + j + 1)
                    nc.vector.tensor_tensor(orow[:, i, 512 * j:512 * j + 512], orow[:, i, 512 * j:512 * j + 512], bank[6 + j], ALU.add) \
                        .then_inc(o_fin, 1)

        @block.gpsimd
        def _(pool):
            if stage < 4:
                return
            pool.wait_ge(r_res, 64)
            nc.gpsimd.memset(cin[:, :, 0:3], 0.0).then_inc(d_zero, 1)
            nc.gpsimd.memset(dtr[:], 0.0).then_inc(d_zero, 1)

            def wide(x, n, k):
                return x.unsqueeze(2).broadcast_to([n, 8, k])

            def heads(x):
                return x.rearrange("p (h d) -> p h d", h=8)

            pool.wait_ge(d_dec, 1)
            for g in range(SG):
                hs = slice(8 * g, 8 * g + 8)

                def decays(i):
                    n = 4 * g + i
                    if n:
                        pool.wait_ge(e_seg, n)
                    else:
                        pool.wait_ge(d_adt, 1)
                    nc.gpsimd.tensor_tensor(lseg[:, 0:8 * P].rearrange("p (h s) -> p h s", h=8), wide(adt[:, i, hs], P, P),
                                            lower.unsqueeze(1).broadcast_to([P, 8, P]), ALU.mult).then_inc(p_lseg, 1)

                decays(0)
                pool.wait_ge(c_tev, 4 + 8 * g + 8)
                if g:
                    pool.wait_ge(e_st, 4 * g)
                    pool.wait_ge(e_y, 4 * g)
                nc.gpsimd.tensor_tensor(heads(xdt[0:META, 0, :]), heads(xrow[0:META, 4, :]), wide(dtv[0:META, 4, hs], META, 64), ALU.mult) \
                    .then_inc(p_xdt, 1)
                pool.wait_ge(p_xdt, 5 * g + 1)
                nc.gpsimd.tensor_tensor(heads(xds[0:META, :]), heads(xdt[0:META, 0, :]), wide(dec[0:META, 320 + 8 * g:328 + 8 * g], META, 64), ALU.mult) \
                    .then_inc(p_xds, 1)
                for i in range(NT):
                    n = 4 * g + i
                    if i >= 2:
                        pool.wait_ge(e_y, n - 1)
                    if i == 1:
                        pool.wait_ge(p_xds, n)
                    nc.gpsimd.tensor_tensor(heads(xdt[:, (i + 1) % 2, :]), heads(xrow[:, i, :]), wide(dtv[:, i, hs], P, 64), ALU.mult) \
                        .then_inc(p_xdt, 1)
                    if i < 3:
                        pool.wait_ge(p_xdt, 5 * g + i + 2)
                        pool.wait_ge(e_st, n + 1)
                        c = 128 + 32 * i + 8 * g
                        nc.gpsimd.tensor_tensor(heads(xds[:]), heads(xdt[:, (i + 1) % 2, :]), wide(dec[:, c:c + 8], P, 64), ALU.mult) \
                            .then_inc(p_xds, 1)
                    if n:
                        pool.wait_ge(e_gated, n)
                    nc.gpsimd.tensor_tensor(heads(xd[:]), heads(xrow[:, i, :]), wide(dskip[:, hs], P, 64), ALU.mult).then_inc(p_xd, 1)
                    if i + 1 < NT:
                        decays(i + 1)
            pool.wait_ge(e_tev, 16)
            nc.gpsimd.memset(qA[DH:DH + 2, :, :], 1.0).then_inc(b_one, 1)
            nc.gpsimd.memset(kA[DH:DH + 2, :, :], 1.0).then_inc(b_one, 1)
            pool.wait_ge(b_one, 2)
            for f in range(4):
                if f:
                    pool.wait_ge(b_s, 16 * f)
                pool.dma_start(kA[DH:DH + 1, :, :], ckT[4 * f:4 * f + 4, :]).then_inc(b_k, 16)
                pool.dma_start(qA[DH + 1:DH + 2, :, :], cqT[4 * f:4 * f + 4, :]).then_inc(b_q, 16)


INPUTS = ['x', 'c', 'ctx', 'c_ctx', 'w_ada', 'b_ada', 'norm_gain', 'ffn_w_in', 'ffn_w_out', 'fnet_w_out', 'fnet_b_out',
          'diff_w_in', 'diff_q_gain', 'diff_k_gain', 'diff_lambda', 'diff_subln_gain', 'diff_w_out',
          'meta_tokens_2', 'norm_pre_2', 'w_in_2', 'conv_w_2', 'conv_b_2', 'dt_bias_2', 'a_log_2', 'd_skip_2',
          'ssd_norm_2', 'fgate_bias_2', 'gate_bias_2', 'w_proj_ssd_2', 'w_proj_att_2', 'w_out_2', 'norm_post_2']
STAGE = 99


def kernel(**inputs):
    import concourse.bacc as bacc
    from concourse.bass_utils import run_bass_kernel_spmd

    nc = bacc.Bacc("TRN2", target_bir_lowering=False, num_devices=1)
    arrays, io = {}, {}
    for name in INPUTS:
        a = np.ascontiguousarray(inputs[name])
        arrays[f"in_{name}"] = a
        io[name] = nc.dram_tensor(f"in_{name}", a.shape, F32, kind="ExternalInput").ap()
    tables = []
    for name, a in zip(("table", "dft_lat", "dft_ctx"), constants()):
        arrays[name] = a
        tables.append(nc.dram_tensor(name, a.shape, F32, kind="ExternalInput").ap())
    out = nc.dram_tensor("out_0", (1, LAT, D), F32, kind="ExternalOutput").ap()
    dump = nc.dram_tensor("dump", (P, KC * ROWS), F32, kind="ExternalOutput").ap() if STAGE < 99 else None
    bass_two_blocks_kernel(nc, io, *tables, out, dump, STAGE)
    result = run_bass_kernel_spmd(nc, [arrays], core_ids=[0])
    return result.results[0]["out_0"]
```

```python
from contextlib import ExitStack

import numpy as np
import concourse.bass as bass
from concourse import mybir

F32 = mybir.dt.float32
F32R = mybir.dt.float32r
ALU = mybir.AluOpType
ACT = mybir.ActivationFunctionType
AX = mybir.AxisListType

P = 128
D = 1024
KC = D // P
LAT, CTX, META = 512, 256, 16
NT = LAT // P
ROWS = LAT + CTX
F = 2816
FC = F // P
GROUPS = [(0, 8), (8, 16), (16, FC)]
HEADS = 8
DH = 64
EPS = 1e-6
LAM_INIT = 0.8 - 0.6 * float(np.exp(-0.3))
SG = 4
COL_Z, COL_X, COL_B, COL_C, COL_DT = 0, 2048, 4096, 4608, 5120
COL_ZA, COL_Q, COL_K, COL_V, COL_F, COL_G = 5152, 6176, 7200, 8224, 9248, 9264
NR = 2
EARLY = 24
NS = 2
NEG = -1e30
ALL = META + LAT
LO = 272

ROW_C, ROW_CC, ROW_NG, ROW_FB, ROW_NP, ROW_SN, ROW_GB, ROW_SUB, ROW_QG, ROW_KG, N_A = 0, 8, 16, 48, 56, 64, 80, 96, 97, 98, 99
ROW_ADA, ROW_CB, N_B = 0, 96, 120
N_C = 96
(K_ID, K_ONE, K_BLK, K_UP, K_LOW, K_NEG, K_DFT, K_COS, K_SIN, N_K) = (0, 128, 256, 384, 512, 640, 768, 1024, 1536, 2048)


def constants():
    i = np.arange(P)
    k = np.zeros((P, N_K), np.float32)
    k[:, K_ID:K_ID + P] = np.eye(P)
    k[:, K_ONE:K_ONE + P] = 1.0
    k[:, K_BLK:K_BLK + P] = (i[:, None] // DH == i[None, :] // DH)
    k[:, K_UP:K_UP + P] = i[:, None] <= i[None, :]
    k[:, K_LOW:K_LOW + P] = i[:, None] > i[None, :]
    k[:, K_NEG:K_NEG + P] = np.where(i[None, :] > i[:, None], NEG, 0.0)
    a = 2 * np.pi * (np.outer(i, i) % P) / P
    k[:, K_DFT:K_DFT + P] = np.cos(a)
    k[:, K_DFT + P:K_DFT + 2 * P] = np.sin(a)
    row = np.repeat(np.arange(LAT // 64, dtype=np.float32), 64)
    col = np.tile(np.arange(64, dtype=np.float32), LAT // 64)
    nf = DH // 4
    inv = (np.float32(10000.0) ** (-np.arange(nf, dtype=np.float32) / np.float32(nf))).astype(np.float32)
    ang = np.concatenate([row[:, None] * inv, col[:, None] * inv], axis=-1).astype(np.float32).astype(np.float64).T
    k[:, K_COS:K_COS + LAT] = np.tile(np.cos(ang), (4, 1))
    k[:, K_SIN:K_SIN + LAT] = np.tile(np.concatenate([-np.sin(ang), np.sin(ang)]), (2, 1))

    def dft(n):
        j = np.arange(n)
        a = 2 * np.pi * (np.outer(j, j) % n) / n
        t = np.stack([np.cos(a), -np.sin(a)], axis=1) / np.sqrt(n * P)
        return np.ascontiguousarray(t.reshape(n // P, P, 2 * n).transpose(1, 0, 2).reshape(P, -1), np.float32)

    return k, dft(LAT), dft(CTX)


def stream_plan():
    plan = [("ada", 0, b) for b in range(8)]
    for g in range(KC):
        plan += [("ada", 0, 8 + 2 * g), ("ada", 0, 9 + 2 * g)]
    plan += [("fnet", cb) for cb in range(4)]
    for layer in range(2):
        late = []
        for lo, hi in GROUPS:
            units = [("in", layer, c) for c in range(lo, hi)] + [("down", layer, lo, cb) for cb in range(4)]
            for unit in units:
                plan += [unit] + late
                late = []
                if layer == 0 and unit[0] == "in":
                    late = [("ada", 1, unit[2])]
                elif (layer, hi) == (0, FC) and unit[3] < 2:
                    late = [("ada", 1, FC + unit[3])]
        if layer == 0:
            plan += [(w, cb) for w in ("dk", "dq", "dv") for cb in range(4)]
            plan += [("dout", cb) for cb in range(4)]
    for g in range(SG):
        plan += [("bc", g)] + ([("ps", g - 1, 0), ("ps", g - 1, 1)] if g else [])
        plan += [("xs", g, 0), ("xs", g, 1), ("z", g, 0), ("z", g, 1)]
    plan += [("ps", SG - 1, 0), ("ps", SG - 1, 1)]
    for f in range(4):
        plan += [("q", f), ("k", f), ("v", f), ("za", f)]
    for cb in range(4):
        plan += [("gs", cb), ("ga", cb), ("pa", cb)]
    plan += [("wo", cb) for cb in range(4)]
    return plan


def step_plan(plan):
    return [(key + (i,) if key[0] == "ps" else key) for key in plan if key[0] != "ada" for i in range(2 if key[0] == "ps" else 1)]


def bass_two_blocks_kernel(nc, io, kt_d, dl_d, dc_d, xsave, out):
    PLAN = stream_plan()
    N_OF = {key: n for n, key in enumerate(PLAN)}
    STEPS = step_plan(PLAN)
    T_OF = {key: t for t, key in enumerate(STEPS)}
    SPLIT = [key for key in PLAN if key[0] != "ada"]
    S_OF = {key: n for n, key in enumerate(SPLIT)}
    w_ada, w_in2 = io["w_ada"], io["w_in_2"][0]

    def source(key):
        kind = key[0]
        if kind == "ada":
            return w_ada[key[1]], 0, KC, 256 * key[2]
        if kind == "fnet":
            return io["fnet_w_out"][0], 0, KC, 256 * key[1]
        if kind == "down":
            _, layer, lo, cb = key
            return io["ffn_w_out"][layer], P * lo, dict(GROUPS)[lo] - lo, 256 * cb
        if kind in ("dq", "dk", "dv"):
            return io["diff_w_in"][0], 0, KC, {"dq": 0, "dk": D, "dv": 2 * D}[kind] + 256 * key[1]
        if kind == "dout":
            return io["diff_w_out"][0], 0, KC, 256 * key[1]
        if kind in ("xs", "z"):
            return w_in2, 0, KC, {"xs": COL_X, "z": COL_Z}[kind] + 512 * key[1] + 256 * key[2]
        if kind in ("q", "k", "v", "za"):
            return w_in2, 0, KC, {"q": COL_Q, "k": COL_K, "v": COL_V, "za": COL_ZA}[kind] + 256 * key[1]
        if kind in ("gs", "ga"):
            return w_in2, 0, KC, COL_G + (D if kind == "ga" else 0) + 256 * key[1]
        if kind == "pa":
            return io["w_proj_att_2"][0], 0, KC, 256 * key[1]
        return io["w_out_2"][0], 0, KC, 256 * key[1]

    with ExitStack() as ctx:
        here = [ctx]

        def sb(name, shape, dt=F32):
            return here[-1].enter_context(nc.sbuf_tensor(name, shape, dt))

        def sem(name):
            return ctx.enter_context(nc.semaphore(name))

        bank = [ctx.enter_context(nc.psum_tensor(f"bank{i}", [P, 512], F32)) for i in range(4, 8)]
        two = [ctx.enter_context(nc.psum_tensor(f"two{i}", [P, 1024], F32)) for i in range(2)]
        bank = [two[0][:, 0:512], two[0][:, 512:1024], two[1][:, 0:512], two[1][:, 512:1024]] + [b[:, :] for b in bank]

        kt = sb("kt", [P, N_K])
        ident, ones, blk = kt[:, K_ID:K_ID + P], kt[:, K_ONE:K_ONE + P], kt[:, K_BLK:K_BLK + P]
        upper, lower, negm = kt[:, K_UP:K_UP + P], kt[:, K_LOW:K_LOW + P], kt[:, K_NEG:K_NEG + P]
        dft128, cosT, sinT = kt[:, K_DFT:K_DFT + 2 * P], kt[:, K_COS:K_COS + LAT], kt[:, K_SIN:K_SIN + LAT]
        colA, colB, colC = sb("colA", [P, N_A]), sb("colB", [P, N_B]), sb("colC", [P, N_C])
        cond = sb("cond", [P, KC, 2])
        ada = [sb(f"ada{i}", [P, 48, 2]) for i in range(2)]
        mult = sb("mult", [P, 4, KC, 2])
        epsc = sb("epsc", [P, 1])
        metaT = sb("metaT", [P, KC, META])
        wdtf = sb("wdtf", [P, KC, 48])
        wd = (sb("wdH", [P, KC, 48], F32R), sb("wdL", [P, KC, 48], F32R))
        bdtf = sb("bdtf", [P, 48])
        alog = sb("alog", [P, 32])
        dskip = sb("dskip", [P, 32])
        lamv = sb("lamv", [P, 4 * DH])
        lamt = sb("lamt", [P, DH])
        lams = sb("lams", [P, 8])
        ring = sb("ring", [P, NR, KC, 256])

        def apart(name, shape):
            return sb(name + "H", shape, F32R), sb(name + "L", shape, F32R)

        def phase():
            s = ExitStack()
            here.append(s)
            return s

        def leave():
            here.pop().close()

        phase()
        early = sb("early", [P, 4, KC, 256])
        leave()
        wH, wL = apart("w", [P, NS, KC, 256])
        phase()
        xT = sb("xT", [P, KC, ROWS])
        adacc = sb("adacc", [P, 2, 2, 256])
        phase()
        sq0, rstd0 = sb("sq0", [P, 2, ROWS]), sb("rstd0", [P, ROWS])
        hT = sb("hT", [P, KC, ROWS])
        phase()
        xraw = sb("xraw", [P, 6, D])
        mraw = sb("mraw", [META, D])
        rowA, rowB, rowC = sb("rowA", [N_A, P]), sb("rowB", [N_B, P]), sb("rowC", [N_C, P])
        leave()
        yT = apart("yT", [P, KC, ROWS])
        dftL = sb("dftL", [P, NT, 2, LAT])
        dftC = sb("dftC", [P, 2, 2, CTX])
        fa = sb("fa", [P, 6, 256])
        gb = sb("gb", [P, KC, 2])
        leave()
        phase()
        sq1, rstd1 = sb("sq1", [P, 2, ROWS]), sb("rstd1", [P, ROWS])
        h1 = apart("h1", [P, KC, ROWS])
        hid = apart("hid", [P, 8, ROWS])
        gateS = sb("gateS", [P, 2, ROWS])
        leave()
        phase()
        kT = sb("kT", [P, HEADS, ROWS])
        qT = sb("qT", [P, HEADS, LAT])
        phase()
        sq2, rstd2 = sb("sq2", [P, 2, ROWS]), sb("rstd2", [P, ROWS])
        krot = sb("krot", [P, LAT])
        kraw = sb("kraw", [P, LAT])
        htmp = sb("htmp", [P, 2, ROWS])
        leave()
        V = sb("V", [P, 6, D])
        phase()
        h2 = apart("h2", [P, KC, ROWS])
        leave()
        prob = sb("prob", [P, 2, 2, ROWS])
        WT = sb("WT", [P, 6, LAT])
        sq3, rstd3 = sb("sq3", [P, 2, LAT]), sb("rstd3", [P, LAT])
        attmx = sb("attmx", [P, 2, 2, 4])
        aoL = sb("aoL", [P, HEADS, LAT], F32R)
        leave()
        phase()
        under_q = sb("under_q", [P, HEADS, ROWS])
        aoH = sb("aoH", [P, HEADS, LAT], F32R)
        leave()
        ao = (aoH, aoL)
        leave()
        here.append(ctx)
        phase()
        acc = sb("acc", [P, KC, LAT])
        zrow = sb("zrow", [P, 4, 512])
        un = apart("un", [P, KC, ALL])
        dtr = sb("dtr", [P, 5, 48])
        dtt = sb("dtt", [P, 4 * 240])
        dta, dtu, dtw, dtl = (dtt[:, 240 * k:240 * k + 240].rearrange("p (a n) -> p a n", a=5) for k in range(4))
        ysq = dtt[:, 0:512]
        dtv = sb("dtv", [P, 5, 32])
        logf = sb("logf", [P, 5, 16])
        expa = sb("expa", [P, 32])
        adt = sb("adt", [P, 5, 32])
        dec = sb("dec", [P, 352])
        ckT, cqT = sb("ckT", [16, ALL]), sb("cqT", [16, LAT])
        stt4 = sb("stt4", [P, 8])
        phase()
        sqb = sb("sqb", [P, 2, ALL])
        rstdb = sb("rstdb", [P, ALL])
        utmp = sb("utmp", [P, 2, ALL])
        dtT = sb("dtT", [48, ALL])
        leave()
        phase()
        xrow = sb("xrow", [P, 5, 512])
        Brow = sb("Brow", [P, 4, P])
        BT = sb("BT", [P, ALL])
        CTt = sb("CTt", [P, LAT])
        cin = sb("cin", [P, 2, ALL + 3])
        cacc = sb("cacc", [P, 2, ALL])
        xdt, xds = sb("xdt", [P, 2, 512]), sb("xds", [P, 512])
        xd = sb("xd", [P, 512])
        lseg = sb("lseg", [P, 8 * P])
        Mt = sb("Mt", [P, 2, 8, P])
        CBm = sb("CBm", [P, P])
        Hst = sb("Hst", [P, 2, 512])
        yrow = sb("yrow", [P, 2, 512])
        ysf = sb("ysf", [P, 4, P])
        ys = apart("ys", [P, 4, LAT])
        leave()
        phase()
        ya = apart("ya", [P, KC, LAT])
        phase()
        qA = sb("qA", [P, 4, LAT])
        kA = sb("kA", [P, 4, ALL])
        vA = sb("vA", [P, 5, 256])
        zA = sb("zA", [P, 4, 256])
        probA = sb("probA", [P, 2, ALL])
        PT = sb("PT", [P, 2, 5 * P])
        amx = sb("amx", [P, 2, 4])
        asum = sb("asum", [P, 4, 4])
        yA = sb("yA", [P, 256])
        leave()
        phase()
        mg = apart("mg", [P, KC, LAT])
        gsb, gab = sb("gsb", [P, 2, LAT]), sb("gab", [P, 2, LAT])
        leave()
        leave()
        leave()
        phase()
        under = sb("under", [P, 6144])
        orow = sb("orow", [P, 4, D])
        xback = sb("xback", [P, KC, LAT])
        gpost = sb("gpost", [P, D])
        leave()

        s_load, s_tab, s_x = sem("s_load"), sem("s_tab"), sem("s_x")
        s_x2, s_dft, s_small = sem("s_x2"), sem("s_dft"), sem("s_small")
        ring_ready = [sem(f"ring_ready{i}") for i in range(NR + 4)]
        s_cols_t, s_cols = sem("s_cols_t"), sem("s_cols")
        s_cond, s_xt, s_xlat, s_xctx, s_meta_t, s_meta = sem("s_cond"), sem("s_xt"), sem("s_xlat"), sem("s_xctx"), sem("s_meta_t"), sem("s_meta")
        ada_done, ada_taken, s_mult = sem("ada_done"), sem("ada_taken"), sem("s_mult")
        n_sq, n_used, n_rstd, h_ready = sem("n_sq"), sem("n_used"), sem("n_rstd"), sem("h_ready")
        tile_done = sem("tile_done")
        f_a, f_acopy, f_y, f_ycopy = sem("f_a"), sem("f_acopy"), sem("f_y"), sem("f_ycopy")
        r_res = sem("r_res")
        g_silu, g_hid = sem("g_silu"), sem("g_hid")
        v_chain, a_chain = sem("v_chain"), sem("a_chain")
        w_hi, w_lo = sem("w_hi"), sem("w_lo")
        ada_acc = sem("ada_acc")
        d_dtT, d_dtc = sem("d_dtT"), sem("d_dtc")
        h_full, h_hi, g_full, g_hi = sem("h_full"), sem("h_hi"), sem("g_full"), sem("g_hi")
        o_post = sem("o_post")
        d_wd, x_out, x_back, m_ps, c_tevm, e_off = (sem(x) for x in ("d_wd", "x_out", "x_back", "m_ps", "c_tevm", "e_off"))
        e_full, e_hi, m_full, m_hi, b_yhi = (sem(x) for x in ("e_full", "e_hi", "m_full", "m_hi", "b_yhi"))
        f_ylo, a_of, a_ohi = sem("f_ylo"), sem("a_of"), sem("a_ohi")
        a_wtd = sem("a_wtd")
        k_sq, k_sum, k_rstd, k_norm, k_done = sem("k_sq"), sem("k_sum"), sem("k_rstd"), sem("k_norm"), sem("k_done")
        v_copy, v_copyd, s_lam, s_lamx = sem("v_copy"), sem("v_copyd"), sem("s_lam"), sem("s_lamx")
        a_s, a_max, a_exp, a_w, a_wt, a_wtc, a_pv, a_sq, a_ms, a_rs, a_o = (sem(x) for x in (
            "a_s", "a_max", "a_exp", "a_w", "a_wt", "a_wtc", "a_pv", "a_sq", "a_ms", "a_rs", "a_o"))

        (c_in, c_acc, c_out, c_t, c_tev, z_act, x_act, x_dve, m_gate, m_mix, o_act) = (sem(x) for x in (
            "c_in", "c_acc", "c_out", "c_t", "c_tev", "z_act", "x_act", "x_dve", "m_gate", "m_mix", "o_act"))
        (d_zero, d_raw, d_biased, d_u, d_w, d_ln, d_expa, d_adt, d_sums, d_dec, d_ct, d_cta) = (sem(x) for x in (
            "d_zero", "d_raw", "d_biased", "d_u", "d_w", "d_ln", "d_expa", "d_adt", "d_sums", "d_dec", "d_ct", "d_cta"))
        (p_lseg, p_xdt, p_xds, p_xd, e_seg, e_exp, e_cb, e_m, e_y, e_yoff, e_st, e_h, e_gated, e_un, e_t, e_tev) = (sem(x) for x in (
            "p_lseg", "p_xdt", "p_xds", "p_xd", "e_seg", "e_exp", "e_cb", "e_m", "e_y", "e_yoff", "e_st", "e_h",
            "e_gated", "e_un", "e_t", "e_tev"))
        (b_one, b_k, b_q, b_s, b_max, b_exp, b_pt, b_pta, b_ptd, b_o, b_y, b_yt, b_ytev) = (sem(x) for x in (
            "b_one", "b_k", "b_q", "b_s", "b_max", "b_exp", "b_pt", "b_pta", "b_ptd", "b_o", "b_y", "b_yt", "b_ytev"))
        (o_ss, o_rs, o_xt, o_fin, s_out) = (sem(x) for x in ("o_ss", "o_rs", "o_xt", "o_fin", "s_out"))

        block = ctx.enter_context(nc.Block())

        class Chain:

            def __init__(self, eng, s):
                self.eng, self.s, self.n = eng, s, 0

            def __call__(self, ins):
                self.n += 1
                ins.then_inc(self.s, 1)

            def wait(self):
                self.eng.wait_ge(self.s, self.n)

        SUMMED = [1, 3, 5, 7] + list(range(8, 48))

        def blocks_used(key):
            if key[0] == "ada":
                i = 24 * key[1] + key[2]
                return (ada_acc, SUMMED.index(i) + 1) if i in SUMMED else (ada_done, i + 1)
            return w_lo, S_OF[key] + 1

        def banks_read(t):
            key = STEPS[t]
            kind = key[0]
            if kind == "fnet":
                return [(r_res, 2 * key[1] + 2)]
            if kind == "in":
                return [(g_full, FC * key[1] + key[2] + 1)]
            if kind == "down":
                _, layer, lo, cb = key
                return [(r_res, (8, 40)[layer] + 8 * [a for a, _ in GROUPS].index(lo) + 2 * cb + 2)]
            if kind == "dout":
                return [(r_res, 32 + 2 * key[1] + 2)]
            if kind in ("dk", "dq"):
                return [(k_norm, (8 if kind == "dq" else 0) + 2 * key[1] + 2)]
            if kind == "dv":
                return [(v_copy, key[1] + 1), (v_copyd, key[1] + 1)]
            if kind in ("bc", "xs"):
                return [(c_in, conv_tile(key, 1) + 1)]
            if kind == "ps":
                return [(m_ps, 4 * key[1] + 2 * key[2] + key[3] + 1)]
            if kind == "z":
                return [(z_act, 2 * key[1] + key[2] + 1)]
            if kind in ("q", "k", "v"):
                i = 3 * key[1] + "qkv".index(kind) + 1
                return [(x_act, i), (x_dve, i)]
            if kind == "za":
                return [(z_act, 2 * SG + key[1] + 1)]
            if kind in ("gs", "ga"):
                return [(m_gate, 2 * key[1] + (kind == "ga") + 1)]
            if kind == "pa":
                return [(m_full, key[1] + 1)]
            if kind == "wo":
                return [(o_act, key[1] + 1)]
            raise KeyError(key)

        def conv_tile(key, j):
            return 6 * key[1] + (0 if key[0] == "bc" else 2 + 2 * key[2]) + j

        def halves(with_ctx):
            return [(0, LAT, 0), (LAT, ROWS, 1)] if with_ctx else [(0, LAT, 0)]

        NORM_SQ = {0: 0, 1: KC, 2: 2 * KC, 3: 3 * KC, 4: 4 * KC}

        def slot_of(n):
            return n % (NR + 4) if n < EARLY else (n - EARLY) % NR

        def slot(n):
            i = slot_of(n)
            return ring[:, i] if i < NR else early[:, i - NR]

        def before_in_slot(n):
            return max((m for m in range(n) if slot_of(m) == slot_of(n)), default=None)

        def last_tile(key):
            return 2 * T_OF[key + (1,) if key[0] == "ps" else key] + 2

        def arrived(n):
            return sum(32 if PLAN[m][0] in ("in", "bc") else 16 for m in range(n + 1) if slot_of(m) == slot_of(n))

        def split_block(n):
            key = SPLIT[n]
            kc = source(key)[2] if key[0] not in ("in", "bc", "ps") else KC
            return slot(N_OF[key])[:, 0:kc], wH[:, n % NS, 0:kc], wL[:, n % NS, 0:kc]

        @block.sync
        def _(sp):
            sp.dma_start(kt[:], kt_d).then_inc(s_load, 16)
            for i in range(4):
                sp.dma_start(xraw[:, i, :], io["x"][0, i * P:(i + 1) * P, :]).then_inc(s_x, 16)

            def stream(n):
                key = PLAN[n]
                before = before_in_slot(n)
                if before is not None:
                    sp.wait_ge(*blocks_used(PLAN[before]))
                to, ready = slot(n), ring_ready[slot_of(n)]
                if key[0] == "ps":
                    w = io["w_proj_ssd_2"][0][512 * key[1]:512 * key[1] + 512, 512 * key[2]:512 * key[2] + 512]
                    sp.dma_start(to.rearrange("p c n -> p (c n)").rearrange("p (k m) -> p k m", k=4),
                                 w.rearrange("(c p) n -> p c n", p=P)).then_inc(ready, 16)
                    return
                if key[0] in ("in", "bc"):
                    c = slice(2 * F) if key[0] == "in" else slice(COL_B, COL_B + 1024)
                    w = (io["ffn_w_in"][key[1]] if key[0] == "in" else w_in2)[:, c].rearrange("(c p) (h n) -> p c h n", p=P, h=2)
                    key = ("in", 0, key[-1])
                    for h in range(2):
                        sp.dma_start(to[:, :, P * h:P * h + P], w[:, :, h, P * key[2]:P * key[2] + P]) \
                            .then_inc(ready, 16)
                    return
                w, r0, kc, c0 = source(key)
                sp.dma_start(to[:, 0:kc, :],
                             w[r0:r0 + kc * P, c0:c0 + 256].rearrange("(c p) n -> p c n", p=P)) \
                    .then_inc(ready, 16)

            for i in range(2):
                sp.dma_start(xraw[:, 4 + i, :], io["ctx"][0, i * P:(i + 1) * P, :]).then_inc(s_x2, 16)
            sp.dma_start(mraw[:, :], io["meta_tokens_2"]).then_inc(s_x2, 16)
            sp.wait_ge(s_tab, 16 * 13)
            for n in range(8):
                stream(n)
            sp.dma_start(dftL[:].rearrange("p a b n -> p (a b n)"), dl_d).then_inc(s_dft, 16)
            sp.dma_start(dftC[:].rearrange("p a b n -> p (a b n)"), dc_d).then_inc(s_dft, 16)
            for n in range(8, len(PLAN)):
                stream(n)
                if n == N_OF[("xs", 0, 0)]:
                    sp.wait_ge(r_res, 64)
                    sp.dma_start(xsave, xT[:, :, 0:LAT]).then_inc(x_out, 16)
            sp.wait_ge(s_small, 16 * 7)
            sp.wait_ge(x_out, 16)
            sp.wait_ge(tile_done, 2 * T_OF[("pa", 3)] + 2)
            sp.dma_start(xback[:], xsave).then_inc(x_back, 16)
            sp.wait_ge(e_tev, 16)
            sp.dma_start(gpost[:], io["norm_post_2"].broadcast_to([P, D])).then_inc(o_post, 16)
            for i in range(NT):
                sp.wait_ge(o_fin, 2 * i + 2)
                sp.dma_start(out[0, i * P:(i + 1) * P, :], orow[:, i, :]).then_inc(s_out, 16)
            sp.wait_ge(s_out, 16 * NT)

        @block.tensor
        def _(pe):
            step = [0]

            def weights(key):
                n = N_OF[key]
                if key[0] != "ada":
                    pe.wait_ge(w_lo, S_OF[key] + 1)
                    return wH[:, S_OF[key] % NS], wL[:, S_OF[key] % NS]
                pe.wait_ge(ring_ready[slot_of(n)], arrived(n))
                return slot(n)

            def begin(key):
                t = step[0]
                assert STEPS[t] == key, (STEPS[t], key)
                step[0] += 1
                if t >= 2:
                    for w in banks_read(t - 2):
                        pe.wait_ge(*w)
                return t % 2

            def tile(s, half, parts, extra):
                n = len(parts)
                for i, (w, r, wait) in enumerate(parts):
                    if wait is not None:
                        pe.wait_ge(*wait)
                    m = nc.tensor.matmul(bank[3 * s + half], w, r[:, 0:LAT], start=i == 0, stop=i == n - 1)
                if extra:
                    for i, (w, r, _) in enumerate(parts):
                        m = nc.tensor.matmul(bank[3 * s + 2][:, 256 * half:256 * half + extra], w,
                                             r[:, LAT:LAT + extra], start=i == 0, stop=i == n - 1)
                m.then_inc(tile_done, 1)

            def exact(w, a, n, c, wait=None):
                parts = []
                for k in range(n):
                    on = (wait[0], wait[1] + k + 1) if wait else None
                    parts += [(w[0][:, k, c:c + P], a[0][:, k, :], on), (w[0][:, k, c:c + P], a[1][:, k, :], None),
                              (w[1][:, k, c:c + P], a[0][:, k, :], None)]
                return parts

            def ada_block(layer, b):
                w = weights(("ada", layer, b))
                i = 24 * layer + b
                assert i not in SUMMED
                if i >= 2:
                    pe.wait_ge(ada_taken, i - 1)
                for j in range(2):
                    for kc in range(KC):
                        m = nc.tensor.matmul(bank[6 + b % 2][:, 2 * j:2 * j + 2], w[:, kc, P * j:P * j + P],
                                             cond[:, kc, :], start=kc == 0, stop=kc == KC - 1)
                m.then_inc(ada_done, 1)

            def ada_reduce(layer, b):
                i = 24 * layer + b
                k = SUMMED.index(i)
                pe.wait_ge(ada_acc, k + 1)
                if i >= 2:
                    pe.wait_ge(ada_taken, i - 1)
                for j in range(2):
                    for c in range(2):
                        o = 4 * j + 2 * c
                        m = nc.tensor.matmul(bank[6 + b % 2][:, o:o + 2], adacc[:, k % 2, c, P * j:P * j + P], ones[:, 0:2],
                                             start=True, stop=True)
                m.then_inc(ada_done, 1)

            def norm_sums(i, with_ctx, chunks=range(KC)):
                sq = (sq0, sq1, sq2, sq1)[i]
                for kc in chunks:
                    pe.wait_ge(n_sq, NORM_SQ[i] + kc + 1)
                    if kc == 0 and i == 1:
                        pe.wait_ge(ada_taken, 24)
                    for a, b, half in halves(with_ctx):
                        m = nc.tensor.matmul(bank[6 + half][:, 0:b - a], ones, sq[:, kc % 2, a:b],
                                             start=kc == 0, stop=kc == KC - 1)
                    m.then_inc(n_used, 1)

            pe.wait_ge(s_load, 16)
            pe.wait_ge(s_tab, 16 * 13)
            nc.tensor.transpose(bank[0][:, 0:N_A], rowA[:, :], kt[0:N_A, K_ID:K_ID + N_A]).then_inc(s_cols_t, 1)
            nc.tensor.transpose(bank[1][:, 0:N_B], rowB[:, :], kt[0:N_B, K_ID:K_ID + N_B]).then_inc(s_cols_t, 1)
            nc.tensor.transpose(bank[2][:, 0:N_C], rowC[:, :], kt[0:N_C, K_ID:K_ID + N_C]).then_inc(s_cols_t, 1)
            pe.wait_ge(s_cond, 2)
            pe.wait_ge(s_x, 64)
            pe.wait_ge(s_x2, 48)
            pe.wait_ge(s_cols, 3)
            for kc in range(KC):
                if kc >= 2:
                    pe.wait_ge(s_xlat, kc - 1)
                    pe.wait_ge(s_xctx, kc - 1)
                for i in range(NT):
                    nc.tensor.transpose(bank[3 * (kc % 2)][:, i * P:(i + 1) * P], xraw[:, i, kc * P:(kc + 1) * P], ident)
                for i in range(2):
                    m = nc.tensor.transpose(bank[3 * (kc % 2) + 2][:, i * P:(i + 1) * P], xraw[:, 4 + i, kc * P:(kc + 1) * P], ident)
                m.then_inc(s_xt, 1)
            for kc in range(KC):
                m = nc.tensor.transpose(bank[1][:, kc * META:(kc + 1) * META], mraw[:, kc * P:(kc + 1) * P],
                                        kt[0:META, K_ID:K_ID + META])
            m.then_inc(s_meta_t, 1)
            norm_sums(0, True)
            pe.wait_ge(n_rstd, 2)
            for b in range(0, 8, 2):
                ada_block(0, b)
                ada_reduce(0, b + 1)

            def dft_features(g):
                pe.wait_ge(h_ready, g + 1)
                if g:
                    pe.wait_ge(f_acopy, 3 * g)
                    pe.wait_ge(f_y, 2 * g)
                else:
                    pe.wait_ge(s_xlat, KC)
                    pe.wait_ge(s_xctx, KC)
                    pe.wait_ge(s_meta, 1)
                for rt in range(6):
                    m = nc.tensor.matmul(bank[rt // 2][:, 256 * (rt % 2):256 * (rt % 2) + 256],
                                         hT[:, g, rt * P:(rt + 1) * P], dft128, start=True, stop=True)
                    if rt % 2:
                        m.then_inc(f_a, 1)

            def dft_rows(g):
                pe.wait_ge(f_acopy, 3 * g + 3)
                if g == 0:
                    pe.wait_ge(s_dft, 32)
                if g >= 2:
                    pe.wait_ge(f_ylo, 2 * (g - 1))
                lat, cx = bank[3 + g % 2], bank[5]
                for i in range(NT):
                    for j in range(2):
                        m = nc.tensor.matmul(lat, fa[:, i, P * j:P * j + P], dftL[:, i, j, :],
                                             start=i + j == 0, stop=i + j == NT)
                m.then_inc(f_y, 1)
                if g:
                    pe.wait_ge(f_ylo, 2 * g)
                for i in range(2):
                    for j in range(2):
                        m = nc.tensor.matmul(cx[:, 0:CTX], fa[:, 4 + i, P * j:P * j + P], dftC[:, i, j, :],
                                             start=i + j == 0, stop=i + j == 2)
                m.then_inc(f_y, 1)

            dft_features(0)
            for g in range(KC):
                if g:
                    ada_reduce(0, 6 + 2 * g)
                dft_rows(g)
                if g:
                    ada_reduce(0, 7 + 2 * g)
                if g + 1 < KC:
                    dft_features(g + 1)
            ada_reduce(0, 22)
            ada_reduce(0, 23)
            pe.wait_ge(f_ylo, 2 * KC)
            for cb in range(4):
                s = begin(("fnet", cb))
                w = weights(("fnet", cb))
                for j in range(2):
                    tile(s, j, exact(w, yT, KC, P * j), CTX)
                if cb:
                    norm_sums(1, True, (2 * cb - 2, 2 * cb - 1))

            def norm_sums4(chunks):
                for kc in chunks:
                    pe.wait_ge(n_sq, NORM_SQ[4] + kc + 1)
                    nc.tensor.matmul(bank[6], ones, sqb[:, kc % 2, 0:LAT], start=kc == 0, stop=kc == KC - 1)
                    nc.tensor.matmul(bank[7][:, 0:META], ones, sqb[:, kc % 2, LAT:ALL], start=kc == 0, stop=kc == KC - 1) \
                        .then_inc(n_used, 1)

            def ffn(layer, first_h):
                extra = CTX if layer == 0 else 0
                for lo, hi in GROUPS:
                    for c in range(lo, hi):
                        s = begin(("in", layer, c))
                        w = weights(("in", layer, c))
                        for half in range(2):
                            tile(s, half, exact(w, h1, KC, P * half, (h_ready, first_h) if c + half == 0 else None), extra)
                        if layer == 0 and c:
                            ada_reduce(1, c - 1)
                    for cb in range(4):
                        s = begin(("down", layer, lo, cb))
                        w = weights(("down", layer, lo, cb))
                        for j in range(2):
                            tile(s, j, exact(w, hid, hi - lo, P * j, (g_hid, FC * layer + lo) if cb + j == 0 else None), extra)
                        if (layer, hi) == (0, FC) and cb < 3:
                            ada_reduce(1, FC - 1 + cb)
                        if (layer, hi) == (1, FC) and cb:
                            norm_sums4((2 * cb - 2, 2 * cb - 1))

            norm_sums(1, True, (6, 7))
            pe.wait_ge(n_rstd, 4)
            ffn(0, KC)

            pe.wait_ge(ada_taken, 48)
            norm_sums(2, True)
            done = [0]

            def stat(i, with_ctx):
                pe.wait_ge(k_sq, i + 1)
                if i:
                    pe.wait_ge(k_rstd, i)
                else:
                    pe.wait_ge(n_rstd, 6)
                for a, b, half in halves(with_ctx):
                    m = nc.tensor.matmul(bank[6 + half][:, 0:b - a], blk, sq2[:, i % 2, a:b], start=True, stop=True)
                m.then_inc(k_sum, 1)

            for i, kind in enumerate(["dk"] * 8 + ["dq"] * 8):
                cb, j = (i % 8) // 2, i % 2
                if j == 0:
                    s = begin((kind, cb))
                    w = weights((kind, cb))
                tile(s, j, exact(w, h2, KC, P * j, (h_ready, 2 * KC) if i == 0 else None), CTX if kind == "dk" else 0)
                if i:
                    stat(i - 1, i - 1 < 8)
            for cb in range(4):
                s = begin(("dv", cb))
                w = weights(("dv", cb))
                for rt in range(6):
                    for k in range(3 * KC):
                        kc, a, b = k // 3, *((0, 0), (0, 1), (1, 0))[k % 3]
                        m = nc.tensor.matmul(bank[3 * s + rt // 2][:, 256 * (rt % 2):256 * (rt % 2) + 256],
                                             h2[a][:, kc, rt * P:(rt + 1) * P], w[b][:, kc, :], start=k == 0, stop=k == 3 * KC - 1)
                m.then_inc(tile_done, 2)
                if cb == 0:
                    stat(15, False)
            for cb in (2, 3):
                for w in banks_read(T_OF[("dv", cb)]):
                    pe.wait_ge(*w)
            pe.wait_ge(k_done, 16)
            pe.wait_ge(k_rstd, 16)

            def scores(u):
                h, i = u // NT, u % NT
                for c in range(2):
                    if u:
                        pe.wait_ge(a_exp, 2 * (u - 1) + c + 1)
                    r = slice(DH * c, DH * c + DH)
                    nc.tensor.matmul(two[c][:, 0:LAT], qT[r, h, i * P:(i + 1) * P], kT[r, h, 0:LAT], start=True, stop=True)
                    nc.tensor.matmul(two[c][:, LAT:ROWS], qT[r, h, i * P:(i + 1) * P], kT[r, h, LAT:ROWS],
                                     start=True, stop=True).then_inc(a_s, 1)

            def turn(u):
                pe.wait_ge(a_w, u + 1)
                for c in range(2):
                    if u:
                        pe.wait_ge((a_wtc, a_wtd)[c], u)
                    for i in range(3):
                        m = nc.tensor.transpose(bank[4 + c][:, i * P:(i + 1) * P], prob[:, u % 2, 1, (3 * c + i) * P:(3 * c + i + 1) * P], ident)
                    m.then_inc(a_wt, 1)

            def head_stat(h):
                pe.wait_ge(a_sq, h + 1)
                if h:
                    pe.wait_ge(a_rs, h)
                nc.tensor.matmul(bank[7], ones, sq3[:, h % 2, 0:LAT], start=True, stop=True).then_inc(a_ms, 1)

            def head_product(h):
                pe.wait_ge(a_wtc, NT * h + NT)
                pe.wait_ge(a_wtd, NT * h + NT)
                if h:
                    pe.wait_ge(a_o, h)
                for k in range(6):
                    m = nc.tensor.matmul(bank[6], V[:, k, h * P:(h + 1) * P], WT[:, k, :], start=k == 0, stop=k == 5)
                m.then_inc(a_pv, 1)

            def after(u):
                turn(u)
                h, i = u // NT, u % NT
                if i == 0 and h:
                    head_product(h - 1)
                if i == 2 and h:
                    head_stat(h - 1)

            scores(0)
            for u in range(4 * HEADS):
                if u + 1 < 4 * HEADS:
                    scores(u + 1)
                if u:
                    after(u - 1)
            after(4 * HEADS - 1)
            head_product(HEADS - 1)
            head_stat(HEADS - 1)
            pe.wait_ge(a_exp, 8 * HEADS)
            pe.wait_ge(a_wtc, 4 * HEADS)
            pe.wait_ge(a_wtd, 4 * HEADS)
            pe.wait_ge(a_o, HEADS)
            for cb in range(4):
                s = begin(("dout", cb))
                w = weights(("dout", cb))
                for j in range(2):
                    tile(s, j, exact(w, ao, KC, P * j), 0)
                if cb:
                    norm_sums(3, False, (2 * cb - 2, 2 * cb - 1))
            norm_sums(3, False, (6, 7))
            ffn(1, 3 * KC)

            norm_sums4((6, 7))
            pe.wait_ge(n_rstd, 9)
            pe.wait_ge(s_small, 16 * 7)
            pe.wait_ge(d_wd, 2)
            for k in range(3 * KC):
                kc, a, b = k // 3, *((0, 0), (0, 1), (1, 0))[k % 3]
                if k % 3 == 0:
                    pe.wait_ge(h_ready, 4 * KC + kc + 1)
                nc.tensor.matmul(bank[6][0:48, 0:LO], wd[b][:, kc, :], un[a][:, kc, 0:LO], start=k == 0, stop=k == 3 * KC - 1)
                m = nc.tensor.matmul(bank[7][0:48, 0:256], wd[b][:, kc, :], un[a][:, kc, LO:ALL], start=k == 0, stop=k == 3 * KC - 1)
            m.then_inc(d_dtT, 1)

            LAT_ROWS = ((META, ALL, False),)
            WITH_META = ((0, LO, False), (LO, ALL, True))
            PLAIN = ((0, LAT, False),)

            def gemm(key, a=un, pieces=LAT_ROWS):
                s = begin(key)
                w = weights(key)
                for j in range(2):
                    for lo, hi, third in pieces:
                        o = bank[3 * s + 2][:, 256 * j:256 * j + hi - lo] if third else bank[3 * s + j][:, 0:hi - lo]
                        for k in range(3 * KC):
                            kc, x, y = k // 3, *((0, 0), (0, 1), (1, 0))[k % 3]
                            m = nc.tensor.matmul(o, w[y][:, kc, P * j:P * j + P], a[x][:, kc, lo:hi], start=k == 0, stop=k == 3 * KC - 1)
                    m.then_inc(tile_done, 1)

            def rows_gemm(key, a, base, extra):
                s = begin(key)
                w = weights(key)
                for i in range(NT + (extra > 0)):
                    r = slice(base + i * P, base + (i + 1) * P) if i < NT else slice(0, extra)
                    for k in range(3 * KC):
                        kc, x, y = k // 3, *((0, 0), (0, 1), (1, 0))[k % 3]
                        m = nc.tensor.matmul(bank[3 * s + i // 2][0:r.stop - r.start, 256 * (i % 2):256 * (i % 2) + 256],
                                             a[x][:, kc, r], w[y][:, kc, :], start=k == 0, stop=k == 3 * KC - 1)
                m.then_inc(tile_done, 2)

            def b_rows(g):
                pe.wait_ge(c_out, 6 * g + 1)
                if g:
                    pe.wait_ge(e_full, 4 * g)
                else:
                    pe.wait_ge(d_cta, 1)
                for i in range(3):
                    nc.tensor.transpose(bank[6][:, i * P:(i + 1) * P], BT[:, META + i * P:META + (i + 1) * P], ident)
                nc.tensor.transpose(bank[6][0:META, 3 * P:4 * P], BT[:, 0:META], ident).then_inc(c_t, 1)

            def project(g):
                pe.wait_ge(e_tev, 4 * g + 4)
                for b in range(2):
                    w = [x.rearrange("p c n -> p (c n)").rearrange("p (k m) -> p k m", k=4) for x in weights(("ps", g, b))]
                    for part in range(2):
                        s = begin(("ps", g, b, part))
                        for j in range(2):
                            tile(s, j, exact(w, ys, 4, 256 * part + P * j), 0)

            pe.wait_ge(n_rstd, 9)
            gemm(("bc", 0), un, WITH_META)
            pe.wait_ge(d_dtc, 1)
            for i in range(5):
                r = slice(META + i * P, META + (i + 1) * P) if i < 4 else slice(0, META)
                m = nc.tensor.transpose(bank[6][0:r.stop - r.start, 48 * i:48 * i + 48], dtT[:, r], kt[0:48, K_ID:K_ID + 48])
            m.then_inc(d_raw, 1)
            gemm(("xs", 0, 0), un, WITH_META)
            pe.wait_ge(d_adt, 1)
            for i in range(NT):
                nc.tensor.matmul(bank[6][:, 32 * i:32 * i + 32], upper, adt[:, i, :], start=True, stop=True)
            for i in range(3):
                nc.tensor.matmul(bank[6][:, 128 + 32 * i:160 + 32 * i], lower, adt[:, i, :], start=True, stop=True)
            for i in range(3):
                nc.tensor.matmul(bank[6][:, 224 + 32 * i:256 + 32 * i], ones, adt[:, i, :], start=True, stop=True)
            nc.tensor.matmul(bank[6][0:META, 320:352], lower[0:META, 0:META], adt[0:META, 4, :], start=True, stop=True).then_inc(d_sums, 1)
            for i in range(NT):
                c = slice(i * P, (i + 1) * P)
                nc.tensor.matmul(bank[7][0:16, c], logf[0:META, 4, :], ones[0:META, :], start=True, stop=False)
                for j in range(i):
                    nc.tensor.matmul(bank[7][0:16, c], logf[:, j, :], ones, start=False, stop=False)
                nc.tensor.matmul(bank[7][0:16, c], logf[:, i, :], upper, start=False, stop=True)
            def turn_inputs(g, tiles):
                for j in tiles:
                    i = 6 * g + 2 + j
                    pe.wait_ge(c_out, i + 1)
                    pe.wait_ge(c_tev, 5 * g + 1 + j)
                    if g + j:
                        pe.wait_ge(c_tevm, 4 * g + j)
                    for k in range(NT):
                        nc.tensor.transpose(bank[6][:, k * P:(k + 1) * P], cacc[:, i % 2, META + k * P:META + (k + 1) * P], ident)
                    nc.tensor.transpose(bank[7][0:META, 0:P], cacc[:, i % 2, 0:META], ident).then_inc(c_t, 1)

            def ssd(g):
                n0 = 4 * g
                for w in banks_read(T_OF[("z", g, 0)]) + banks_read(T_OF[("z", g, 1)]):
                    pe.wait_ge(*w)
                pe.wait_ge(c_tev, 5 * g + 5)
                pe.wait_ge(c_tevm, 4 * g + 4)
                pe.wait_ge(p_xds, n0 + 1)
                nc.tensor.matmul(bank[5], Brow[0:META, 3, :], xds[0:META, :], start=True, stop=True).then_inc(e_st, 1)

                def segments(i):
                    pe.wait_ge(p_lseg, n0 + i + 1)
                    if i:
                        pe.wait_ge(e_exp, n0 + i)
                    for h in range(8):
                        m = nc.tensor.matmul(two[0][:, h * P:(h + 1) * P], lseg[:, h * P:(h + 1) * P], upper, start=True, stop=True)
                    m.then_inc(e_seg, 1)

                def products(i):
                    if i:
                        pe.wait_ge(e_m, n0 + i)
                    nc.tensor.matmul(bank[2][:, 0:P], BT[:, META + i * P:META + (i + 1) * P], CTt[:, i * P:(i + 1) * P],
                                     start=True, stop=True).then_inc(e_cb, 1)

                def back(n):
                    pe.wait_ge(e_un, n + 1)
                    if n:
                        pe.wait_ge(e_full, n)
                    for j in range(4):
                        m = nc.tensor.transpose(bank[6][:, j * P:(j + 1) * P], yrow[:, n % 2, j * P:(j + 1) * P], ident)
                    m.then_inc(e_t, 1)

                segments(0)
                products(0)
                for i in range(NT):
                    n = n0 + i
                    pe.wait_ge(e_h, n + 1)
                    if i:
                        pe.wait_ge(e_off, n)
                    nc.tensor.matmul(bank[4], CTt[:, i * P:(i + 1) * P], Hst[:, i % 2, :], start=True, stop=True).then_inc(e_yoff, 1)
                    if i < 3:
                        pe.wait_ge(p_xds, n + 2)
                        nc.tensor.matmul(bank[5], Brow[:, i, :], xds[:, :], start=True, stop=True).then_inc(e_st, 1)
                        segments(i + 1)
                    if i:
                        pe.wait_ge(e_gated, n)
                    pe.wait_ge(p_xdt, 5 * g + i + 2)
                    pe.wait_ge(e_m, n + 1)
                    for h in range(8):
                        m = nc.tensor.matmul(bank[3][:, 64 * h:64 * h + 64], Mt[:, i % 2, h, :], xdt[:, (i + 1) % 2, 64 * h:64 * h + 64],
                                             start=True, stop=True)
                    m.then_inc(e_y, 1)
                    if i < 3:
                        products(i + 1)
                    if i:
                        back(n - 1)
                back(n0 + 3)

            for g in range(SG):
                if g:
                    pe.wait_ge(e_gated, 4 * g)
                    gemm(("bc", g), un, WITH_META)
                    project(g - 1)
                else:
                    pe.wait_ge(d_dec, 1)
                    nc.tensor.matmul(bank[6][0:16, 0:META], logf[0:META, 4, :], upper[0:META, 0:META], start=True, stop=True).then_inc(d_ct, 1)
                if g:
                    gemm(("xs", g, 0), un, WITH_META)
                b_rows(g)
                gemm(("xs", g, 1), un, WITH_META)
                turn_inputs(g, (0, 1))
                rows_gemm(("z", g, 0), un, META, 0)
                turn_inputs(g, (2, 3))
                rows_gemm(("z", g, 1), un, META, 0)
                ssd(g)
            pe.wait_ge(e_gated, 4 * SG)
            project(SG - 1)

            def spans(i):
                n = META + (i + 1) * P
                return [(0, min(n, 512))] + ([(512, n)] if n > 512 else [])

            def fox_scores(u):
                f, i, h = u // 16, u // 4 % 4, u % 4
                S = two[u % 2]
                if u >= 2:
                    pe.wait_ge(b_exp, u - 1)
                n = META + (i + 1) * P
                for a, b in spans(i):
                    nc.tensor.matmul(S[:, a:b], qA[0:DH + 2, h, i * P:(i + 1) * P], kA[0:DH + 2, h, a:b], start=True, stop=False)
                    o = max(a, n - P)
                    m = nc.tensor.matmul(S[:, o:b], ident, negm[:, o - (n - P):b - (n - P)], start=False, stop=True)
                m.then_inc(b_s, 1)

            def fox_turn(u):
                f, i, h = u // 16, u // 4 % 4, u % 4
                pe.wait_ge(b_exp, u + 1)
                if u:
                    pe.wait_ge(b_pta, u)
                    pe.wait_ge(b_ptd, u)
                for j in range(i + 1):
                    nc.tensor.transpose(bank[4][:, j * P:(j + 1) * P], probA[:, u % 2, META + j * P:META + (j + 1) * P], ident)
                nc.tensor.transpose(bank[5][0:META, 0:P], probA[:, u % 2, 0:META], ident).then_inc(b_pt, 1)

            def fox_out(u):
                f, i, h = u // 16, u // 4 % 4, u % 4
                pe.wait_ge(b_pta, u + 1)
                pe.wait_ge(b_ptd, u + 1)
                if h == 0 and u:
                    pe.wait_ge(b_y, u // 4)
                o = bank[7][:, 64 * h:64 * h + 64]
                nc.tensor.matmul(o, PT[0:META, u % 2, 4 * P:5 * P], vA[0:META, 4, 64 * h:64 * h + 64], start=True, stop=False)
                for j in range(i + 1):
                    m = nc.tensor.matmul(o, PT[:, u % 2, j * P:(j + 1) * P], vA[:, j, 64 * h:64 * h + 64], start=False, stop=j == i)
                m.then_inc(b_o, 1)

            def fox_back(v):
                pe.wait_ge(b_y, v + 1)
                if v:
                    pe.wait_ge(b_ytev, v)
                for j in range(2):
                    m = nc.tensor.transpose(bank[6][:, j * P:(j + 1) * P], yA[:, j * P:(j + 1) * P], ident)
                m.then_inc(b_yt, 1)

            for f in range(4):
                if f:
                    pe.wait_ge(b_exp, 16 * f)
                    pe.wait_ge(b_pta, 16 * f)
                    pe.wait_ge(b_ptd, 16 * f)
                gemm(("q", f))
                gemm(("k", f), un, WITH_META)
                rows_gemm(("v", f), un, META, META)
                rows_gemm(("za", f), un, META, 0)
                pe.wait_ge(b_q, 16 * (f + 1))
                pe.wait_ge(b_k, 16 * (f + 1))
                for w in sum((banks_read(T_OF[(k, f)]) for k in ("k", "v", "za")), []):
                    pe.wait_ge(*w)
                fox_scores(16 * f)
                for u in range(16 * f, 16 * f + 16):
                    if u + 1 < 16 * f + 16:
                        fox_scores(u + 1)
                    fox_turn(u)
                    if u > 16 * f:
                        fox_out(u - 1)
                    if u % 4 == 1 and u > 16 * f + 1:
                        fox_back(u // 4 - 1)
                fox_out(16 * f + 15)
                fox_back(4 * f + 3)

            pe.wait_ge(b_exp, 64)
            pe.wait_ge(b_pta, 64)
            pe.wait_ge(b_ptd, 64)
            pe.wait_ge(b_ytev, 16)
            for cb in range(4):
                gemm(("gs", cb))
                gemm(("ga", cb))
                gemm(("pa", cb), ya, PLAIN)
            pe.wait_ge(m_mix, 4)
            for cb in range(4):
                rows_gemm(("wo", cb), mg, 0, 0)
            pe.wait_ge(x_back, 16)
            for i in range(2 * NT):
                if i >= 2:
                    pe.wait_ge(o_fin, i - 1)
                for j in range(4):
                    m = nc.tensor.transpose(bank[6 + i % 2][:, j * P:(j + 1) * P],
                                            xback[:, 4 * (i % 2) + j, (i // 2) * P:(i // 2 + 1) * P], ident)
                m.then_inc(o_xt, 1)

        @block.scalar
        def _(act):
            link = Chain(act, a_chain)
            def rows(dst, a, n, src):
                act.dma_start(dst[a:a + n, :], src).then_inc(s_tab, 16)

            rows(rowA, ROW_C, 8, io["c"].rearrange("a (m p) -> (a m) p", p=P))
            rows(rowA, ROW_CC, 8, io["c_ctx"].rearrange("(m p) -> m p", p=P))
            rows(rowA, ROW_NG, 32, io["norm_gain"].rearrange("a b (m p) -> (a b m) p", p=P))
            rows(rowA, ROW_FB, 8, io["fnet_b_out"].rearrange("a (m p) -> (a m) p", p=P))
            rows(rowA, ROW_NP, 8, io["norm_pre_2"].rearrange("a (m p) -> (a m) p", p=P))
            rows(rowA, ROW_SN, 16, io["ssd_norm_2"].rearrange("a (m p) -> (a m) p", p=P))
            rows(rowA, ROW_GB, 16, io["gate_bias_2"].rearrange("a (m p) -> (a m) p", p=P))
            rows(rowA, ROW_SUB, 1, io["diff_subln_gain"])
            rows(rowA, ROW_QG, 1, io["diff_q_gain"].rearrange("a b d -> a (b d)"))
            rows(rowA, ROW_KG, 1, io["diff_k_gain"].rearrange("a b d -> a (b d)"))
            act.dma_start(rowB[0:96, :], io["b_ada"].rearrange("a (m p) -> (a m) p", p=P)).then_inc(s_tab, 16)
            act.dma_start(rowB[96:120, :], io["conv_b_2"].rearrange("a (m p) -> (a m) p", p=P)).then_inc(s_tab, 16)
            act.dma_start(rowC[:, :], io["conv_w_2"].rearrange("a k (m p) -> (a k m) p", p=P)).then_inc(s_tab, 16)
            act.dma_start(lamv[:], io["diff_lambda"].rearrange("a b d -> a (b d)").broadcast_to([P, 4 * DH])).then_inc(s_small, 16)
            act.dma_start(wdtf[:, :, 0:32], w_in2[:, COL_DT:COL_DT + 32].rearrange("(c p) n -> p c n", p=P)).then_inc(s_small, 16)
            act.dma_start(wdtf[:, :, 32:48], w_in2[:, COL_F:COL_F + 16].rearrange("(c p) n -> p c n", p=P)).then_inc(s_small, 16)
            act.dma_start(bdtf[:, 0:32], io["dt_bias_2"].broadcast_to([P, 32])).then_inc(s_small, 16)
            act.dma_start(bdtf[:, 32:48], io["fgate_bias_2"].broadcast_to([P, 16])).then_inc(s_small, 16)
            act.dma_start(alog[:], io["a_log_2"].broadcast_to([P, 32])).then_inc(s_small, 16)
            act.dma_start(dskip[:], io["d_skip_2"].broadcast_to([P, 32])).then_inc(s_small, 16)

            act.wait_ge(s_cols_t, 3)
            for b, c, n in ((0, colA, N_A), (1, colB, N_B), (2, colC, N_C)):
                nc.scalar.activation(c[:], bank[b][:, 0:n], ACT.Copy).then_inc(s_cols, 1)
            act.wait_ge(s_cols, 3)
            for j, r in enumerate((ROW_C, ROW_CC)):
                nc.scalar.activation(cond[:, :, j], colA[:, r:r + 8], ACT.Silu).then_inc(s_cond, 1)
            for kc in range(KC):
                act.wait_ge(s_xt, kc + 1)
                nc.scalar.activation(xT[:, kc, LAT:ROWS], bank[3 * (kc % 2) + 2][:, 0:CTX], ACT.Copy).then_inc(s_xctx, 1)
            act.wait_ge(s_meta_t, 1)
            nc.scalar.activation(metaT[:].rearrange("p c r -> p (c r)"), bank[1][:, 0:P], ACT.Copy).then_inc(s_meta, 1)

            def split_hi(n):
                if n >= len(SPLIT):
                    return
                at = N_OF[SPLIT[n]]
                act.wait_ge(ring_ready[slot_of(at)], arrived(at))
                if n < NS:
                    act.wait_ge(ada_done, EARLY)
                if n >= NS:
                    act.wait_ge(tile_done, last_tile(SPLIT[n - NS]))
                raw, hi, _ = split_block(n)
                nc.scalar.activation(hi, raw, ACT.Copy).then_inc(w_hi, 1)

            def modulated_hi(i):
                if i == 0:
                    return
                h = h2 if i == 2 else h1
                end = LAT if i == 3 else ROWS
                tmp = htmp if i == 2 else gateS
                o = 24 * (i % 2)
                for kc in range(KC):
                    act.wait_ge(h_full, KC * (i - 1) + kc + 1)
                    for a, b, half in halves(i < 3):
                        m = nc.scalar.activation(h[0][:, kc, a:b], tmp[:, kc % 2, a:b], ACT.Identity, bias=ada[i // 2][:, o + kc, half:half + 1])
                        if i < 3 and not half:
                            link(m)
                    m.then_inc(h_hi, 1)

            def squares(i, with_ctx, chunks=range(KC)):
                end = ROWS if with_ctx else LAT
                sq = (sq0, sq1, sq2, sq1)[i]
                for kc in chunks:
                    if i:
                        act.wait_ge(r_res, (0, 0, 24, 32)[i] + kc + 1)
                    k = NORM_SQ[i] + kc
                    if k >= 2:
                        act.wait_ge(n_used, k - 1)
                    nc.scalar.activation(sq[:, kc % 2, 0:end], xT[:, kc, 0:end], ACT.Square).then_inc(n_sq, 1)

            def norm(i, with_ctx, chunks=range(KC)):
                sq, rstd = ((sq0, rstd0), (sq1, rstd1), (sq2, rstd2), (sq1, rstd1))[i]
                squares(i, with_ctx, chunks)
                act.wait_ge(n_used, NORM_SQ[i] + KC)
                for a, b, half in halves(with_ctx):
                    link(nc.scalar.activation(rstd[:, a:b], bank[6 + half][:, 0:b - a], ACT.Ln, bias=epsc[:], scale=1.0 / D))
                link.wait()
                for a, b, half in halves(with_ctx):
                    nc.scalar.activation(rstd[:, a:b], rstd[:, a:b], ACT.Exp, scale=-0.5).then_inc(n_rstd, 1)

            act.wait_ge(s_xlat, KC)
            act.wait_ge(s_xctx, KC)
            norm(0, True)

            for g in range(KC):
                for i in range(3):
                    act.wait_ge(f_a, 3 * g + i + 1)
                    if g and i == 0:
                        act.wait_ge(f_y, 2 * g)
                    nc.scalar.activation(fa[:, 2 * i:2 * i + 2, :].rearrange("p a n -> p (a n)"), bank[i], ACT.Copy).then_inc(f_acopy, 1)
                act.wait_ge(f_y, 2 * g + 1)
                nc.scalar.activation(yT[0][:, g, 0:LAT], bank[3 + g % 2], ACT.Copy).then_inc(f_ycopy, 1)
                act.wait_ge(f_y, 2 * g + 2)
                nc.scalar.activation(yT[0][:, g, LAT:ROWS], bank[5][:, 0:CTX], ACT.Copy).then_inc(f_ycopy, 1)
            for n in range(4 + NS):
                if n > NS:
                    squares(1, True, (2 * (n - NS) - 2, 2 * (n - NS) - 1))
                split_hi(n)

            def squares4(chunks):
                for kc in chunks:
                    act.wait_ge(r_res, 56 + kc + 1)
                    k = NORM_SQ[4] + kc
                    act.wait_ge(n_used, k - 1)
                    link(nc.scalar.activation(sqb[:, kc % 2, 0:LAT], xT[:, kc, 0:LAT], ACT.Square))
                    nc.scalar.activation(sqb[:, kc % 2, LAT:ALL], metaT[:, kc, :], ACT.Square).then_inc(n_sq, 1)

            def ffn(layer):
                for lo, hi in GROUPS:
                    for k in range(lo, hi):
                        t = T_OF[("in", layer, k)]
                        s, c = t % 2, FC * layer + k
                        act.wait_ge(tile_done, 2 * t + (2 if layer == 0 else 1))
                        if c >= 2:
                            act.wait_ge(g_hid, c - 1)
                        m = nc.scalar.activation(gateS[:, c % 2, 0:LAT], bank[3 * s], ACT.Silu)
                        if layer == 0:
                            link(m)
                            m = nc.scalar.activation(gateS[:, c % 2, LAT:ROWS], bank[3 * s + 2][:, 0:CTX], ACT.Silu)
                        m.then_inc(g_silu, 1)
                        end = ROWS if layer == 0 else LAT
                        act.wait_ge(g_full, c + 1)
                        nc.scalar.activation(hid[0][:, k - lo, 0:end], gateS[:, c % 2, 0:end], ACT.Copy).then_inc(g_hi, 1)
                        split_hi(S_OF[("in", layer, k)] + NS)
                    for cb in range(4):
                        if (layer, hi) == (1, FC) and cb:
                            squares4((2 * cb - 2, 2 * cb - 1))
                        split_hi(S_OF[("down", layer, lo, cb)] + NS)

            norm(1, True, (6, 7))
            modulated_hi(1)
            ffn(0)
            norm(2, True)
            modulated_hi(2)

            def stats(i):
                with_ctx = i < 8
                t, j = T_OF[("dk", 0)] + i // 2, i % 2
                act.wait_ge(tile_done, 2 * t + 2)
                if i >= 2:
                    act.wait_ge(k_sum, i - 1)
                else:
                    act.wait_ge(n_used, NORM_SQ[2] + KC)
                m = nc.scalar.activation(sq2[:, i % 2, 0:LAT], bank[3 * (t % 2) + j], ACT.Square)
                if with_ctx:
                    link(m)
                    m = nc.scalar.activation(sq2[:, i % 2, LAT:ROWS], bank[3 * (t % 2) + 2][:, 256 * j:256 * j + 256], ACT.Square)
                m.then_inc(k_sq, 1)

            def finish(i):
                with_ctx = i < 8
                act.wait_ge(k_sum, i + 1)
                if i:
                    act.wait_ge(k_norm, i)
                for a, b, half in halves(with_ctx):
                    link(nc.scalar.activation(rstd2[:, a:b], bank[6 + half][:, 0:b - a], ACT.Ln, bias=epsc[:], scale=1.0 / DH))
                link.wait()
                end = ROWS if with_ctx else LAT
                nc.scalar.activation(rstd2[:, 0:end], rstd2[:, 0:end], ACT.Exp, scale=-0.5).then_inc(k_rstd, 1)

            act.wait_ge(h_ready, 3 * KC)
            for i in range(16):
                stats(i)
                if i % 2:
                    split_hi(S_OF[("dk", 0)] + i // 2 + NS)
                    finish(i - 1)
                    finish(i)
            for cb in range(4):
                t = T_OF[("dv", cb)]
                act.wait_ge(tile_done, 2 * t + 2)
                act.wait_ge(k_done, 16)
                nc.scalar.activation(V[:, 2:4, 256 * cb:256 * cb + 256], bank[3 * (t % 2) + 1].rearrange("p (a n) -> p a n", a=2), ACT.Copy) \
                    .then_inc(v_copy, 1)
                split_hi(S_OF[("dv", cb)] + NS)

            def weights_of(u):
                for c in range(2):
                    act.wait_ge(a_max, 2 * u + c + 1)
                    if u >= 2:
                        act.wait_ge(a_wt, 2 * (u - 1))
                    nc.scalar.activation(prob[:, u % 2, c, :], two[c][:, 0:ROWS], ACT.Exp, bias=attmx[:, u % 2, c, 1:2],
                                         scale=DH ** -0.5, accum_out=attmx[:, u % 2, c, 2:3]).then_inc(a_exp, 1)

            def head_square(h):
                act.wait_ge(a_pv, h + 1)
                nc.scalar.activation(sq3[:, h % 2, 0:LAT], bank[6], ACT.Square).then_inc(a_sq, 1)

            def head_root(h):
                act.wait_ge(a_ms, h + 1)
                if h:
                    act.wait_ge(a_o, h)
                link(nc.scalar.activation(rstd3[:, 0:LAT], bank[7], ACT.Ln, bias=epsc[:], scale=1.0 / P))
                link.wait()
                nc.scalar.activation(rstd3[:, 0:LAT], rstd3[:, 0:LAT], ACT.Exp, scale=-0.5).then_inc(a_rs, 1)

            def head_hi(h):
                act.wait_ge(a_of, h + 1)
                nc.scalar.activation(aoH[:, h, :], sq3[:, h % 2, :], ACT.Copy).then_inc(a_ohi, 1)

            def keep_turned(u):
                h, i = u // NT, u % NT
                act.wait_ge(a_wt, 2 * u + 1)
                if i == 0 and h:
                    act.wait_ge(a_pv, h)
                nc.scalar.activation(WT[:, 0:3, i * P:(i + 1) * P], bank[4][:, 0:3 * P].rearrange("p (a n) -> p a n", a=3), ACT.Copy) \
                    .then_inc(a_wtc, 1)
                if i == 1 and h:
                    head_square(h - 1)
                if i == 2 and h:
                    head_root(h - 1)
                if i == 3 and h:
                    head_hi(h - 1)

            act.wait_ge(s_lam, 1)
            nc.scalar.activation(lams[:, 2:4], lams[:, 4:6], ACT.Exp).then_inc(s_lamx, 1)
            act.wait_ge(k_done, 16)
            weights_of(0)
            for u in range(4 * HEADS):
                if u + 1 < 4 * HEADS:
                    weights_of(u + 1)
                if u:
                    keep_turned(u - 1)
            keep_turned(4 * HEADS - 1)
            head_square(HEADS - 1)
            head_root(HEADS - 1)
            head_hi(HEADS - 1)
            for cb in range(4):
                if cb:
                    squares(3, False, (2 * cb - 2, 2 * cb - 1))
                split_hi(S_OF[("dout", cb)] + NS)
            norm(3, False, (6, 7))
            modulated_hi(3)
            ffn(1)

            squares4((6, 7))
            act.wait_ge(n_used, NORM_SQ[4] + KC)
            for a, b, half in ((0, LAT, 0), (LAT, ALL, 1)):
                link(nc.scalar.activation(rstdb[:, a:b], bank[6 + half][:, 0:b - a], ACT.Ln, bias=epsc[:], scale=1.0 / D))
            link.wait()
            for a, b in ((0, LAT), (LAT, ALL)):
                nc.scalar.activation(rstdb[:, a:b], rstdb[:, a:b], ACT.Exp, scale=-0.5).then_inc(n_rstd, 1)
            nc.scalar.activation(wd[0][:], wdtf[:], ACT.Copy).then_inc(d_wd, 1)
            for kc in range(KC):
                act.wait_ge(h_full, 3 * KC + kc + 1)
                nc.scalar.activation(un[0][:, kc, :], utmp[:, kc % 2, :], ACT.Copy).then_inc(h_hi, 1)
            act.wait_ge(d_dtT, 1)
            link(nc.scalar.activation(dtT[:, 0:LO], bank[6][0:48, 0:LO], ACT.Copy))
            nc.scalar.activation(dtT[:, LO:ALL], bank[7][0:48, 0:256], ACT.Copy).then_inc(d_dtc, 1)
            nc.scalar.activation(expa[:], alog[:], ACT.Exp).then_inc(d_expa, 1)
            act.wait_ge(d_biased, 1)
            nc.scalar.activation(dtu, dta, ACT.Exp, scale=-1.0).then_inc(d_u, 1)
            act.wait_ge(d_w, 1)
            nc.scalar.activation(dtl, dtw, ACT.Ln).then_inc(d_ln, 1)

            def conv(key):
                t = T_OF[key]
                b = bank[3 * (t % 2):3 * (t % 2) + 3]
                act.wait_ge(tile_done, 2 * t + 2)
                for j in range(2):
                    i = conv_tile(key, j)
                    if i >= 2:
                        act.wait_ge(c_acc, i - 1)
                    else:
                        act.wait_ge(d_zero, 1)
                    link(nc.scalar.activation(cin[:, i % 2, 3:3 + LO], b[j][:, 0:LO], ACT.Copy))
                    nc.scalar.activation(cin[:, i % 2, 3 + LO:3 + ALL], b[2][:, 256 * j:256 * j + 256], ACT.Copy).then_inc(c_in, 1)
                for j in range(2):
                    i = conv_tile(key, j)
                    ch = (16 + 4 * j + key[1]) if key[0] == "bc" else 4 * key[1] + 2 * key[2] + j
                    bias = colB[:, ROW_CB + ch:ROW_CB + ch + 1]
                    act.wait_ge(c_acc, i + 1)
                    if key[0] == "bc" and key[1] and j == 0:
                        act.wait_ge(e_y, 4 * key[1])
                    if key[0] == "xs":
                        m = nc.scalar.activation(cacc[:, i % 2, :], cacc[:, i % 2, :], ACT.Silu, bias=bias)
                    elif j == 0:
                        m = nc.scalar.activation(BT[:], cacc[:, i % 2, :], ACT.Silu, bias=bias)
                    else:
                        m = nc.scalar.activation(CTt[:], cacc[:, i % 2, META:ALL], ACT.Silu, bias=bias)
                    m.then_inc(c_out, 1)
                split_hi(S_OF[key] + NS)

            def gates(g, j):
                t = T_OF[("z", g, j)]
                act.wait_ge(tile_done, 2 * t + 2)
                if j == 0:
                    if g:
                        act.wait_ge(e_gated, 4 * g)
                    else:
                        act.wait_ge(x_out, 16)
                for i in range(2):
                    m = nc.scalar.activation(zrow[:, 2 * i:2 * i + 2, 256 * j:256 * j + 256],
                                             bank[3 * (t % 2) + i].rearrange("p (a n) -> p a n", a=2), ACT.Silu)
                    if i == 0:
                        link(m)
                m.then_inc(z_act, 1)
                split_hi(S_OF[("z", g, j)] + NS)

            act.wait_ge(d_sums, 1)
            link(nc.scalar.activation(dec[:, 0:320], bank[6][:, 0:320], ACT.Exp))
            nc.scalar.activation(dec[0:META, 320:352], bank[6][0:META, 320:352], ACT.Exp).then_inc(d_dec, 1)
            for g in range(SG):
                conv(("bc", g))
                if g == 0:
                    act.wait_ge(d_ct, 1)
                    link(nc.scalar.activation(ckT[:, META:ALL], bank[7][0:16, :], ACT.Copy, scale=-8.0))
                    link(nc.scalar.activation(cqT[:, :], bank[7][0:16, :], ACT.Copy, scale=8.0))
                    nc.scalar.activation(ckT[:, 0:META], bank[6][0:16, 0:META], ACT.Copy, scale=-8.0).then_inc(d_cta, 1)
                if g:
                    for b in range(2):
                        split_hi(S_OF[("ps", g - 1, b)] + NS)
                for j in range(2):
                    conv(("xs", g, j))
                    if j:
                        gates(g, 0)
                    for jj in range(2):
                        i = 2 * j + jj
                        act.wait_ge(c_t, 5 * g + 1 + i + 1)
                        nc.scalar.activation(xrow[0:META, 4, P * i:P * i + P], bank[7][0:META, 0:P], ACT.Copy).then_inc(c_tevm, 1)

                def decay_exp(i):
                    n = 4 * g + i
                    act.wait_ge(e_seg, n + 1)
                    if n >= 2:
                        act.wait_ge(e_y, n - 1)
                    nc.scalar.activation(Mt[:, i % 2].rearrange("p a n -> p (a n)"), two[0][:, :], ACT.Exp).then_inc(e_exp, 1)

                def ys_hi(n):
                    act.wait_ge(e_full, n + 1)
                    if g and n == 4 * g:
                        act.wait_ge(tile_done, last_tile(("ps", g - 1, 1)))
                    nc.scalar.activation(ys[0][:, :, (n % 4) * P:(n % 4 + 1) * P], ysf[:], ACT.Copy).then_inc(e_hi, 1)

                gates(g, 1)
                decay_exp(0)
                for i in range(NT):
                    n = 4 * g + i
                    if i + 1 < NT:
                        decay_exp(i + 1)
                    act.wait_ge(e_gated, n + 1)
                    link(nc.scalar.activation(ysq, yrow[:, i % 2, :], ACT.Square, accum_out=stt4[:, 0:1]))
                    link.wait()
                    link(nc.scalar.activation(stt4[:, 1:2], stt4[:, 0:1], ACT.Ln, bias=epsc[:], scale=1.0 / 512))
                    link.wait()
                    link(nc.scalar.activation(stt4[:, 2:3], stt4[:, 1:2], ACT.Exp, scale=-0.5))
                    link.wait()
                    nc.scalar.activation(yrow[:, i % 2, :], yrow[:, i % 2, :], ACT.Copy, scale=stt4[:, 2:3]).then_inc(e_un, 1)
                    if i:
                        ys_hi(n - 1)
                ys_hi(4 * g + 3)
            for b in range(2):
                split_hi(S_OF[("ps", SG - 1, b)] + NS)

            for f in range(4):
                t = T_OF[("q", f)]
                act.wait_ge(tile_done, 2 * t + 1)
                if f:
                    act.wait_ge(b_s, 16 * f)
                else:
                    act.wait_ge(m_ps, 16)
                link(nc.scalar.activation(qA[0:DH, 0, :], bank[3 * (t % 2)][0:DH, :], ACT.Copy))
                nc.scalar.activation(qA[0:DH, 1, :], bank[3 * (t % 2)][DH:P, :], ACT.Copy).then_inc(x_act, 1)
                split_hi(S_OF[("q", f)] + NS)
                t = T_OF[("k", f)]
                act.wait_ge(tile_done, 2 * t + 2)
                for h in range(4):
                    m = nc.scalar.activation(kA[0:DH, h, 0:LO], bank[3 * (t % 2) + h // 2][DH * (h % 2):DH * (h % 2) + DH, 0:LO], ACT.Copy)
                    if h < 3:
                        link(m)
                m.then_inc(x_act, 1)
                split_hi(S_OF[("k", f)] + NS)
                t = T_OF[("v", f)]
                act.wait_ge(tile_done, 2 * t + 2)
                if f:
                    act.wait_ge(b_o, 16 * f)
                nc.scalar.activation(vA[:, 0:2, :], bank[3 * (t % 2)].rearrange("p (a n) -> p a n", a=2), ACT.Copy).then_inc(x_act, 1)
                split_hi(S_OF[("v", f)] + NS)
                t = T_OF[("za", f)]
                act.wait_ge(tile_done, 2 * t + 2)
                if f:
                    act.wait_ge(b_y, 4 * f)
                link(nc.scalar.activation(zA[:, 0:2, :], bank[3 * (t % 2)].rearrange("p (a n) -> p a n", a=2), ACT.Silu))
                nc.scalar.activation(zA[:, 2:4, :], bank[3 * (t % 2) + 1].rearrange("p (a n) -> p a n", a=2), ACT.Silu).then_inc(z_act, 1)
                split_hi(S_OF[("za", f)] + NS)

                def fox_hi(v):
                    i = v % 4
                    act.wait_ge(b_yt, v + 1)
                    nc.scalar.activation(ya[0][:, 2 * f:2 * f + 2, i * P:(i + 1) * P], bank[6][:, 0:256].rearrange("p (a n) -> p a n", a=2), ACT.Copy) \
                        .then_inc(b_yhi, 1)

                def fox_exp(u):
                    i, h = u // 4 % 4, u % 4
                    n = META + (i + 1) * P
                    act.wait_ge(b_max, u + 1)
                    if u >= 2:
                        act.wait_ge(b_pt, u - 1)
                    if h == 0 and u >= 16:
                        act.wait_ge(b_y, u // 4 - 3)
                    nc.scalar.activation(probA[:, u % 2, 0:n], two[u % 2][:, 0:n], ACT.Exp, bias=amx[:, u % 2, 1:2],
                                         scale=DH ** -0.5, accum_out=asum[:, i, h:h + 1]).then_inc(b_exp, 1)

                fox_exp(16 * f)
                for u in range(16 * f, 16 * f + 16):
                    i = u // 4 % 4
                    if u + 1 < 16 * f + 16:
                        fox_exp(u + 1)
                    if u % 4 == 2 and u > 16 * f + 2:
                        fox_hi(u // 4 - 1)
                    act.wait_ge(b_pt, u + 1)
                    if u >= 2:
                        act.wait_ge(b_o, u - 1)
                    nc.scalar.activation(PT[:, u % 2, 0:(i + 1) * P], bank[4][:, 0:(i + 1) * P], ACT.Copy).then_inc(b_pta, 1)
                fox_hi(4 * f + 3)

            for cb in range(4):
                for k, (kind, dst) in enumerate((("gs", gsb), ("ga", gab))):
                    t = T_OF[(kind, cb)]
                    for j in range(2):
                        act.wait_ge(tile_done, 2 * t + 1 + j)
                        if cb:
                            act.wait_ge(m_mix, cb)
                        c = ROW_GB + 8 * k + 2 * cb + j
                        m = nc.scalar.activation(dst[:, j, :], bank[3 * (t % 2) + j], ACT.Sigmoid, bias=colA[:, c:c + 1])
                        if j == 0:
                            link(m)
                    m.then_inc(m_gate, 1)
                    split_hi(S_OF[(kind, cb)] + NS)
                split_hi(S_OF[("pa", cb)] + NS)
                act.wait_ge(m_full, cb + 1)
                nc.scalar.activation(mg[0][:, 2 * cb:2 * cb + 2, :], gsb[:], ACT.Copy).then_inc(m_hi, 1)
            for cb in range(4):
                t = T_OF[("wo", cb)]
                act.wait_ge(tile_done, 2 * t + 2)
                for i in range(2):
                    m = nc.scalar.activation(orow[:, 2 * i:2 * i + 2, 256 * cb:256 * cb + 256],
                                             bank[3 * (t % 2) + i].rearrange("p (a n) -> p a n", a=2), ACT.Copy)
                    if i == 0:
                        link(m)
                m.then_inc(o_act, 1)
                split_hi(S_OF[("wo", cb)] + NS)
            act.wait_ge(o_ss, 4)
            link(nc.scalar.activation(stt4[:, 4:8], stt4[:, 0:4], ACT.Ln, bias=epsc[:], scale=1.0 / D))
            link.wait()
            nc.scalar.activation(stt4[:, 4:8], stt4[:, 4:8], ACT.Exp, scale=-0.5).then_inc(o_rs, 1)

        @block.vector
        def _(dve):
            link = Chain(dve, v_chain)
            nc.vector.memset(epsc[:], EPS)
            for kc in range(KC):
                dve.wait_ge(s_xt, kc + 1)
                nc.vector.tensor_copy(xT[:, kc, 0:LAT], bank[3 * (kc % 2)]).then_inc(s_xlat, 1)

            def take_ada(layer, b):
                dve.wait_ge(ada_done, 24 * layer + b + 1)
                o = 48 * layer + 2 * b
                o2 = 2 if 24 * layer + b in SUMMED else 1
                src = bank[6 + b % 2][:, 0:4 * o2].rearrange("p (a n k) -> p a n k", a=2, k=o2)[:, :, :, 0]
                nc.vector.tensor_tensor(ada[layer][:, 2 * b:2 * b + 2, :], src,
                                        colB[:, o:o + 2].unsqueeze(2).broadcast_to([P, 2, 2]), ALU.add).then_inc(ada_taken, 1)

            def sum_ada(layer, b):
                i, n = 24 * layer + b, N_OF[("ada", layer, b)]
                k = SUMMED.index(i)
                dve.wait_ge(ring_ready[slot_of(n)], arrived(n))
                if k >= 2:
                    dve.wait_ge(ada_done, SUMMED[k - 2] + 1)
                w = slot(n)
                for kc in range(KC):
                    for c in range(2):
                        o, x = adacc[:, k % 2, c, :], cond[:, kc, c:c + 1]
                        if kc == 0:
                            m = nc.vector.tensor_scalar(o, w[:, kc, :], x, None, ALU.mult)
                        else:
                            dve.wait_ge(v_chain, link.n - 1)
                            m = nc.vector.scalar_tensor_tensor(out=o, in0=w[:, kc, :], scalar=x, in1=o, op0=ALU.mult, op1=ALU.add)
                        if kc < KC - 1 or c == 0:
                            link(m)
                m.then_inc(ada_acc, 1)

            def multipliers(i):
                layer, w = i // 2, i % 2
                dve.wait_ge(ada_taken, 24 * layer + 12 * w + 8)
                nc.vector.scalar_tensor_tensor(out=mult[:, i], in0=ada[layer][:, 24 * w + 8:24 * w + 16, :], scalar=1.0,
                                               in1=colA[:, ROW_NG + 8 * i:ROW_NG + 8 * i + 8].unsqueeze(2).broadcast_to([P, KC, 2]),
                                               op0=ALU.add, op1=ALU.mult).then_inc(s_mult, 1)
                dve.wait_ge(s_mult, i + 1)

            def modulated_full():
                dve.wait_ge(n_rstd, 2)
                for kc in range(KC):
                    link(nc.vector.tensor_tensor(hT[:, kc, :], xT[:, kc, :], rstd0[:], ALU.mult))
                    if kc:
                        scale_shift(kc - 1)
                scale_shift(KC - 1)

            def scale_shift(kc):
                link.wait()
                for a, b, half in halves(True):
                    m = nc.vector.tensor_scalar(hT[:, kc, a:b], hT[:, kc, a:b], mult[:, 0, kc, half:half + 1],
                                                ada[0][:, kc, half:half + 1], ALU.mult, ALU.add)
                m.then_inc(h_ready, 1)

            def modulated(i, with_ctx):
                layer, w = i // 2, i % 2
                h, rstd, tmp = (None, (h1, rstd1, gateS), (h2, rstd2, htmp), (h1, rstd1, gateS))[i]
                dve.wait_ge(n_rstd, {1: 4, 2: 6, 3: 7}[i])

                def low(kc):
                    dve.wait_ge(h_hi, KC * (i - 1) + kc + 1)
                    for a, b, half in halves(with_ctx):
                        m = nc.vector.scalar_tensor_tensor(out=h[1][:, kc, a:b], in0=tmp[:, kc % 2, a:b], scalar=ada[layer][:, 24 * w + kc, half:half + 1],
                                                           in1=h[0][:, kc, a:b].bitcast(F32), op0=ALU.add, op1=ALU.subtract)
                        if with_ctx and not half:
                            link(m)
                    m.then_inc(h_ready, 1)

                for kc in range(KC):
                    if kc >= 2:
                        dve.wait_ge(h_ready, KC * i + kc - 1)
                    for a, b, half in halves(with_ctx):
                        m = nc.vector.scalar_tensor_tensor(out=tmp[:, kc % 2, a:b], in0=xT[:, kc, a:b], scalar=mult[:, i, kc, half:half + 1],
                                                           in1=rstd[:, a:b], op0=ALU.mult, op1=ALU.mult)
                        if with_ctx and not half:
                            link(m)
                    m.then_inc(h_full, 1)
                    if kc:
                        low(kc - 1)
                low(KC - 1)

            def split_lo(n):
                if n >= len(SPLIT):
                    return
                dve.wait_ge(w_hi, n + 1)
                raw, hi, lo = split_block(n)
                nc.vector.tensor_tensor(lo, raw, hi.bitcast(F32), ALU.subtract).then_inc(w_lo, 1)

            dve.wait_ge(s_cols, 3)
            dve.wait_ge(s_cond, 2)
            sum_ada(0, 1)
            sum_ada(0, 3)
            take_ada(0, 0)
            take_ada(0, 1)
            sum_ada(0, 5)
            take_ada(0, 2)
            take_ada(0, 3)
            sum_ada(0, 7)
            for b in range(4, 8):
                take_ada(0, b)
            multipliers(0)
            dve.wait_ge(s_xctx, KC)
            modulated_full()
            for g in range(KC):
                if g:
                    take_ada(0, 6 + 2 * g)
                sum_ada(0, 8 + 2 * g)
                dve.wait_ge(f_ycopy, 2 * g + 1)
                nc.vector.tensor_tensor(yT[1][:, g, 0:LAT], bank[3 + g % 2], yT[0][:, g, 0:LAT].bitcast(F32), ALU.subtract).then_inc(f_ylo, 1)
                dve.wait_ge(f_ycopy, 2 * g + 2)
                nc.vector.tensor_tensor(yT[1][:, g, LAT:ROWS], bank[5][:, 0:CTX], yT[0][:, g, LAT:ROWS].bitcast(F32), ALU.subtract).then_inc(f_ylo, 1)
                if g:
                    take_ada(0, 7 + 2 * g)
                sum_ada(0, 9 + 2 * g)
            take_ada(0, 22)
            take_ada(0, 23)
            multipliers(1)
            link(nc.vector.tensor_tensor(gb[:], ada[0][:, 16:24, :], colA[:, ROW_FB:ROW_FB + KC].unsqueeze(2).broadcast_to([P, KC, 2]), ALU.mult))
            link.wait()
            split_lo(0)
            split_lo(1)
            for m in range(KC):
                for a, b, half in halves(True):
                    link(nc.vector.tensor_scalar(xT[:, m, a:b], xT[:, m, a:b], gb[:, m, half:half + 1], None, ALU.add))
            link.wait()

            def residual(t, layer, piece, cb, with_ctx):
                s = t % 2
                dve.wait_ge(tile_done, 2 * t + 2)
                for j in range(2):
                    m = 2 * cb + j
                    for a, b, half in halves(with_ctx):
                        src = bank[3 * s + 2][:, 256 * j:256 * j + 256] if half else bank[3 * s + j]
                        i = nc.vector.scalar_tensor_tensor(out=xT[:, m, a:b], in0=src, scalar=ada[layer][:, 8 * piece + m, half:half + 1],
                                                           in1=xT[:, m, a:b], op0=ALU.mult, op1=ALU.add)
                        if with_ctx and not half:
                            link(i)
                    i.then_inc(r_res, 1)

            for cb in range(4):
                residual(T_OF[("fnet", cb)], 0, 2, cb, True)
                split_lo(cb + NS)

            def ffn(layer):
                end = ROWS if layer == 0 else LAT
                for g, (lo, hi) in enumerate(GROUPS):
                    for k in range(lo, hi):
                        t = T_OF[("in", layer, k)]
                        s, c = t % 2, FC * layer + k
                        dve.wait_ge(tile_done, 2 * t + 2)
                        dve.wait_ge(g_silu, c + 1)
                        m = nc.vector.tensor_tensor(gateS[:, c % 2, 0:LAT], gateS[:, c % 2, 0:LAT], bank[3 * s + 1], ALU.mult)
                        if layer == 0:
                            link(m)
                            m = nc.vector.tensor_tensor(gateS[:, c % 2, LAT:ROWS], gateS[:, c % 2, LAT:ROWS],
                                                        bank[3 * s + 2][:, 256:512], ALU.mult)
                        m.then_inc(g_full, 1)
                        dve.wait_ge(g_hi, c + 1)
                        nc.vector.tensor_tensor(hid[1][:, k - lo, 0:end], gateS[:, c % 2, 0:end], hid[0][:, k - lo, 0:end].bitcast(F32), ALU.subtract) \
                            .then_inc(g_hid, 1)
                        split_lo(S_OF[("in", layer, k)] + NS)
                        if layer == 0:
                            if k:
                                take_ada(1, k - 1)
                            sum_ada(1, k)
                    for cb in range(4):
                        residual(T_OF[("down", layer, lo, cb)], layer, 5, cb, layer == 0)
                        split_lo(S_OF[("down", layer, lo, cb)] + NS)
                        if (layer, hi) == (0, FC) and cb < 3:
                            take_ada(1, FC - 1 + cb)
                            if cb < 2:
                                sum_ada(1, FC + cb)

            modulated(1, True)
            ffn(0)

            dve.wait_ge(s_small, 16 * 7)
            multipliers(2)
            multipliers(3)
            modulated(2, True)

            def normed(i):
                with_ctx = i < 8
                gain = colA[:, ROW_KG:ROW_KG + 1] if i < 8 else colA[:, ROW_QG:ROW_QG + 1]
                t, j = T_OF[("dk", 0)] + i // 2, i % 2
                dst = kT if i < 8 else qT
                h = i % 8
                dve.wait_ge(k_rstd, i + 1)
                if with_ctx:
                    link(nc.vector.scalar_tensor_tensor(out=kT[:, h, LAT:ROWS], in0=bank[3 * (t % 2) + 2][:, 256 * j:256 * j + 256],
                                                        scalar=gain, in1=rstd2[:, LAT:ROWS], op0=ALU.mult, op1=ALU.mult))
                nc.vector.scalar_tensor_tensor(out=kraw[:], in0=bank[3 * (t % 2) + j], scalar=gain,
                                               in1=rstd2[:, 0:LAT], op0=ALU.mult, op1=ALU.mult).then_inc(k_norm, 1)
                dve.wait_ge(k_norm, i + 1)
                link(nc.vector.tensor_tensor(dst[:, h, 0:LAT], kraw[:], cosT, ALU.mult))
                if i:
                    dve.wait_ge(k_done, i)
                for q in range(4):
                    o = 32 * (q ^ 1)
                    link(nc.vector.tensor_copy(krot[32 * q:32 * q + 32, :], kraw[o:o + 32, :]))
                link.wait()
                link(nc.vector.tensor_tensor(krot[:], krot[:], sinT, ALU.mult))
                link.wait()
                nc.vector.tensor_tensor(dst[:, h, 0:LAT], dst[:, h, 0:LAT], krot[:], ALU.add).then_inc(k_done, 1)

            for i in range(16):
                normed(i)
                if i % 2:
                    split_lo(S_OF[("dk", 0)] + i // 2 + NS)
            for cb in range(4):
                t = T_OF[("dv", cb)]
                dve.wait_ge(tile_done, 2 * t + 2)
                for b in (0, 2):
                    m = nc.vector.tensor_copy(V[:, 2 * b:2 * b + 2, 256 * cb:256 * cb + 256],
                                              bank[3 * (t % 2) + b].rearrange("p (a n) -> p a n", a=2))
                m.then_inc(v_copyd, 1)
                split_lo(S_OF[("dv", cb)] + NS)
            for j in range(2):
                link(nc.vector.tensor_tensor_reduce(lamt[:], lamv[:, 2 * j * DH:(2 * j + 1) * DH], lamv[:, (2 * j + 1) * DH:(2 * j + 2) * DH],
                                                    1.0, 0.0, ALU.mult, ALU.add, lams[:, j:j + 1]))
                link.wait()
            nc.vector.tensor_copy(lams[:, 4:6], lams[:, 0:2]).then_inc(s_lam, 1)
            dve.wait_ge(s_lamx, 1)
            link(nc.vector.tensor_tensor(lams[:, 0:1], lams[:, 3:4], lams[:, 2:3], ALU.subtract))
            link.wait()
            link(nc.vector.tensor_scalar(lams[:, 6:7], lams[:, 0:1], -LAM_INIT, None, ALU.add))
            link(nc.vector.tensor_scalar(lamt[:, 0:1], colA[:, ROW_SUB:ROW_SUB + 1], 1.0 - LAM_INIT, None, ALU.mult))

            def combine(u):
                dve.wait_ge(a_exp, 2 * u + 2)
                m = attmx[:, u % 2]
                link(nc.vector.reciprocal(m[:, :, 3:4], m[:, :, 2:3]))
                link.wait()
                link(nc.vector.tensor_scalar(m[:, 1, 3:4], m[:, 1, 3:4], lams[:, 6:7], None, ALU.mult))
                link(nc.vector.tensor_scalar(prob[:, u % 2, 0, :], prob[:, u % 2, 0, :], m[:, 0, 3:4], None, ALU.mult))
                link.wait()
                nc.vector.scalar_tensor_tensor(out=prob[:, u % 2, 1, :], in0=prob[:, u % 2, 1, :], scalar=m[:, 1, 3:4],
                                               in1=prob[:, u % 2, 0, :], op0=ALU.mult, op1=ALU.add).then_inc(a_w, 1)

            def maxima(u):
                for c in range(2):
                    dve.wait_ge(a_s, 2 * u + c + 1)
                    m = attmx[:, u % 2, c]
                    link(nc.vector.tensor_reduce(m[:, 0:1], two[c][:, 0:ROWS], AX.X, ALU.max))
                    link.wait()
                    nc.vector.tensor_scalar(m[:, 1:2], m[:, 0:1], -DH ** -0.5, None, ALU.mult).then_inc(a_max, 1)

            def head_out(h):
                dve.wait_ge(a_rs, h + 1)
                nc.vector.scalar_tensor_tensor(out=sq3[:, h % 2, :], in0=bank[6], scalar=lamt[:, 0:1], in1=rstd3[:],
                                               op0=ALU.mult, op1=ALU.mult).then_inc(a_of, 1)

            def head_lo(h):
                dve.wait_ge(a_ohi, h + 1)
                nc.vector.tensor_tensor(aoL[:, h, :], sq3[:, h % 2, :], aoH[:, h, :].bitcast(F32), ALU.subtract).then_inc(a_o, 1)

            def keep_turned(u):
                h, i = u // NT, u % NT
                if i == 0 and h >= 2:
                    head_lo(h - 2)
                dve.wait_ge(a_wt, 2 * u + 2)
                if i == 0 and h:
                    dve.wait_ge(a_pv, h)
                if i == 3 and h:
                    head_out(h - 1)
                nc.vector.tensor_copy(WT[:, 3:6, i * P:(i + 1) * P], bank[5][:, 0:3 * P].rearrange("p (a n) -> p a n", a=3)).then_inc(a_wtd, 1)

            maxima(0)
            for u in range(4 * HEADS):
                if u + 1 < 4 * HEADS:
                    maxima(u + 1)
                combine(u)
                if u:
                    keep_turned(u - 1)
            keep_turned(4 * HEADS - 1)
            head_lo(HEADS - 2)
            head_out(HEADS - 1)
            head_lo(HEADS - 1)
            for cb in range(4):
                residual(T_OF[("dout", cb)], 1, 2, cb, False)
                split_lo(S_OF[("dout", cb)] + NS)
            modulated(3, False)
            ffn(1)

            dve.wait_ge(n_rstd, 9)

            def u_low(kc):
                dve.wait_ge(h_hi, 3 * KC + kc + 1)
                nc.vector.tensor_tensor(un[1][:, kc, :], utmp[:, kc % 2, :], un[0][:, kc, :].bitcast(F32), ALU.subtract).then_inc(h_ready, 1)

            dve.wait_ge(d_wd, 1)
            nc.vector.tensor_tensor(wd[1][:], wdtf[:], wd[0][:].bitcast(F32), ALU.subtract).then_inc(d_wd, 1)
            for kc in range(KC):
                gain = colA[:, ROW_NP + kc:ROW_NP + kc + 1]
                if kc >= 2:
                    dve.wait_ge(h_ready, 4 * KC + kc - 1)
                link(nc.vector.scalar_tensor_tensor(out=utmp[:, kc % 2, META:ALL], in0=xT[:, kc, 0:LAT], scalar=gain, in1=rstdb[:, 0:LAT],
                                               op0=ALU.mult, op1=ALU.mult))
                nc.vector.scalar_tensor_tensor(out=utmp[:, kc % 2, 0:META], in0=metaT[:, kc, :], scalar=gain, in1=rstdb[:, LAT:ALL],
                                               op0=ALU.mult, op1=ALU.mult).then_inc(h_full, 1)
                if kc:
                    u_low(kc - 1)
            u_low(KC - 1)
            dve.wait_ge(d_raw, 1)
            dve.wait_ge(d_zero, 2)
            link(nc.vector.tensor_tensor(dtr[:, 0:4, :], bank[6][:, 0:192].rearrange("p (a n) -> p a n", a=4),
                                    bdtf[:].unsqueeze(1).broadcast_to([P, 4, 48]), ALU.add))
            link(nc.vector.tensor_tensor(dtr[0:META, 4, :], bank[6][0:META, 192:240], bdtf[0:META, :], ALU.add))
            link.wait()
            nc.vector.scalar_tensor_tensor(out=dta, in0=dtr[:], scalar=-1.0, in1=dtr[:], op0=ALU.mult, op1=ALU.max).then_inc(d_biased, 1)
            dve.wait_ge(d_u, 1)
            nc.vector.tensor_scalar(dtw, dtu, 1.0, None, ALU.add).then_inc(d_w, 1)
            dve.wait_ge(d_w, 1)
            link(nc.vector.reciprocal(dta, dtw))
            link(nc.vector.scalar_tensor_tensor(out=dtu, in0=dtw, scalar=-1.0, in1=dtu, op0=ALU.add, op1=ALU.subtract))
            link.wait()
            link(nc.vector.scalar_tensor_tensor(out=dtu, in0=dtu, scalar=-1.0, in1=dta, op0=ALU.mult, op1=ALU.mult))
            link.wait()
            dve.wait_ge(d_ln, 1)
            link(nc.vector.tensor_tensor(dtl, dtl, dtu, ALU.add))
            link.wait()
            link(nc.vector.scalar_tensor_tensor(out=dtv[:], in0=dtr[:, :, 0:32], scalar=0.0, in1=dtl[:, :, 0:32], op0=ALU.max, op1=ALU.add))
            link(nc.vector.scalar_tensor_tensor(out=logf[:], in0=dtr[:, :, 32:48], scalar=0.0, in1=dtl[:, :, 32:48], op0=ALU.min, op1=ALU.subtract))
            link.wait()
            dve.wait_ge(d_expa, 1)
            nc.vector.scalar_tensor_tensor(out=adt[:], in0=dtv[:], scalar=-1.0, in1=expa[:].unsqueeze(1).broadcast_to([P, 5, 32]),
                                           op0=ALU.mult, op1=ALU.mult).then_inc(d_adt, 1)

            def conv(i):
                g, k6 = i // 6, i % 6
                ch = 16 + 4 * k6 + g if k6 < 2 else 4 * g + k6 - 2
                dve.wait_ge(c_in, i + 1)
                if i >= 2:
                    dve.wait_ge(c_out, i - 1)
                    before = (i - 2) % 6
                    if before >= 2:
                        dve.wait_ge(c_t, 5 * ((i - 2) // 6) + before)
                for k in range(4):
                    w = colC[:, 24 * k + ch:24 * k + ch + 1]
                    x = cin[:, i % 2, k:k + ALL]
                    if k == 0:
                        m = nc.vector.tensor_scalar(cacc[:, i % 2, :], x, w, None, ALU.mult)
                    else:
                        m = nc.vector.scalar_tensor_tensor(out=cacc[:, i % 2, :], in0=x, scalar=w, in1=cacc[:, i % 2, :],
                                                           op0=ALU.mult, op1=ALU.add)
                    if k < 3:
                        link(m)
                        link.wait()
                m.then_inc(c_acc, 1)

            def wide(x, n, k):
                return x.unsqueeze(2).broadcast_to([n, 8, k])

            def heads(x):
                return x.rearrange("p (h d) -> p h d", h=8)

            def projected(g):
                for b in range(2):
                    for part in range(2):
                        t = T_OF[("ps", g, b, part)]
                        for j in range(2):
                            m = 4 * b + 2 * part + j
                            dve.wait_ge(tile_done, 2 * t + 1 + j)
                            if g == 0:
                                o = nc.vector.tensor_copy(acc[:, m, :], bank[3 * (t % 2) + j])
                            else:
                                o = nc.vector.tensor_tensor(acc[:, m, :], acc[:, m, :], bank[3 * (t % 2) + j], ALU.add)
                            if j == 0:
                                link(o)
                        o.then_inc(m_ps, 1)
                    split_lo(S_OF[("ps", g, b)] + NS)

            for g in range(SG):
                hs = slice(8 * g, 8 * g + 8)
                conv(6 * g)
                conv(6 * g + 1)
                split_lo(S_OF[("bc", g)] + NS)
                if g:
                    projected(g - 1)
                for j in range(4):
                    conv(6 * g + 2 + j)
                    if j == 1:
                        dve.wait_ge(c_t, 5 * g + 1)
                        link(nc.vector.tensor_copy(Brow[:, 0:3, :], bank[6][:, 0:384].rearrange("p (a n) -> p a n", a=3)))
                        nc.vector.tensor_copy(Brow[0:META, 3, :], bank[6][0:META, 384:512]).then_inc(c_tev, 1)
                    if j % 2:
                        split_lo(S_OF[("xs", g, j // 2)] + NS)
                        for jj in (j - 1, j):
                            dve.wait_ge(c_t, 5 * g + 1 + jj + 1)
                            nc.vector.tensor_copy(xrow[:, 0:4, P * jj:P * jj + P], bank[6].rearrange("p (a n) -> p a n", a=4)).then_inc(c_tev, 1)
                split_lo(S_OF[("z", g, 0)] + NS)
                split_lo(S_OF[("z", g, 1)] + NS)
                dve.wait_ge(e_st, 4 * g + 1)
                if g:
                    dve.wait_ge(e_yoff, 4 * g)
                nc.vector.tensor_copy(Hst[:, 0, :], bank[5]).then_inc(e_h, 1)

                def keep(n):
                    dve.wait_ge(e_t, n + 1)
                    c = ROW_SN + 4 * (n // 4)
                    if n:
                        dve.wait_ge(e_tev, n)
                    nc.vector.tensor_tensor(ysf[:], bank[6].rearrange("p (a n) -> p a n", a=4),
                                            colA[:, c:c + 4].unsqueeze(2).broadcast_to([P, 4, P]), ALU.mult).then_inc(e_full, 1)

                def keep_lo(n):
                    dve.wait_ge(e_hi, n + 1)
                    r = slice((n % 4) * P, (n % 4 + 1) * P)
                    nc.vector.tensor_tensor(ys[1][:, :, r], ysf[:], ys[0][:, :, r].bitcast(F32), ALU.subtract).then_inc(e_tev, 1)

                for i in range(NT):
                    n = 4 * g + i
                    y = yrow[:, i % 2, :]
                    dve.wait_ge(e_cb, n + 1)
                    link(nc.vector.tensor_tensor(CBm[:], bank[2][:, 0:P], upper, ALU.mult))
                    link.wait()
                    dve.wait_ge(e_exp, n + 1)
                    nc.vector.tensor_tensor(Mt[:, i % 2], Mt[:, i % 2], CBm[:].unsqueeze(1).broadcast_to([P, 8, P]), ALU.mult).then_inc(e_m, 1)
                    if i < 3:
                        if n >= 2:
                            dve.wait_ge(e_yoff, n)
                        dve.wait_ge(e_h, n + 1)
                        c = 224 + 32 * i + 8 * g
                        link(nc.vector.tensor_tensor(heads(Hst[:, (i + 1) % 2, :]), heads(Hst[:, i % 2, :]), wide(dec[:, c:c + 8], P, 64), ALU.mult))
                        link.wait()
                        dve.wait_ge(e_st, n + 2)
                        nc.vector.tensor_tensor(Hst[:, (i + 1) % 2, :], Hst[:, (i + 1) % 2, :], bank[5], ALU.add).then_inc(e_h, 1)
                    c = 32 * i + 8 * g
                    dve.wait_ge(e_yoff, n + 1)
                    if n >= 2:
                        dve.wait_ge(e_t, n - 1)
                    nc.vector.tensor_tensor(heads(y), heads(bank[4]), wide(dec[:, c:c + 8], P, 64), ALU.mult).then_inc(e_off, 1)
                    dve.wait_ge(e_off, n + 1)
                    dve.wait_ge(p_xd, n + 1)
                    link(nc.vector.tensor_tensor(y, y, xd[:], ALU.add))
                    link.wait()
                    dve.wait_ge(e_y, n + 1)
                    link(nc.vector.tensor_tensor(y, y, bank[3], ALU.add))
                    link.wait()
                    dve.wait_ge(z_act, 2 * g + 2)
                    nc.vector.tensor_tensor(y, y, zrow[:, i, :], ALU.mult).then_inc(e_gated, 1)
                    if i >= 2:
                        keep_lo(n - 2)
                    if i:
                        keep(n - 1)
                keep_lo(4 * g + 2)
                keep(4 * g + 3)
                keep_lo(4 * g + 3)

            projected(SG - 1)
            for f in range(4):
                t = T_OF[("q", f)]
                dve.wait_ge(tile_done, 2 * t + 2)
                if f:
                    dve.wait_ge(b_s, 16 * f)
                link(nc.vector.tensor_copy(qA[0:DH, 2, :], bank[3 * (t % 2) + 1][0:DH, :]))
                nc.vector.tensor_copy(qA[0:DH, 3, :], bank[3 * (t % 2) + 1][DH:P, :]).then_inc(x_dve, 1)
                split_lo(S_OF[("q", f)] + NS)
                t = T_OF[("k", f)]
                dve.wait_ge(tile_done, 2 * t + 2)
                for h in range(4):
                    m = nc.vector.tensor_copy(kA[0:DH, h, LO:ALL], bank[3 * (t % 2) + 2][DH * (h % 2):DH * (h % 2) + DH, 256 * (h // 2):256 * (h // 2) + 256])
                    if h < 3:
                        link(m)
                m.then_inc(x_dve, 1)
                split_lo(S_OF[("k", f)] + NS)
                t = T_OF[("v", f)]
                dve.wait_ge(tile_done, 2 * t + 2)
                if f:
                    dve.wait_ge(b_o, 16 * f)
                link(nc.vector.tensor_copy(vA[:, 2:4, :], bank[3 * (t % 2) + 1].rearrange("p (a n) -> p a n", a=2)))
                nc.vector.tensor_copy(vA[0:META, 4, :], bank[3 * (t % 2) + 2][0:META, 0:256]).then_inc(x_dve, 1)
                split_lo(S_OF[("v", f)] + NS)
                split_lo(S_OF[("za", f)] + NS)

                def fox_max(u):
                    i = u // 4 % 4
                    dve.wait_ge(b_s, u + 1)
                    link(nc.vector.tensor_reduce(amx[:, u % 2, 0:1], two[u % 2][:, 0:META + (i + 1) * P], AX.X, ALU.max))
                    link.wait()
                    if u >= 2:
                        dve.wait_ge(b_exp, u - 1)
                    nc.vector.tensor_scalar(amx[:, u % 2, 1:2], amx[:, u % 2, 0:1], -DH ** -0.5, None, ALU.mult).then_inc(b_max, 1)

                def fox_gate(v):
                    i = v % 4
                    dve.wait_ge(b_exp, 4 * v + 4)
                    link(nc.vector.reciprocal(asum[:, i, :], asum[:, i, :]))
                    link.wait()
                    dve.wait_ge(b_o, 4 * v + 4)
                    if v:
                        dve.wait_ge(b_yt, v)
                    link(nc.vector.tensor_tensor(yA[:].rearrange("p (h d) -> p h d", h=4), bank[7][:, 0:256].rearrange("p (h d) -> p h d", h=4),
                                                 asum[:, i, :].unsqueeze(2).broadcast_to([P, 4, 64]), ALU.mult))
                    link.wait()
                    dve.wait_ge(z_act, 2 * SG + f + 1)
                    nc.vector.tensor_tensor(yA[:], yA[:], zA[:, i, :], ALU.mult).then_inc(b_y, 1)

                def fox_keep(v):
                    i = v % 4
                    dve.wait_ge(b_yhi, v + 1)
                    nc.vector.tensor_tensor(ya[1][:, 2 * f:2 * f + 2, i * P:(i + 1) * P], bank[6][:, 0:256].rearrange("p (a n) -> p a n", a=2),
                                            ya[0][:, 2 * f:2 * f + 2, i * P:(i + 1) * P].bitcast(F32), ALU.subtract).then_inc(b_ytev, 1)

                fox_max(16 * f)
                for u in range(16 * f, 16 * f + 16):
                    i, h = u // 4 % 4, u % 4
                    if u + 1 < 16 * f + 16:
                        fox_max(u + 1)
                    dve.wait_ge(b_pt, u + 1)
                    if u >= 2:
                        dve.wait_ge(b_o, u - 1)
                    nc.vector.tensor_copy(PT[0:META, u % 2, 4 * P:5 * P], bank[5][0:META, 0:P]).then_inc(b_ptd, 1)
                    if h == 0 and u > 16 * f:
                        fox_gate(u // 4 - 1)
                    if h == 3 and u > 16 * f + 3:
                        fox_keep(u // 4 - 1)
                fox_gate(4 * f + 3)
                fox_keep(4 * f + 3)

            for cb in range(4):
                t = T_OF[("pa", cb)]
                for k, kind in enumerate(("gs", "ga")):
                    dve.wait_ge(m_gate, 2 * cb + k + 1)
                    if k == 0:
                        link(nc.vector.tensor_tensor(gsb[:], gsb[:], acc[:, 2 * cb:2 * cb + 2, :], ALU.mult))
                    split_lo(S_OF[(kind, cb)] + NS)
                for j in range(2):
                    dve.wait_ge(tile_done, 2 * t + 1 + j)
                    link(nc.vector.tensor_tensor(gab[:, j, :], gab[:, j, :], bank[3 * (t % 2) + j], ALU.mult))
                link.wait()
                nc.vector.tensor_tensor(gsb[:], gsb[:], gab[:], ALU.add).then_inc(m_full, 1)
                dve.wait_ge(m_hi, cb + 1)
                nc.vector.tensor_tensor(mg[1][:, 2 * cb:2 * cb + 2, :], gsb[:], mg[0][:, 2 * cb:2 * cb + 2, :].bitcast(F32), ALU.subtract).then_inc(m_mix, 1)
                split_lo(S_OF[("pa", cb)] + NS)
            for cb in range(4):
                split_lo(S_OF[("wo", cb)] + NS)
            dve.wait_ge(o_act, 4)
            junk = acc[:].rearrange("p a n -> p (a n)")
            dve.wait_ge(tile_done, 2 * T_OF[("wo", 3)] + 2)
            for i in range(NT):
                nc.vector.tensor_tensor_reduce(junk[:, D * i:D * i + D], orow[:, i, :], orow[:, i, :], 1.0, 0.0, ALU.mult, ALU.add, stt4[:, i:i + 1]) \
                    .then_inc(o_ss, 1)
            dve.wait_ge(o_rs, 1)
            dve.wait_ge(o_post, 16)
            for i in range(NT):
                link(nc.vector.scalar_tensor_tensor(out=orow[:, i, :], in0=orow[:, i, :], scalar=stt4[:, 4 + i:5 + i], in1=gpost[:],
                                               op0=ALU.mult, op1=ALU.mult))
                link.wait()
                for j in range(2):
                    dve.wait_ge(o_xt, 2 * i + j + 1)
                    nc.vector.tensor_tensor(orow[:, i, 512 * j:512 * j + 512], orow[:, i, 512 * j:512 * j + 512], bank[6 + j], ALU.add) \
                        .then_inc(o_fin, 1)

        @block.gpsimd
        def _(pool):
            pool.wait_ge(r_res, 64)
            nc.gpsimd.memset(cin[:, :, 0:3], 0.0).then_inc(d_zero, 1)
            nc.gpsimd.memset(dtr[:], 0.0).then_inc(d_zero, 1)

            def wide(x, n, k):
                return x.unsqueeze(2).broadcast_to([n, 8, k])

            def heads(x):
                return x.rearrange("p (h d) -> p h d", h=8)

            pool.wait_ge(d_dec, 1)
            for g in range(SG):
                hs = slice(8 * g, 8 * g + 8)

                def decays(i):
                    n = 4 * g + i
                    if n:
                        pool.wait_ge(e_seg, n)
                    else:
                        pool.wait_ge(d_adt, 1)
                    nc.gpsimd.tensor_tensor(lseg[:, 0:8 * P].rearrange("p (h s) -> p h s", h=8), wide(adt[:, i, hs], P, P),
                                            lower.unsqueeze(1).broadcast_to([P, 8, P]), ALU.mult).then_inc(p_lseg, 1)

                decays(0)
                pool.wait_ge(c_tev, 5 * g + 5)
                pool.wait_ge(c_tevm, 4 * g + 4)
                if g:
                    pool.wait_ge(e_st, 4 * g)
                    pool.wait_ge(e_y, 4 * g)
                nc.gpsimd.tensor_tensor(heads(xdt[0:META, 0, :]), heads(xrow[0:META, 4, :]), wide(dtv[0:META, 4, hs], META, 64), ALU.mult) \
                    .then_inc(p_xdt, 1)
                pool.wait_ge(p_xdt, 5 * g + 1)
                nc.gpsimd.tensor_tensor(heads(xds[0:META, :]), heads(xdt[0:META, 0, :]), wide(dec[0:META, 320 + 8 * g:328 + 8 * g], META, 64), ALU.mult) \
                    .then_inc(p_xds, 1)
                for i in range(NT):
                    n = 4 * g + i
                    if i >= 2:
                        pool.wait_ge(e_y, n - 1)
                    if i == 1:
                        pool.wait_ge(p_xds, n)
                    nc.gpsimd.tensor_tensor(heads(xdt[:, (i + 1) % 2, :]), heads(xrow[:, i, :]), wide(dtv[:, i, hs], P, 64), ALU.mult) \
                        .then_inc(p_xdt, 1)
                    if i < 3:
                        pool.wait_ge(p_xdt, 5 * g + i + 2)
                        pool.wait_ge(e_st, n + 1)
                        c = 128 + 32 * i + 8 * g
                        nc.gpsimd.tensor_tensor(heads(xds[:]), heads(xdt[:, (i + 1) % 2, :]), wide(dec[:, c:c + 8], P, 64), ALU.mult) \
                            .then_inc(p_xds, 1)
                    if n:
                        pool.wait_ge(e_gated, n)
                    nc.gpsimd.tensor_tensor(heads(xd[:]), heads(xrow[:, i, :]), wide(dskip[:, hs], P, 64), ALU.mult).then_inc(p_xd, 1)
                    if i + 1 < NT:
                        decays(i + 1)
            pool.wait_ge(tile_done, last_tile(("ps", 3, 1)))
            nc.gpsimd.memset(qA[DH:DH + 2, :, :], 1.0).then_inc(b_one, 1)
            nc.gpsimd.memset(kA[DH:DH + 2, :, :], 1.0).then_inc(b_one, 1)
            pool.wait_ge(b_one, 2)
            for f in range(4):
                if f:
                    pool.wait_ge(b_s, 16 * f)
                pool.dma_start(kA[DH:DH + 1, :, :], ckT[4 * f:4 * f + 4, :]).then_inc(b_k, 16)
                pool.dma_start(qA[DH + 1:DH + 2, :, :], cqT[4 * f:4 * f + 4, :]).then_inc(b_q, 16)


INPUTS = ['x', 'c', 'ctx', 'c_ctx', 'w_ada', 'b_ada', 'norm_gain', 'ffn_w_in', 'ffn_w_out', 'fnet_w_out', 'fnet_b_out',
          'diff_w_in', 'diff_q_gain', 'diff_k_gain', 'diff_lambda', 'diff_subln_gain', 'diff_w_out',
          'meta_tokens_2', 'norm_pre_2', 'w_in_2', 'conv_w_2', 'conv_b_2', 'dt_bias_2', 'a_log_2', 'd_skip_2',
          'ssd_norm_2', 'fgate_bias_2', 'gate_bias_2', 'w_proj_ssd_2', 'w_proj_att_2', 'w_out_2', 'norm_post_2']


def kernel(**inputs):
    import concourse.bacc as bacc
    from concourse.bass_utils import run_bass_kernel_spmd

    nc = bacc.Bacc("TRN2", target_bir_lowering=False, num_devices=1)
    arrays, io = {}, {}
    for name in INPUTS:
        a = np.ascontiguousarray(inputs[name])
        arrays[f"in_{name}"] = a
        io[name] = nc.dram_tensor(f"in_{name}", a.shape, F32, kind="ExternalInput").ap()
    tables = []
    for name, a in zip(("table", "dft_lat", "dft_ctx"), constants()):
        arrays[name] = a
        tables.append(nc.dram_tensor(name, a.shape, F32, kind="ExternalInput").ap())
    out = nc.dram_tensor("out_0", (1, LAT, D), F32, kind="ExternalOutput").ap()
    xsave = nc.dram_tensor("xsave", (P, KC, LAT), F32).ap()
    bass_two_blocks_kernel(nc, io, *tables, xsave, out)
    result = run_bass_kernel_spmd(nc, [arrays], core_ids=[0])
    return result.results[0]["out_0"]
```
